# Optimizing a Trainium2 kernel written in Bass

```python
import math
import jax, jax.numpy as jnp
from jax import lax
import numpy as np

D_MODEL = 1024
BATCH = 1
SEQ = 256
DEPTH = 1

N_META = 16
BLOCK = 128
PAD_FRONT = BLOCK - N_META
N_HEADS = 8
QK_NOPE = 64
QK_ROPE = 32
V_DIM = 64
Q_LORA = 256
KV_LORA = 128
ROPE_THETA = 10000.0
ATTN_SCALE = (QK_NOPE + QK_ROPE) ** -0.5
ATTN_WIDTH = N_HEADS * V_DIM
CONV_DIM = 512
CONV_GROUPS = 8
CONV_W = 3
MIX_WIDTH = ATTN_WIDTH + CONV_DIM
IN_COLS = Q_LORA + KV_LORA + QK_ROPE + 3 * CONV_DIM
SPLITS = [Q_LORA, Q_LORA + KV_LORA, Q_LORA + KV_LORA + QK_ROPE,
          Q_LORA + KV_LORA + QK_ROPE + CONV_DIM, Q_LORA + KV_LORA + QK_ROPE + 2 * CONV_DIM]
N_GROUPS = 4
EXPERTS_PER_GROUP = 8
N_EXPERTS = N_GROUPS * EXPERTS_PER_GROUP
TOP_K = 2
D_FF = 256
EPS = 1e-6
NEG_INF = -1e30


def rms_norm(x, g):
    xf = x.astype(jnp.float32)
    y = xf * lax.rsqrt(jnp.mean(xf * xf, axis=-1, keepdims=True) + EPS)
    return (y * g.astype(jnp.float32)).astype(x.dtype)

def rope_angles(pos):
    inv_freq = 1.0 / (ROPE_THETA ** (jnp.arange(0, QK_ROPE, 2, dtype=jnp.float32) / QK_ROPE))
    ang = pos.astype(jnp.float32)[..., None] * inv_freq
    return jnp.cos(ang), jnp.sin(ang)

def apply_rope(x, cos, sin):
    xf = x.astype(jnp.float32)
    x1, x2 = jnp.split(xf, 2, axis=-1)
    return jnp.concatenate([x1 * cos - x2 * sin, x2 * cos + x1 * sin], axis=-1).astype(x.dtype)

def causal_block_attention(q_nope, q_rope, k_nope, k_rope, v):
    bsz, plen = q_nope.shape[0], q_nope.shape[1]
    nb = plen // BLOCK
    qn = q_nope.reshape(bsz, nb, BLOCK, N_HEADS, QK_NOPE).transpose(1, 0, 2, 3, 4)
    qr = q_rope.reshape(bsz, nb, BLOCK, N_HEADS, QK_ROPE).transpose(1, 0, 2, 3, 4)
    starts = jnp.arange(nb, dtype=jnp.int32) * BLOCK
    k_idx = jnp.arange(plen, dtype=jnp.int32)

    def one_block(args):
        qn_b, qr_b, s0 = args
        s = (jnp.einsum('bqhd,bkhd->bhqk', qn_b, k_nope, preferred_element_type=jnp.float32)
             + jnp.einsum('bqhr,bkr->bhqk', qr_b, k_rope, preferred_element_type=jnp.float32)) * ATTN_SCALE
        q_idx = s0 + jnp.arange(BLOCK, dtype=jnp.int32)
        mask = (k_idx[None, :] >= PAD_FRONT) & (k_idx[None, :] <= q_idx[:, None])
        s = jnp.where(mask[None, None], s, NEG_INF)
        p = jax.nn.softmax(s, axis=-1).astype(v.dtype)
        return jnp.einsum('bhqk,bkhd->bqhd', p, v)

    out = lax.map(one_block, (qn, qr, starts))
    return out.transpose(1, 0, 2, 3, 4).reshape(bsz, plen, N_HEADS * V_DIM)

def hybrid_mixer(h, cos, sin, w_in, q_norm, w_uq, kv_norm, w_ukv, conv_w,
                 attn_out_norm, conv_out_norm, w_out):
    bsz = h.shape[0]
    hp = jnp.pad(h, ((0, 0), (PAD_FRONT, 0), (0, 0)))
    plen = hp.shape[1]
    z = hp @ w_in
    c_q, c_kv, k_pe, gate_b, gate_c, x_in = jnp.split(z, SPLITS, axis=-1)

    q = (rms_norm(c_q, q_norm) @ w_uq).reshape(bsz, plen, N_HEADS, QK_NOPE + QK_ROPE)
    q_nope = q[..., :QK_NOPE]
    q_rope = apply_rope(q[..., QK_NOPE:], cos[:, :, None, :], sin[:, :, None, :])
    kv = (rms_norm(c_kv, kv_norm) @ w_ukv).reshape(bsz, plen, N_HEADS, QK_NOPE + V_DIM)
    k_nope, v = kv[..., :QK_NOPE], kv[..., QK_NOPE:]
    k_rope = apply_rope(k_pe, cos, sin)
    attn = causal_block_attention(q_nope, q_rope, k_nope, k_rope, v)

    u = gate_c * x_in
    u_pad = jnp.pad(u, ((0, 0), (CONV_W - 1, 0), (0, 0)))
    y = sum(conv_w[k] * u_pad[:, k:k + plen] for k in range(CONV_W))
    conv = gate_b * y

    merged = jnp.concatenate([rms_norm(attn[:, PAD_FRONT:], attn_out_norm),
                              rms_norm(conv[:, PAD_FRONT:], conv_out_norm)], axis=-1)
    return merged @ w_out

def hier_moe(h, w_group_router, b_group_router, w_expert_router, b_expert_router,
             w_gate, w_up, w_down, w_sh_gate, w_sh_up, w_sh_down):
    bsz, slen, d = h.shape
    t = h.reshape(-1, d)
    g_prob = jax.nn.softmax((t @ w_group_router).astype(jnp.float32) + b_group_router.astype(jnp.float32), axis=-1)
    g_w, g_idx = lax.top_k(g_prob, 1)
    e_logits = ((t @ w_expert_router).astype(jnp.float32) + b_expert_router.astype(jnp.float32))
    e_logits = e_logits.reshape(-1, N_GROUPS, EXPERTS_PER_GROUP)
    e_logits = jnp.take_along_axis(e_logits, g_idx[:, :, None], axis=1)[:, 0]
    e_prob = jax.nn.softmax(e_logits, axis=-1)
    e_w, e_idx = lax.top_k(e_prob, TOP_K)
    e_w = e_w / jnp.sum(e_w, axis=-1, keepdims=True)
    weights = g_w * e_w
    eid = g_idx * EXPERTS_PER_GROUP + e_idx
    combine = jnp.einsum('nk,nke->ne', weights,
                         jax.nn.one_hot(eid, N_EXPERTS, dtype=jnp.float32)).astype(t.dtype)
    a = jnp.einsum('nd,edf->nef', t, w_gate)
    b = jnp.einsum('nd,edf->nef', t, w_up)
    hid = jax.nn.silu(a) * b * combine[:, :, None]
    routed = jnp.einsum('nef,efd->nd', hid, w_down)
    shared = (jax.nn.silu(t @ w_sh_gate) * (t @ w_sh_up)) @ w_sh_down
    return (routed + shared).reshape(bsz, slen, d)

def first_inputs(seed: int = 0) -> dict:
    key = jax.random.key(seed)
    ks = jax.random.split(key, 32)
    f32 = jnp.float32

    def nrm(k, shape, fan_in):
        return jax.random.normal(k, shape, f32) * (fan_in ** -0.5)

    def gain(k, shape):
        return 1.0 + 0.05 * jax.random.normal(k, shape, f32)

    L = DEPTH
    return {
        "x": jax.random.normal(ks[0], (BATCH, SEQ, D_MODEL), f32),
        "positions": jnp.broadcast_to(jnp.arange(SEQ, dtype=jnp.int32), (BATCH, SEQ)),
        "meta_tokens": jax.random.normal(ks[1], (N_META, D_MODEL), f32),
        "pre_mix_norm": gain(ks[2], (L, D_MODEL)),
        "w_in": nrm(ks[3], (L, D_MODEL, IN_COLS), D_MODEL),
        "q_norm": gain(ks[4], (L, Q_LORA)),
        "w_uq": nrm(ks[5], (L, Q_LORA, N_HEADS * (QK_NOPE + QK_ROPE)), Q_LORA),
        "kv_norm": gain(ks[6], (L, KV_LORA)),
        "w_ukv": nrm(ks[7], (L, KV_LORA, N_HEADS * (QK_NOPE + V_DIM)), KV_LORA),
        "conv_w": nrm(ks[8], (L, CONV_W, CONV_DIM), CONV_W),
        "attn_out_norm": gain(ks[9], (L, ATTN_WIDTH)),
        "conv_out_norm": gain(ks[10], (L, CONV_DIM)),
        "w_out": nrm(ks[11], (L, MIX_WIDTH, D_MODEL), MIX_WIDTH),
        "post_mix_norm": gain(ks[12], (L, D_MODEL)),
        "pre_ffn_norm": gain(ks[13], (L, D_MODEL)),
        "w_group_router": nrm(ks[14], (L, D_MODEL, N_GROUPS), D_MODEL),
        "b_group_router": 0.01 * jax.random.normal(ks[15], (L, N_GROUPS), f32),
        "w_expert_router": nrm(ks[16], (L, D_MODEL, N_EXPERTS), D_MODEL),
        "b_expert_router": 0.01 * jax.random.normal(ks[17], (L, N_EXPERTS), f32),
        "w_gate": nrm(ks[18], (L, N_EXPERTS, D_MODEL, D_FF), D_MODEL),
        "w_up": nrm(ks[19], (L, N_EXPERTS, D_MODEL, D_FF), D_MODEL),
        "w_down": nrm(ks[20], (L, N_EXPERTS, D_FF, D_MODEL), D_FF),
        "w_sh_gate": nrm(ks[21], (L, D_MODEL, D_FF), D_MODEL),
        "w_sh_up": nrm(ks[22], (L, D_MODEL, D_FF), D_MODEL),
        "w_sh_down": nrm(ks[23], (L, D_FF, D_MODEL), D_FF),
        "post_ffn_norm": gain(ks[24], (L, D_MODEL)),
    }

def first_block(x, positions, meta_tokens, pre_mix_norm, w_in, q_norm, w_uq, kv_norm, w_ukv, conv_w,
              attn_out_norm, conv_out_norm, w_out, post_mix_norm, pre_ffn_norm,
              w_group_router, b_group_router, w_expert_router, b_expert_router,
              w_gate, w_up, w_down, w_sh_gate, w_sh_up, w_sh_down, post_ffn_norm):
    bsz = x.shape[0]
    meta = jnp.broadcast_to(meta_tokens[None].astype(x.dtype), (bsz, N_META, D_MODEL))
    h = jnp.concatenate([meta, x], axis=1)
    rope_pos = jnp.concatenate([
        jnp.zeros((bsz, PAD_FRONT), jnp.int32),
        jnp.broadcast_to(jnp.arange(N_META, dtype=jnp.int32), (bsz, N_META)),
        positions.astype(jnp.int32) + N_META], axis=1)
    cos, sin = rope_angles(rope_pos)

    for l in range(DEPTH):
        mix = hybrid_mixer(rms_norm(h, pre_mix_norm[l]), cos, sin, w_in[l], q_norm[l], w_uq[l],
                           kv_norm[l], w_ukv[l], conv_w[l], attn_out_norm[l], conv_out_norm[l], w_out[l])
        h = h + rms_norm(mix, post_mix_norm[l])
        ffn = hier_moe(rms_norm(h, pre_ffn_norm[l]), w_group_router[l], b_group_router[l],
                       w_expert_router[l], b_expert_router[l], w_gate[l], w_up[l], w_down[l],
                       w_sh_gate[l], w_sh_up[l], w_sh_down[l])
        h = h + rms_norm(ffn, post_ffn_norm[l])

    return h[:, N_META:]


LRU_WIDTH = D_MODEL
LRU_BLOCKS = 16
LRU_BLOCK_W = LRU_WIDTH // LRU_BLOCKS
LRU_C = 8.0
CONV_W_2 = 4
ATT_HEADS = 16
ATT_HEAD_DIM = 64
ATT_WIDTH = ATT_HEADS * ATT_HEAD_DIM
Q_BLOCK = 128
D_FF_2 = 4 * D_MODEL
PLE_DIM = 256
NORM_EPS = 1e-6

IN_SPLITS = [LRU_WIDTH, LRU_WIDTH, ATT_WIDTH, ATT_WIDTH, ATT_WIDTH, D_MODEL, D_MODEL]
IN_WIDTH = sum(IN_SPLITS)


def rmsnorm(x, g):
    x32 = x.astype(jnp.float32)
    y = x32 * lax.rsqrt(jnp.mean(x32 * x32, axis=-1, keepdims=True) + NORM_EPS)
    return (y * g.astype(jnp.float32)).astype(x.dtype)

def causal_depthwise_conv(x, w, b):
    S = x.shape[1]
    xp = jnp.pad(x, ((0, 0), (CONV_W_2 - 1, 0), (0, 0)))
    y = b
    for k in range(CONV_W_2):
        y = y + w[k] * xp[:, k:k + S]
    return y

def rg_lru(x, w_r, b_r, w_i, b_i, lam):
    B, S, W = x.shape
    xb = x.reshape(B, S, LRU_BLOCKS, LRU_BLOCK_W)
    r = jax.nn.sigmoid((jnp.einsum('bsnc,ncd->bsnd', xb, w_r).reshape(B, S, W) + b_r).astype(jnp.float32))
    i = jax.nn.sigmoid((jnp.einsum('bsnc,ncd->bsnd', xb, w_i).reshape(B, S, W) + b_i).astype(jnp.float32))
    log_a = -LRU_C * r * jax.nn.softplus(-lam.astype(jnp.float32))
    a = jnp.exp(log_a)
    mult = jnp.sqrt(-jnp.expm1(2.0 * log_a))
    u = mult * (i * x.astype(jnp.float32))

    def combine(left, right):
        a_l, u_l = left
        a_r, u_r = right
        return a_l * a_r, a_r * u_l + u_r

    _, h = lax.associative_scan(combine, (a, u), axis=1)
    return h.astype(x.dtype)

def stick_breaking_attention(q, k, v):
    B, H, S, Dh = q.shape
    n_blk = S // Q_BLOCK
    scale = Dh ** -0.5
    q_blocks = q.reshape(B, H, n_blk, Q_BLOCK, Dh).transpose(2, 0, 1, 3, 4)
    key_pos = jnp.arange(S)

    def one_block(args):
        q_blk, blk = args
        z = jnp.einsum('bhqd,bhkd->bhqk', q_blk, k).astype(jnp.float32) * scale
        q_pos = blk * Q_BLOCK + jnp.arange(Q_BLOCK)
        causal = key_pos[None, :] < q_pos[:, None]
        log_1m = jnp.where(causal, jax.nn.log_sigmoid(-z), 0.0)
        suffix = lax.cumsum(log_1m, axis=3, reverse=True) - log_1m
        att = jnp.where(causal, jnp.exp(jax.nn.log_sigmoid(z) + suffix), 0.0)
        return jnp.einsum('bhqk,bhkd->bhqd', att.astype(v.dtype), v)

    out = lax.map(one_block, (q_blocks, jnp.arange(n_blk)))
    return out.transpose(1, 2, 0, 3, 4).reshape(B, H, S, Dh)

def second_inputs(seed: int = 0) -> dict:
    key = jax.random.key(seed)
    ks = jax.random.split(key, 24)
    f32 = jnp.float32

    def nrm(k, shape, fan_in):
        return jax.random.normal(k, shape, f32) * (fan_in ** -0.5)

    def gain(k, shape):
        return 1.0 + 0.02 * jax.random.normal(k, shape, f32)

    u = jax.random.uniform(ks[10], (DEPTH, LRU_WIDTH), f32, 0.9, 0.999)
    a0 = u ** (1.0 / LRU_C)
    lam = jnp.log(a0) - jnp.log1p(-a0)
    return {
        'x': jax.random.normal(ks[0], (BATCH, SEQ, D_MODEL), f32),
        'p': jax.random.normal(ks[1], (DEPTH, BATCH, SEQ, PLE_DIM), f32),
        'norm_mix_g': gain(ks[2], (DEPTH, D_MODEL)),
        'w_in': nrm(ks[3], (DEPTH, D_MODEL, IN_WIDTH), D_MODEL),
        'conv_w': nrm(ks[4], (DEPTH, CONV_W_2, LRU_WIDTH), CONV_W_2),
        'conv_b': 0.02 * jax.random.normal(ks[5], (DEPTH, LRU_WIDTH), f32),
        'w_rgate': nrm(ks[6], (DEPTH, LRU_BLOCKS, LRU_BLOCK_W, LRU_BLOCK_W), LRU_BLOCK_W),
        'b_rgate': 0.02 * jax.random.normal(ks[7], (DEPTH, LRU_WIDTH), f32),
        'w_igate': nrm(ks[8], (DEPTH, LRU_BLOCKS, LRU_BLOCK_W, LRU_BLOCK_W), LRU_BLOCK_W),
        'b_igate': 0.02 * jax.random.normal(ks[9], (DEPTH, LRU_WIDTH), f32),
        'lru_lambda': lam,
        'w_br_lru': nrm(ks[11], (DEPTH, LRU_WIDTH, D_MODEL), LRU_WIDTH),
        'w_br_att': nrm(ks[12], (DEPTH, ATT_WIDTH, D_MODEL), ATT_WIDTH),
        'w_out': nrm(ks[13], (DEPTH, D_MODEL, D_MODEL), D_MODEL),
        'norm_mlp_g': gain(ks[14], (DEPTH, D_MODEL)),
        'w_mlp_up': nrm(ks[15], (DEPTH, D_MODEL, D_FF_2), D_MODEL),
        'w_mlp_down': nrm(ks[16], (DEPTH, D_FF_2, D_MODEL), D_FF_2),
        'norm_ple_g': gain(ks[17], (DEPTH, D_MODEL)),
        'w_ple_gate': nrm(ks[18], (DEPTH, D_MODEL, D_MODEL), D_MODEL),
        'w_ple': nrm(ks[19], (DEPTH, PLE_DIM, D_MODEL), PLE_DIM),
        'norm_final_g': gain(ks[20], (D_MODEL,)),
    }

def second_block(x, p, norm_mix_g, w_in, conv_w, conv_b, w_rgate, b_rgate, w_igate, b_igate,
              lru_lambda, w_br_lru, w_br_att, w_out, norm_mlp_g, w_mlp_up, w_mlp_down,
              norm_ple_g, w_ple_gate, w_ple, norm_final_g):
    B, S, _ = x.shape
    split_idx = [int(s) for s in np.cumsum(IN_SPLITS)[:-1]]
    for l in range(DEPTH):
        h = rmsnorm(x, norm_mix_g[l])
        proj = h @ w_in[l]
        u_x, u_g, q, k, v, g_lru, g_att = jnp.split(proj, split_idx, axis=-1)

        c = causal_depthwise_conv(u_x, conv_w[l], conv_b[l])
        y_lru = rg_lru(c, w_rgate[l], b_rgate[l], w_igate[l], b_igate[l], lru_lambda[l]) * jax.nn.gelu(u_g)

        to_heads = lambda t: t.reshape(B, S, ATT_HEADS, ATT_HEAD_DIM).transpose(0, 2, 1, 3)
        y_att = stick_breaking_attention(to_heads(q), to_heads(k), to_heads(v))
        y_att = y_att.transpose(0, 2, 1, 3).reshape(B, S, ATT_WIDTH)

        merged = jax.nn.sigmoid(g_lru) * (y_lru @ w_br_lru[l]) + jax.nn.sigmoid(g_att) * (y_att @ w_br_att[l])
        x = x + merged @ w_out[l]

        h2 = rmsnorm(x, norm_mlp_g[l])
        x = x + jnp.square(jax.nn.relu(h2 @ w_mlp_up[l])) @ w_mlp_down[l]

        h3 = rmsnorm(x, norm_ple_g[l])
        x = x + jax.nn.sigmoid(h3 @ w_ple_gate[l]) * (p[l] @ w_ple[l])
    return rmsnorm(x, norm_final_g)


def setup_inputs(seed=0):
    out = dict(first_inputs(seed))
    for name, value in second_inputs(seed + 1).items():
        if name != "x":
            out[name + "_2"] = value
    return out


def reference(
    x, positions, meta_tokens, pre_mix_norm, w_in, q_norm, w_uq, kv_norm, w_ukv, conv_w,
    attn_out_norm, conv_out_norm, w_out, post_mix_norm, pre_ffn_norm, w_group_router,
    b_group_router, w_expert_router, b_expert_router, w_gate, w_up, w_down, w_sh_gate, w_sh_up,
    w_sh_down, post_ffn_norm, p_2, norm_mix_g_2, w_in_2, conv_w_2, conv_b_2, w_rgate_2,
    b_rgate_2, w_igate_2, b_igate_2, lru_lambda_2, w_br_lru_2, w_br_att_2, w_out_2,
    norm_mlp_g_2, w_mlp_up_2, w_mlp_down_2, norm_ple_g_2, w_ple_gate_2, w_ple_2, norm_final_g_2,
):
    x = first_block(
        x, positions, meta_tokens, pre_mix_norm, w_in, q_norm, w_uq, kv_norm, w_ukv, conv_w,
        attn_out_norm, conv_out_norm, w_out, post_mix_norm, pre_ffn_norm, w_group_router,
        b_group_router, w_expert_router, b_expert_router, w_gate, w_up, w_down, w_sh_gate,
        w_sh_up, w_sh_down, post_ffn_norm,
    )
    return second_block(
        x, p_2, norm_mix_g_2, w_in_2, conv_w_2, conv_b_2, w_rgate_2, b_rgate_2, w_igate_2,
        b_igate_2, lru_lambda_2, w_br_lru_2, w_br_att_2, w_out_2, norm_mlp_g_2, w_mlp_up_2,
        w_mlp_down_2, norm_ple_g_2, w_ple_gate_2, w_ple_2, norm_final_g_2,
    )


_drawn_inputs = setup_inputs


def setup_inputs(seed=0):
    import zlib

    import numpy as np

    out = dict(_drawn_inputs(seed))
    spreads = {}
    factors = {'b_group_router': 4.257,
     'b_expert_router': 2.755,
     'norm_mix_g_2': 7.537,
     'conv_b_2': 3.743,
     'b_rgate_2': 31.076,
     'b_igate_2': 23.48,
     'norm_mlp_g_2': 16.132,
     'norm_ple_g_2': 200.0,
     'norm_final_g_2': 22.251,
     'p_2': 8.426,
     'w_ple_gate_2': 18.304,
     'w_ple_2': 8.485}
    for name, (base, spread) in spreads.items():
        noise = np.random.default_rng([zlib.crc32(name.encode()), seed]).standard_normal(out[name].shape)
        drawn = base * np.exp(spread * noise) if base else spread * noise
        out[name] = __import__('jax').numpy.asarray(drawn.astype(out[name].dtype))
    for name, factor in factors.items():
        out[name] = (out[name] * factor).astype(out[name].dtype)
    return out
```

```python
import math
from contextlib import ExitStack

import numpy as np
import concourse.bass as bass
from concourse import mybir

F32 = mybir.dt.float32
F32R = mybir.dt.float32r
BF16 = mybir.dt.bfloat16
I32 = mybir.dt.int32
ALU = mybir.AluOpType
ACT = mybir.ActivationFunctionType
AX = mybir.AxisListType

P = 128
D = 1024
DC = D // P
S = 256
META = 16
T = S + META
TT = S // P
EPS = 1e-6
HEADS, NOPE, ROPE, VD = 8, 64, 32, 64
QD = NOPE + ROPE
Q_LORA, KV_LORA, CONV = 256, 128, 512
ATTN = HEADS * VD
SCALE1 = QD ** -0.5
GROUPS, EPG, EXPERTS, FF = 4, 8, 32, 256
CAP = 64
RANKS = S
HEADS2, DH2 = 16, 64
SCALE2 = DH2 ** -0.5
FF2 = 4 * D
LRU_C = 8.0
MASKED = -(2.0 ** 100)

SLAB = 2048
RING = 12
RING2 = 8
NB = 4
UNIT = 1024

SLABS1 = [("cq", 2), ("kv", 2), ("gc0", 2), ("gc1", 2), ("xin0", 2), ("xin1", 2), ("gb0", 2), ("gb1", 2),
          ("uq", 8), ("ukv", 1), ("out0", 2), ("out1", 2), ("out2", 2), ("out3", 2),
          ("shg", 2), ("shu", 2), ("shd", 2)]
N1 = len(SLABS1)
SHIFT1 = (-N1) % RING
U1 = sum(n for _, n in SLABS1)
UNITS1 = [(i, name, j) for i, (name, n) in enumerate(SLABS1) for j in range(n)]
LAST1 = [max(u for u, (i, _, _) in enumerate(UNITS1) if i == s) for s in range(N1)]
FIRST1 = {name: min(u for u, (i, _, _) in enumerate(UNITS1) if i == s) for s, (name, _) in enumerate(SLABS1)}
BY_VECTOR = ("xin0", "xin1", "gb0", "gb1")
UNCOUNTED = ("ukv", "shu", "shd")

SLABS2 = ([("col", "w_in_2", s) for s in range(8)] + [("lru", "", 0)] + [("col", "w_in_2", s) for s in range(8, 28)]
          + [("col", "w_br_lru_2", s) for s in range(4)] + [("col", "w_br_att_2", s) for s in range(4)]
          + [("col", "w_out_2", s) for s in range(4)]
          + [(("col", "w_mlp_up_2", s), ("row", "w_mlp_down_2", s))[k] for s in range(FF2 // 256) for k in range(2)]
          + [("col", "w_ple_gate_2", 0), ("row", "w_ple_2", 0)] + [("col", "w_ple_gate_2", s) for s in (1, 2, 3)])
N2 = len(SLABS2)
UNITS2 = [(m, j) for m, (kind, _, _) in enumerate(SLABS2) if kind != "lru" for j in range(2)]
U2 = len(UNITS2)
SLAB_LRU = 8
SLAB_MLP = 28 + 3 * 4 + 1
U_IN, U_GATT, U_BRL, U_BRA, U_OUT, U_MLP, U_PLE = 0, 48, 56, 64, 72, 80, 144

VEC1 = [("pre_mix_norm", 8), ("post_mix_norm", 8), ("pre_ffn_norm", 8), ("post_ffn_norm", 8), ("q_norm", 2),
        ("kv_norm", 1), ("attn_out_norm", 4), ("conv_out_norm", 4), ("conv_w", 12)]
VEC2 = [("norm_mix_g_2", 8), ("conv_w_2", 32), ("conv_b_2", 8), ("b_rgate_2", 8), ("b_igate_2", 8),
        ("lru_lambda_2", 8), ("norm_mlp_g_2", 8), ("norm_ple_g_2", 8), ("norm_final_g_2", 8)]


def offsets(table):
    at, out = 0, {}
    for name, n in table:
        out[name] = at
        at += n
    return out, at


V1, NV1 = offsets(VEC1)
V2, NV2 = offsets(VEC2)
NORMS = [("pre_mix", 8), ("ckv", 1), ("cq", 2), ("conv", 4), ("attn", 4), ("post_mix", 8), ("pre_ffn", 8),
         ("post_ffn", 8), ("mix2", 8), ("mlp2", 8), ("ple2", 8), ("final2", 8)]
SQ_AT, _ = offsets(NORMS)
NORM_NO = {name: i for i, (name, _) in enumerate(NORMS)}
NCH = dict(NORMS)
SPLITS = [("pre_mix", 8), ("ckv", 1), ("cq", 2), ("conv", 4), ("attn", 4), ("ffn", 8), ("shared", 2),
          ("mix2", 8), ("y_lru", 8), ("y_att", 8), ("merged2", 8), ("mlp2", 8), ("p2", 2), ("ple2", 8)]
SP_AT, _ = offsets(SPLITS)
NSP = dict(SPLITS)


def build(nc, A, out):
    ctx = ExitStack()
    with ctx:
        def sb(name, shape, dt=F32):
            return ctx.enter_context(nc.sbuf_tensor(name, shape, dt))

        made = {}

        def ev(name):
            if name not in made:
                made[name] = ctx.enter_context(nc.semaphore(name))
            return made[name]

        y_rows = nc.dram_tensor("expert_rows", [EXPERTS * CAP, D], F32, kind="Internal").ap()
        y_more = nc.dram_tensor("expert_rows_behind", [EXPERTS * (RANKS - CAP), D], F32, kind="Internal").ap()

        ARENA = RING * SLAB
        big = sb("big", [P, ARENA + 8448])
        WH = sb("WH", [P, NB, UNIT], F32R)
        WL = sb("WL", [P, NB, UNIT], F32R)
        XH = sb("XH", [P, DC * T], F32R)
        XL = sb("XL", [P, DC * T], F32R)
        HH = sb("HH", [P, 2, S], F32R)
        HL = sb("HL", [P, 2, S], F32R)
        KH = sb("KH", [P, 3 * P], F32R)
        KL = sb("KL", [P, 3 * P], F32R)
        hT = sb("hT", [P, DC, T])
        XT = sb("XT", [P, 2, T])
        std = sb("std", [P, T])
        rstd = sb("rstd", [P, T])
        cos_t = sb("cos_t", [P, T])
        sin_t = sb("sin_t", [P, T])
        ident = sb("ident", [P, P])
        ones = sb("ones", [P, P])
        before = sb("before", [P, P])
        swap = sb("swap", [QD, QD])
        causal = sb("causal", [P, P])
        strict = sb("strict", [P, P])
        sel = sb("sel", [P, 2, TT, 2 * CAP], F32R)
        w_router = sb("w_router", [P, DC, GROUPS + EXPERTS])
        b_router = sb("b_router", [1, GROUPS + EXPERTS])
        vec1 = sb("vec1", [P, NV1])
        vec2 = sb("vec2", [P, NV2])
        rank_or = sb("rank_or", [P, TT, EXPERTS + 2])
        iota_slot = sb("iota_slot", [P, CAP])
        iota_e = sb("iota_e", [P, EXPERTS])
        small = sb("small", [P, 12])
        small_lru = sb("small_lru", [P, 5 * DC])
        overflow = sb("overflow", [1, 1], I32)
        slot_i = sb("slot_i", [P, 4 * TT], I32)
        ps = ctx.enter_context(nc.psum_tensor("ps", [P, 8, 512], F32))

        def ar(a, n, **k):
            return big[:, ARENA + a:ARENA + a + n]

        def slot(s):
            return big[:, s * SLAB:(s + 1) * SLAB]

        x_tok = ar(0, 3 * D).rearrange("p (t d) -> p t d", t=3)
        vrow1, vrow2 = ar(3072, P), ar(3200, P)
        inv_row, pos_row = ar(3328, P), ar(3456, T)
        pos_int = ar(3728, S).bitcast(I32)
        kpe = ar(0, T)
        cq = ar(272, 2 * T).rearrange("p (c t) -> p c t", c=2)
        ckv = ar(816, T)
        u = ar(1088, 4 * T).rearrange("p (c t) -> p c t", c=4)
        yc = ar(2176, 4 * S).rearrange("p (c t) -> p c t", c=4)
        vtok = ar(640, 3 * ATTN).rearrange("p (k n) -> p k n", k=3)
        qcat = ar(3200, HEADS * S).rearrange("p (h t) -> p h t", h=HEADS)
        kcat = ar(5248, HEADS * T).rearrange("p (h t) -> p h t", h=HEADS)
        prob = ar(7424, 2 * T).rearrange("p (b t) -> p b t", b=2)
        probT = ar(7968, 3 * P).rearrange("p (k t) -> p k t", k=3)
        rope_a = ar(7424, 2 * S)
        ang = ar(5248, T)
        ang_k = ar(5520, T)
        aT = ar(2176, 4 * S).rearrange("p (c t) -> p c t", c=4)
        mixT = ar(3200, DC * S).rearrange("p (c t) -> p c t", c=DC)
        tT = ar(5248, DC * S).rearrange("p (c t) -> p c t", c=DC)
        xg = ar(0, 2 * DC * 2 * CAP).rearrange("p (b c s) -> p b c s", b=2, c=DC)
        yrow = ar(2048, 2 * D).rearrange("p (b d) -> p b d", b=2)
        gact = ar(4096, FF)
        hid = ar(4352, FF)
        hidT = ar(4608, FF).rearrange("p (f s) -> p f s", f=2)
        sact = ar(4608, 2 * S).rearrange("p (f t) -> p f t", f=2)
        rt = ar(7296, 1152)
        shT = ar(5248, DC * S).rearrange("p (c t) -> p c t", c=DC)
        gath = ar(0, 4 * D).rearrange("p (k d) -> p k d", k=4)
        gath_more = big[:, RING2 * SLAB:RING2 * SLAB + 4 * D].rearrange("p (k d) -> p k d", k=4)
        Z0 = RING2 * SLAB

        def z(g):
            return big[:, Z0 + g * SLAB:Z0 + (g + 1) * SLAB].rearrange("p (c t) -> p c t", c=DC)

        zx, zg, zq, zk, zv, zl, zc, zi = (z(g) for g in range(8))
        vtok2 = big[:, Z0 + 6 * SLAB:Z0 + 7 * SLAB].rearrange("p (k n) -> p k n", k=TT)

        def att_buf(i):
            g = (0, 4, 7)[i // 4]
            at = Z0 + g * SLAB + (i % 4) * 512
            return big[:, at:at + 512]

        def cum(b):
            at = Z0 + 4 * SLAB + b * 2 * (S + 1)
            return big[:, at:at + 2 * (S + 1)].rearrange("p (h k) -> p h k", h=2)

        def att(b):
            at = (Z0 + 4 * SLAB + 4 * (S + 1), Z0 + 7 * SLAB + 512)[b]
            return big[:, at:at + 2 * S].rearrange("p (h k) -> p h k", h=2)

        def p_tok(t):
            return big[:, Z0 + 6 * SLAB + t * 256:Z0 + 6 * SLAB + (t + 1) * 256]

        def out_tok(k):
            return big[:, Z0 + (2 + k) * SLAB:Z0 + (2 + k) * SLAB + D]

        zero_w = cos_t[0:1, 0:P // 2].bitcast(BF16)
        zero_x = sin_t[0:1, 0:256].bitcast(BF16)

        X8 = lambda t, n: t[:, 0:DC * n].rearrange("p (c t) -> p c t", c=DC)
        xh1, xl1 = X8(XH, T), X8(XL, T)
        xh2, xl2 = X8(XH, S), X8(XL, S)
        th = XH[:, 0:TT * D].rearrange("p (k d) -> p k d", k=TT)
        tl = XL[:, 0:TT * D].rearrange("p (k d) -> p k d", k=TT)
        hx = hT[:, :, META:T]

        def pcn(ap, c=DC):
            return ap.rearrange("(c p) n -> p c n", p=P)

        w_in, w_uq, w_ukv, w_out = A["w_in"][0], A["w_uq"][0], A["w_ukv"][0], A["w_out"][0]

        def pack1(u_no, buf):
            i, name, j = UNITS1[u_no]
            s = slot((i + SHIFT1) % RING)
            if name == "kv":
                v = s[:, 0:8 * 160].rearrange("p (c n) -> p c n", c=DC)
                o = buf.rearrange("p (c n) -> p c n", c=DC)
                if j == 0:
                    return v[:, :, 0:P], o
                rep = v[:, :, P:P + ROPE].unsqueeze(2).to_broadcast([P, DC, 4, ROPE])
                return rep, buf.rearrange("p (c r n) -> p c r n", c=DC, r=4)
            if name == "uq":
                v = s[:, 0:2 * 768].rearrange("p (c n) -> p c n", c=2)
                return v[:, :, j * QD:(j + 1) * QD], buf[:, 0:2 * QD].rearrange("p (c n) -> p c n", c=2)
            if name == "ukv":
                v = s[:, 0:D].rearrange("p (h two n) -> p two h n", h=HEADS, two=2)
                return v, buf.rearrange("p (two h n) -> p two h n", h=HEADS, two=2)
            if name == "shd":
                return s[:, j * D:(j + 1) * D], buf
            return col_half(s, j), buf.rearrange("p (c n) -> p c n", c=DC)

        def col_half(s, j):
            return s.rearrange("p (c n) -> p c n", c=DC)[:, :, j * P:(j + 1) * P]

        def pack2(u_no, buf):
            m, j = UNITS2[u_no]
            s = slot(m % RING2)
            if SLABS2[m][0] == "row":
                return s[:, j * D:(j + 1) * D], buf
            return col_half(s, j), buf.rearrange("p (c n) -> p c n", c=DC)

        def slab1(i):
            s = (i + SHIFT1) % RING
            return ev(f"slab_in_slot_{s}"), 16 * (1 + sum((k + SHIFT1) % RING == s for k in range(i)))

        uses1 = [sum((k + SHIFT1) % RING == s for k in range(N1)) for s in range(RING)]
        GROUP = 4
        TURNS = EXPERTS // GROUP

        def slab_e(i, s):
            return ev(f"slab_in_slot_{s}"), 16 * (uses1[s] + 1) + i * 16

        def slab2(m, turn=None, per=0):
            s = m % RING2
            v = 16 * (uses1[s] + TURNS + m // RING2 + 1)
            return ev(f"slab_in_slot_{s}"), v if turn is None else turn * (16 * per // RING2) + v

        def taken1(u_no):
            names = [UNITS1[k][1] for k in range(u_no + 1) if UNITS1[k][1] not in UNCOUNTED]
            mine = names[-1] in BY_VECTOR
            n = sum((x in BY_VECTOR) == mine for x in names)
            return ev("unit_taken_by_vector" if mine else "unit_taken_by_scalar"), n

        TAKEN_S1 = sum(n for x, n in SLABS1 if x not in BY_VECTOR + UNCOUNTED)
        TAKEN_V1 = sum(n for x, n in SLABS1 if x in BY_VECTOR)

        g1 = lambda name, c=0: vec1[:, V1[name] + c:V1[name] + c + 1]
        g2 = lambda name, c=0: vec2[:, V2[name] + c:V2[name] + c + 1]

        def rts(a, n, k=None):
            v = rt[:, a:a + TT * n]
            return v.rearrange("p (t n) -> p t n", t=TT)

        logit = rts(0, 36)
        glog, elog = logit[:, :, 0:GROUPS], logit[:, :, GROUPS:]
        r_oh1, r_oh2 = rts(72, 32), rts(136, 32)
        r_em, r_key = rts(200, 32), rts(264, 32)
        r_m = rts(392, 32)
        r_g4, r_g4k, r_ohg = rts(456, 4), rts(464, 4), rts(472, 4)
        r_ge = rts(480, 4)
        r_s = lambda i: rt[:, 488 + 2 * i:490 + 2 * i]
        w_k = lambda k: small[:, 2 * k:2 * k + 2]
        behind = lambda k: small[:, 4 + 2 * k:6 + 2 * k]
        before_cap = lambda k: small[:, 8 + 2 * k:10 + 2 * k]

        block = ctx.enter_context(nc.Block())

        @block.sync
        def _(sp):
            for k in range(TT):
                sp.dma_start(x_tok[:, k, :], A["x"][0, k * P:(k + 1) * P, :]).then_inc(ev("x_loaded"), 16)
            sp.dma_start(x_tok[0:META, 2, :], A["meta_tokens"]).then_inc(ev("x_loaded"), 16)
            cols = {"cq": (0, 256), "kv": (256, 416), "gb0": (416, 672), "gb1": (672, 928), "gc0": (928, 1184),
                    "gc1": (1184, 1440), "xin0": (1440, 1696), "xin1": (1696, 1952)}
            for i, (name, _) in enumerate(SLABS1):
                if i >= RING:
                    sp.wait_ge(ev("unit_split"), LAST1[i - RING] + 1)
                s = slot((i + SHIFT1) % RING)
                if name in cols:
                    a, b = cols[name]
                    dst, src = s[:, 0:DC * (b - a)].rearrange("p (c n) -> p c n", c=DC), pcn(w_in)[:, :, a:b]
                elif name == "uq":
                    dst, src = s[:, 0:2 * 768].rearrange("p (c n) -> p c n", c=2), pcn(w_uq)
                elif name == "ukv":
                    dst, src = s[:, 0:D], w_ukv
                elif name.startswith("out"):
                    a = 256 * int(name[3:])
                    dst, src = s.rearrange("p (c n) -> p c n", c=DC), pcn(w_out)[:, :, a:a + 256]
                elif name in ("shg", "shu"):
                    w = A["w_sh_gate" if name == "shg" else "w_sh_up"][0]
                    dst, src = s.rearrange("p (c n) -> p c n", c=DC), pcn(w)
                else:
                    dst, src = s.rearrange("p (c n) -> p c n", c=2), pcn(A["w_sh_down"][0])
                sp.dma_start(dst, src).then_inc(slab1(i)[0], 16)

            def expert_slab(e, s, kind):
                if kind < 2:
                    w = A["w_gate" if kind == 0 else "w_up"][0]
                    src = w[bass.ds(e, 1)].rearrange("e (p c) n -> p (e c) n", p=P)
                    dst = slot(s).rearrange("p (c n) -> p c n", c=DC)
                else:
                    src = A["w_down"][0][bass.ds(e, 1)].rearrange("e (c p) n -> p (e c) n", p=P)
                    dst = slot(s).rearrange("p (c n) -> p c n", c=2)
                sp.dma_start(dst, src).then_inc(ev(f"slab_in_slot_{s}"), 16)

            KINDS = [(0, 0), (1, 0), (0, 1), (1, 1), (0, 2), (1, 2)]

            for s in range(RING):
                last = max(i for i in range(N1) if (i + SHIFT1) % RING == s)
                sp.wait_ge(ev("unit_split"), LAST1[last] + 1)
                e, kind = KINDS[s % 6]
                expert_slab(2 * (s // 6) + e, s, kind)
            with sp.Fori(0, TURNS - 1) as i:
                for s in range(RING):
                    sp.wait_ge(ev("expert_slab_used"), i * RING + (s + 1))
                    e, kind = KINDS[s % 6]
                    expert_slab(i * GROUP + (GROUP + 2 * (s // 6) + e), s, kind)

            def second_slab(m, ds=0):
                kind, name, j = SLABS2[m]
                s = slot(m % RING2)
                if kind == "lru":
                    for k, (w, done) in enumerate(((A["w_rgate_2"], ev("rgate_loaded")), (A["w_igate_2"], slab2(m)[0]))):
                        sp.dma_start(s[:, k * 512:(k + 1) * 512].rearrange("p (c n) -> p c n", c=DC),
                                     w[0].rearrange("(c b) r n -> (b r) c n", b=2)).then_inc(done, 16)
                    return
                w = A[name][0]
                if kind == "col":
                    sp.dma_start(s.rearrange("p (c n) -> p c n", c=DC),
                                 pcn(w)[:, :, bass.ds(j * 256 + ds, 256)]).then_inc(slab2(m)[0], 16)
                else:
                    sp.dma_start(s.rearrange("p (c n) -> p c n", c=2),
                                 w[bass.ds(j * 256 + ds, 256), :].rearrange("(c p) n -> p c n", p=P))\
                        .then_inc(slab2(m)[0], 16)

            for m in range(RING2):
                sp.wait_ge(ev("expert_slab_used"), RING * (TURNS - 1) + m + 1)
                second_slab(m)

            def slot_empty(m):
                before_m = m - RING2
                if before_m == SLAB_LRU:
                    sp.wait_ge(ev("gates_done"), DC)
                else:
                    done = max(k for k, (mm, _) in enumerate(UNITS2) if mm == before_m) + 1
                    sp.wait_ge(ev("unit_split"), U1 + done)

            for m in range(RING2, SLAB_MLP + RING2):
                slot_empty(m)
                second_slab(m)
            with sp.Fori(0, 3) as i:
                for m in range(SLAB_MLP + RING2, SLAB_MLP + 2 * RING2):
                    sp.wait_ge(ev("unit_split"), i * (2 * RING2) + (U1 + U_MLP + 2 * (m - RING2 - SLAB_MLP + 1)))
                    second_slab(m, i * (RING2 // 2 * 256))
            for m in range(SLAB_MLP + 4 * RING2, N2):
                slot_empty(m)
                second_slab(m)

            for k in range(TT):
                sp.wait_ge(ev("out_tokens_by_scalar"), k + 1)
                sp.wait_ge(ev("out_tokens_by_vector"), k + 1)
                sp.dma_start(out[0, k * P:(k + 1) * P, :], out_tok(k))\
                    .then_inc(ev("out_stored"), 16)
            sp.wait_ge(ev("out_stored"), 16 * TT)

        @block.gpsimd
        def _(pool):
            g = nc.gpsimd
            row = 0
            for name, n in VEC2:
                v = A[name] if name == "norm_final_g_2" else A[name][0]
                if len(v.shape) == 2:
                    v = v.rearrange("k n -> (k n)")
                pool.dma_start(vrow2[row:row + n, :], v.rearrange("(c p) -> c p", p=P)).then_inc(ev("vec2_loaded"), 16)
                row += n
            g.memset(ident[:], 0.0).then_inc(ev("pool_zeroed"), 1)
            g.memset(before[:], 0.0).then_inc(ev("pool_zeroed"), 1)
            g.memset(swap[:], 0.0).then_inc(ev("pool_zeroed"), 1)
            g.memset(causal[:], 0.0).then_inc(ev("pool_zeroed"), 1)
            g.memset(strict[:], 0.0).then_inc(ev("pool_zeroed"), 1)
            g.memset(inv_row[0:1, :], 0.0).then_inc(ev("pool_zeroed"), 1)
            pool.wait_ge(ev("pool_zeroed"), 6)
            g.affine_select(out=ident[:], in_=ident[:], compare_op=ALU.not_equal, fill=1.0, base=0,
                            pattern=[[-1, P]], channel_multiplier=1).then_inc(ev("ident_ready"), 1)
            g.memset(zero_w, 0.0).then_inc(ev("zeros_ready"), 1)
            g.memset(zero_x, 0.0).then_inc(ev("zeros_ready"), 1)
            g.memset(ones[:], 1.0).then_inc(ev("ones_ready"), 1)
            for f in range(ROPE // 2):
                inv = float(np.float32(1.0) / np.float32(np.float32(10000.0) ** np.float32(2 * f / ROPE)))
                g.memset(inv_row[0:1, NOPE + f:QD:ROPE // 2], inv).then_inc(ev("inv_ready"), 1)
            g.affine_select(out=before[:], in_=before[:], compare_op=ALU.is_ge, fill=1.0, base=0,
                            pattern=[[-1, P]], channel_multiplier=1).then_inc(ev("routing_consts"), 1)
            g.affine_select(out=causal[:], in_=causal[:], compare_op=ALU.is_ge, fill=MASKED, base=0,
                            pattern=[[-1, P]], channel_multiplier=1).then_inc(ev("masks_ready"), 1)
            g.affine_select(out=strict[:], in_=strict[:], compare_op=ALU.is_gt, fill=MASKED, base=0,
                            pattern=[[-1, P]], channel_multiplier=1).then_inc(ev("masks_ready"), 1)
            half = ROPE // 2
            a = swap[:, NOPE:NOPE + half]
            g.affine_select(out=a, in_=a, compare_op=ALU.not_equal, fill=-1.0, base=-(NOPE + half),
                            pattern=[[-1, half]], channel_multiplier=1).then_inc(ev("swap_ready"), 1)
            a = swap[:, NOPE + half:QD]
            g.affine_select(out=a, in_=a, compare_op=ALU.not_equal, fill=1.0, base=-NOPE,
                            pattern=[[-1, half]], channel_multiplier=1).then_inc(ev("swap_ready"), 1)
            g.iota(iota_slot[:], [[1, CAP]], base=0, channel_multiplier=0,
                   allow_small_or_imprecise_dtypes=True).then_inc(ev("routing_consts"), 1)
            g.iota(iota_e[:], [[1, EXPERTS]], base=0, channel_multiplier=0,
                   allow_small_or_imprecise_dtypes=True).then_inc(ev("routing_consts"), 1)
            g.iota(pos_row[0:1, 0:META], [[1, META]], base=0, channel_multiplier=0,
                   allow_small_or_imprecise_dtypes=True).then_inc(ev("meta_pos"), 1)
            g.memset(rank_or[:], -1.0).then_inc(ev("routing_consts"), 1)

            pool.sem_inc(ev("row_buffer_free"), 2)
            with pool.Fori(0, TURNS) as i:
                for h in range(2):
                    pool.wait_ge(ev("rows_by_scalar"), i * 2 + (h + 1 + 2))
                    pool.wait_ge(ev("rows_by_vector"), i * 2 + (h + 1 + 2))
                    pool.dma_start(y_rows[bass.ds((i * 2 + h) * (2 * CAP), 2 * CAP), :], yrow[:, h, :])\
                        .then_inc(ev("rows_stored"), 16)
                    pool.wait_ge(ev("rows_stored"), i * 32 + 16 * (h + 1))
                    pool.sem_inc(ev("row_buffer_free"), 1)
            pool.wait_ge(ev("overflow_known"), 1)
            more = pool.value_load(overflow[0:1, 0:1], min_val=0, max_val=1)
            with pool.If(more > 0):
                with pool.Fori(0, RANKS // CAP - 1) as r:
                    with pool.Fori(0, EXPERTS) as e:
                        b = r * EXPERTS + e
                        for kind, w in enumerate((A["w_gate"], A["w_up"], A["w_down"])):
                            lay = "e (p c) n -> p (e c) n" if kind < 2 else "e (c p) n -> p (e c) n"
                            pool.dma_start(slot(RING2 + kind).rearrange("p (c n) -> p c n", c=DC if kind < 2 else 2),
                                           w[0][bass.ds(e, 1)].rearrange(lay, p=P)).then_inc(ev("o_loaded"), 16)
                        pool.wait_ge(ev("o_rows"), 2 * b + 2)
                        pool.dma_start(y_more[bass.ds(e * (RANKS - CAP) + r * CAP, CAP), :], yrow[0:CAP, 0, :])\
                            .then_inc(ev("o_stored"), 16)
                        pool.wait_ge(ev("o_stored"), b * 16 + 16)
                for k in range(2 * TT):
                    g.indirect_dma_start(gath_more[:, k, :], None, y_more[:, :],
                                         bass.IndirectOffsetOnAxis(ap=slot_i[:, 2 * TT + k:2 * TT + k + 1], axis=0))\
                        .then_inc(ev("o_rows_gathered"), 16)
            for k in range(2):
                for t in range(TT):
                    g.indirect_dma_start(gath[:, 2 * k + t, :], None, y_rows[:, :],
                                         bass.IndirectOffsetOnAxis(ap=slot_i[:, 2 * k + t:2 * k + t + 1], axis=0))\
                        .then_inc(ev("rows_gathered"), 16)
            pool.wait_ge(ev("y_att"), HEADS2)
            for t in range(TT):
                pool.dma_start(p_tok(t), A["p_2"][0, 0, t * P:(t + 1) * P, :]).then_inc(ev("p_loaded"), 16)

        @block.scalar
        def _(act):
            s = nc.scalar
            row = 0
            act.dma_start(pos_int[0:1, :], A["positions"]).then_inc(ev("pos_loaded"), 16)
            for name, n in VEC1:
                v = A[name][0]
                if len(v.shape) == 2:
                    v = v.rearrange("k n -> (k n)")
                act.dma_start(vrow1[row:row + n, :], v.rearrange("(c p) -> c p", p=P)).then_inc(ev("vec1_loaded"), 16)
                row += n
            act.dma_start(w_router[:, :, 0:GROUPS], pcn(A["w_group_router"][0])).then_inc(ev("router_loaded"), 16)
            act.dma_start(w_router[:, :, GROUPS:], pcn(A["w_expert_router"][0])).then_inc(ev("router_loaded"), 16)
            act.dma_start(b_router[:, 0:GROUPS], A["b_group_router"]).then_inc(ev("router_loaded"), 16)
            act.dma_start(b_router[:, GROUPS:], A["b_expert_router"]).then_inc(ev("router_loaded"), 16)

            def high1(u_no):
                if u_no >= U1:
                    return
                if u_no >= NB:
                    act.wait_ge(ev("unit_used"), u_no - NB + 1)
                act.wait_ge(*slab1(UNITS1[u_no][0]))
                src, dst = pack1(u_no, WH[:, u_no % NB, :])
                s.activation(dst, src, ACT.Copy).then_inc(ev("unit_high"), 1)

            def high2(v, turn=None):
                if v >= U2:
                    return
                n = U1 + v
                m = UNITS2[v][0]
                base = 0 if turn is None else turn * 16
                act.wait_ge(ev("unit_used"), base + (n - NB + 1))
                act.wait_ge(*slab2(m, turn, RING2))
                src, dst = pack2(v, WH[:, v % NB, :])
                s.activation(dst, src, ACT.Copy).then_inc(ev("unit_high"), 1)

            def take1(u_no, dst, func=ACT.Copy, rows=P, n=T):
                act.wait_ge(ev("unit_used"), u_no + 1)
                s.activation(dst, ps[0:rows, u_no % 4, 0:n], func).then_inc(ev("unit_taken_by_scalar"), 1)

            def squares(name, srcs, n):
                k0, no = SQ_AT[name], NORM_NO[name]
                splits_before = {"pre_mix": 0, "ckv": 8, "cq": 9, "conv": 11, "attn": 15, "post_mix": 19,
                                 "pre_ffn": 19, "post_ffn": 29, "mix2": 29, "mlp2": 61, "ple2": 71, "final2": 79}
                if splits_before[name]:
                    act.wait_ge(ev("split_low"), splits_before[name])
                for c, src in enumerate(srcs):
                    k = k0 + c
                    if k >= 2:
                        act.wait_ge(ev("squares_summed"), k - 1)
                    s.activation(XT[:, k % 2, 0:n], src, ACT.Square).then_inc(ev("square_ready"), 1)
                act.wait_ge(ev("squares_summed"), k0 + len(srcs))
                if no:
                    act.wait_ge(ev("rstd_ready"), no)
                s.activation(std[:, 0:n], ps[:, 7, 0:n], ACT.Sqrt, scale=1.0 / (len(srcs) * P), bias=EPS)\
                    .then_inc(ev("std_ready"), 1)

            def highs(name, dsts, n, wait=None):
                if wait:
                    act.wait_ge(*wait)
                for c, dst in enumerate(dsts):
                    k = SP_AT[name] + c
                    act.wait_ge(ev("split_value"), k + 1)
                    s.activation(dst, XT[:, k % 2, 0:n], ACT.Copy).then_inc(ev("split_high"), 1)

            for k in range(NB - 1):
                high1(k)
            for c in range(0, DC, 2):
                act.wait_ge(ev("x_turned"), c + 1)
                s.activation(hT[:, c, :], ps[:, c % 4, 0:T], ACT.Copy).then_inc(ev("hT_by_scalar"), 1)
            act.wait_ge(ev("hT_by_scalar"), 4)
            act.wait_ge(ev("hT_by_vector"), 4)
            squares("pre_mix", [hT[:, c, :] for c in range(DC)], T)
            highs("pre_mix", [xh1[:, c, :] for c in range(DC)], T)
            for k, t in enumerate((sin_t, cos_t)):
                act.wait_ge(ev("angle_reduced"), k + 1)
                s.activation(t[NOPE:QD, :], (ang if k else ang_k)[NOPE:QD, :], ACT.Sin).then_inc(ev("rope_table"), 1)
            for k, dst in enumerate((cq[:, 0, :], cq[:, 1, :], ckv, kpe)):
                high1(k + 3)
                take1(k, dst)
            act.wait_ge(ev("unit_taken_by_scalar"), 3)
            squares("ckv", [ckv], T)
            for k in range(4):
                high1(k + 7)
                take1(FIRST1["gc0"] + k, u[:, k, :])
            highs("ckv", [KH[:, 0:T]], T, (ev("k_padded"), 2))
            squares("cq", [cq[:, c, META:T] for c in range(2)], S)
            highs("cq", [HH[:, c, :] for c in range(2)], S)
            for k in range(8):
                high1(k + 11)
            u0 = FIRST1["uq"]
            for k in range(HEADS):
                high1(u0 + 3 + k)
                if k == 0:
                    act.wait_ge(ev("unit_taken_by_vector"), 8)
                    squares("conv", [yc[:, c, :] for c in range(4)], S)
                    highs("conv", [xh2[:, 4 + c, :] for c in range(4)], S, (ev("unit_used"), FIRST1["gb0"] + 4))
                take1(u0 + k, qcat[0:QD, k, :], rows=QD, n=S)
            for h in range(HEADS):
                act.wait_ge(ev("nope_keys"), h + 1)
                if h == 0:
                    act.wait_ge(ev("rope_table"), 2)
                s.activation(kcat[0:NOPE, h, :], ps[0:NOPE, h % 4, 0:T], ACT.Copy)\
                    .then_inc(ev("nope_keys_taken"), 1)
            high1(u0 + 8 + 3)
            for n in range(HEADS * TT):
                h, qt = divmod(n, TT)
                keys = META + (qt + 1) * P
                b = n % 2
                act.wait_ge(ev("neg_max"), n + 1)
                if n >= 2:
                    act.wait_ge(ev("prob_turned"), n - 1)
                s.activation(prob[:, b, 0:keys], ps[:, 4 + b, 0:keys], ACT.Exp, scale=SCALE1,
                             bias=small[:, 6 + b:7 + b], accum_out=small[:, 8 + b:9 + b]).then_inc(ev("exp_done"), 1)
                act.wait_ge(ev("prob_turned"), n + 1)
                if n:
                    act.wait_ge(ev("att_out"), n)
                full = qt + 1
                s.activation(probT[:, 0:full, :], ps[:, 6, 0:full * P].rearrange("p (k t) -> p k t", k=full), ACT.Copy)
                s.activation(probT[0:META, 2, :], ps[0:META, 6, 3 * P:4 * P], ACT.Copy).then_inc(ev("probT_ready"), 1)
            act.wait_ge(ev("att_out"), HEADS * TT)
            act.wait_ge(ev("unit_taken_by_vector"), 8)
            act.wait_ge(ev("split_low"), SP_AT["attn"])
            for c in range(4):
                s.activation(aT[:, c, :], ps[:, c, 0:S], ACT.Copy).then_inc(ev("aT_ready"), 1)
            act.wait_ge(ev("aT_ready"), 4)
            squares("attn", [aT[:, c, :] for c in range(4)], S)
            highs("attn", [xh2[:, c, :] for c in range(4)], S)
            for k in range(8):
                uu = FIRST1["out0"] + k
                high1(uu + 3)
                take1(uu, mixT[:, k, :], n=S)
            act.wait_ge(ev("unit_taken_by_scalar"), taken1(FIRST1["out3"] + 1)[1])
            squares("post_mix", [mixT[:, c, :] for c in range(DC)], S)
            act.wait_ge(ev("h_mixed"), DC)
            squares("pre_ffn", [hx[:, c, :] for c in range(DC)], S)
            highs("ffn", [xh2[:, c, :] for c in range(DC)], S)
            u0 = FIRST1["shg"]
            for k in range(2):
                high1(u0 + 3 + k)
                take1(u0 + k, sact[:, k, :], func=ACT.Silu, n=S)
            high1(u0 + 5)
            act.wait_ge(ev("group_centred"), 1)
            s.activation(r_ge, r_g4, ACT.Exp).then_inc(ev("group_exp"), 1)
            act.wait_ge(ev("pair_diff"), 1)
            s.activation(r_s(5), r_s(4), ACT.Exp).then_inc(ev("pair_exp"), 1)
            highs("shared", [HH[:, c, :] for c in range(2)], S)
            for k in range(TT):
                act.wait_ge(ev("t_turned"), k + 1)
                s.activation(th[:, k, :].rearrange("p (b n) -> p b n", b=2), ps[:, 4:6, :], ACT.Copy)\
                    .then_inc(ev("th_ready"), 1)
            act.wait_ge(ev("unit_used"), U1)
            for k in range(2):
                s.activation(shT[:, 4 * k:4 * k + 4, :], ps[:, 2 * k:2 * k + 2, :].rearrange("p b (c t) -> p (b c) t", c=2),
                             ACT.Copy).then_inc(ev("shT_ready"), 1)

            def gathered(b, done):
                s.activation(xg[:, b, 0:4, :], ps[:, 0, :].rearrange("p (c s) -> p c s", c=4), ACT.Copy)\
                    .then_inc(done, 1)

            act.wait_ge(ev("first_half_gathered"), 1)
            gathered(0, ev("xg_by_scalar"))
            with act.Fori(0, TURNS) as i:
                for h in range(2):
                    act.wait_ge(ev("expert_slab_used"), i * RING + (6 * h + 2))
                    s.activation(gact, ps[:, 2, 0:FF], ACT.Silu).then_inc(ev("silu_done"), 1)
                    act.wait_ge(ev("first_half_gathered"), i * 2 + (h + 2))
                    gathered((h + 1) % 2, ev("xg_by_scalar"))
                    act.wait_ge(ev("expert_slab_used"), i * RING + (6 * h + 6))
                    act.wait_ge(ev("row_buffer_free"), i * 2 + (h + 1))
                    s.activation(yrow[:, h, 0:512], ps[:, 4 + 2 * h, :], ACT.Copy)\
                        .then_inc(ev("rows_by_scalar"), 1)
            act.wait_ge(ev("overflow_known"), 1)
            more = act.value_load(overflow[0:1, 0:1], min_val=0, max_val=1)
            with act.If(more > 0):
                with act.Fori(0, RANKS // CAP - 1) as r:
                    with act.Fori(0, EXPERTS) as e:
                        b = r * EXPERTS + e
                        act.wait_ge(ev("o_gate_up"), b + 1)
                        s.activation(gact[0:CAP, :], ps[0:CAP, 2, 0:FF], ACT.Silu).then_inc(ev("o_silu"), 1)
                        act.wait_ge(ev("o_down"), b + 1)
                        s.activation(yrow[0:CAP, 0, 0:512], ps[0:CAP, 4, :], ACT.Copy).then_inc(ev("o_rows"), 1)

            for v in range(NB - 1):
                high2(v)
            act.wait_ge(ev("lambda_abs"), 1)
            s.activation(small_lru[:, 2 * DC:3 * DC], small_lru[:, DC:2 * DC], ACT.Exp).then_inc(ev("lambda_exp"), 1)
            act.wait_ge(ev("ffn_ready"), DC)
            squares("post_ffn", [shT[:, c, :] for c in range(DC)], S)
            act.wait_ge(ev("h_ffn"), DC)
            squares("mix2", [hx[:, c, :] for c in range(DC)], S)
            highs("mix2", [xh2[:, c, :] for c in range(DC)], S)
            half_of = lambda t, b: t[:, 4 * b:4 * b + 4, :]
            for k in range(48):
                high2(k + 3)
                act.wait_ge(ev("unit_used"), U1 + k + 1)
                s.activation(z(k // DC)[:, k % DC, :], ps[:, k % 4, 0:S], ACT.Copy)\
                    .then_inc(ev("unit_taken_by_scalar"), 1)
                if k in (16, 17, 20, 21):
                    for c in range(*{16: (0, 2), 17: (2, 4), 20: (4, 6), 21: (6, 8)}[k]):
                        act.wait_ge(ev("gates_done"), c + 1)
                        s.activation(zx[:, c, :], ps[:, 4 + c % 4, 0:S], ACT.Sigmoid, bias=g2("b_rgate_2", c))
                        s.activation(zi[:, c, :], ps[:, 4 + c % 4, 256:512], ACT.Sigmoid, bias=g2("b_igate_2", c))\
                            .then_inc(ev("gate_act"), 1)
                if k in (27, 28):
                    if k == 27:
                        act.wait_ge(ev("log_a"), 4)
                        act.wait_ge(ev("gated_input"), 4)
                    s.activation(half_of(zc, k - 27), half_of(zx, k - 27), ACT.Tanh).then_inc(ev("tanh_done"), 1)
                if k in (29, 30):
                    act.wait_ge(ev("tanh_done"), k - 28)
                    s.activation(half_of(zx, k - 29), half_of(zx, k - 29), ACT.Exp).then_inc(ev("a_ready"), 1)
                if k in (31, 32):
                    if k == 31:
                        act.wait_ge(ev("unit_taken_by_scalar"), TAKEN_S1 + 16)
                    s.activation(half_of(zg, k - 31), half_of(zg, k - 31), ACT.Gelu_apprx_tanh)\
                        .then_inc(ev("gelu_done"), 1)
                if k in (38, 39):
                    act.wait_ge(ev("one_minus_a2"), 4 * (k - 37))
                    s.activation(half_of(zc, k - 38), half_of(zc, k - 38), ACT.Sqrt).then_inc(ev("mult_ready"), 1)
            act.wait_ge(ev("unit_taken_by_scalar"), TAKEN_S1 + 48)
            s.activation(zl, zl, ACT.Sigmoid).then_inc(ev("g_lru_ready"), 1)

            for k in range(TT):
                act.wait_ge(ev("v_turned"), k + 1)
                act.wait_ge(ev("lru_done"), 4)
                s.activation(vtok2[:, k, :].rearrange("p (b n) -> p b n", b=2), ps[:, 4:6, :], ACT.Copy)\
                    .then_inc(ev("v_ready"), 1)
            for n in range(HEADS2):
                j, qt = divmod(n, TT)
                keys = (qt + 1) * P
                b = n % 2
                if n >= 2:
                    act.wait_ge(ev("att_ready"), n - 1)
                act.wait_ge(ev("z_masked"), n + 1)
                zz = ps[:, 2 * b:2 * b + 2, 0:keys]
                beta = att_buf(b).rearrange("p (h k) -> p h k", h=2)[:, :, 0:keys]
                omb = att_buf(2 + b).rearrange("p (h k) -> p h k", h=2)[:, :, 0:keys]
                s.activation(omb, zz, ACT.Sigmoid, scale=-SCALE2).then_inc(ev("sigm_done"), 1)
                s.activation(beta, zz, ACT.Sigmoid, scale=SCALE2).then_inc(ev("sigm_done"), 1)
                act.wait_ge(ev("att_turned"), n + 1)
                if n:
                    act.wait_ge(ev("y_att"), n)
                s.activation(att_buf(8)[:, 0:2 * keys], ps[:, 4, 0:2 * keys], ACT.Copy).then_inc(ev("attT_ready"), 1)

            def take2(v, dst, func=ACT.Copy):
                act.wait_ge(ev("unit_used"), U1 + v + 1)
                s.activation(dst, ps[:, v % 4, 0:S], func).then_inc(ev("unit_taken_by_scalar"), 1)

            for k in range(8):
                high2(U_GATT + 3 + k)
                take2(U_GATT + k, zq[:, k, :], ACT.Sigmoid)
            highs("y_lru", [xh2[:, c, :] for c in range(DC)], S, (ev("unit_used"), U1 + U_BRL))
            for k in range(8):
                high2(U_BRL + 3 + k)
            highs("y_att", [xh2[:, c, :] for c in range(DC)], S, (ev("unit_used"), U1 + U_BRA))
            for k in range(8):
                high2(U_BRA + 3 + k)
            highs("merged2", [xh2[:, c, :] for c in range(DC)], S, (ev("unit_used"), U1 + U_OUT))
            for k in range(8):
                high2(U_OUT + 3 + k)
            act.wait_ge(ev("h_mixed2"), DC)
            squares("mlp2", [hx[:, c, :] for c in range(DC)], S)
            highs("mlp2", [xh2[:, c, :] for c in range(DC)], S)
            with act.Fori(0, 4) as i:
                for v in range(16):
                    high2(U_MLP + v + 3, i)
                    if v % 4 < 2:
                        f = (v // 4) * 2 + v % 4
                        act.wait_ge(ev("relu_done"), i * 8 + (f + 1))
                        act.wait_ge(ev("unit_used"), i * 16 + (U1 + U_MLP + v - 1))
                        s.activation(HH[:, f % 2, :], zx[:, f % 2, :], ACT.Copy).then_inc(ev("relu_high"), 1)
            highs("p2", [HH[:, c, :] for c in range(2)], S, (ev("unit_used"), U1 + U_PLE))
            act.wait_ge(ev("h_mlp"), DC)
            squares("ple2", [hx[:, c, :] for c in range(DC)], S)
            highs("ple2", [xh2[:, c, :] for c in range(DC)], S)
            for k in range(10):
                v = U_PLE + k
                high2(v + 3)
                if SLABS2[UNITS2[v][0]][0] == "col":
                    g = k if k < 2 else k - 2
                    take2(v, zq[:, g, :], ACT.Sigmoid)
            act.wait_ge(ev("h_ple"), DC)
            squares("final2", [hx[:, c, :] for c in range(DC)], S)
            for k in range(TT):
                act.wait_ge(ev("result_turned"), k + 1)
                s.activation(out_tok(k)[:, 0:512], ps[:, 4 * k, :], ACT.Copy)\
                    .then_inc(ev("out_tokens_by_scalar"), 1)

        @block.vector
        def _(dve):
            v = nc.vector
            steps = [0]

            def chain(ins):
                steps[0] += 1
                ins.then_inc(ev("vector_step"), 1)
                dve.wait_ge(ev("vector_step"), steps[0])

            def low1(u_no):
                if u_no >= U1:
                    return
                dve.wait_ge(ev("unit_high"), u_no + 1)
                src, h = pack1(u_no, WH[:, u_no % NB, :])
                _, dst = pack1(u_no, WL[:, u_no % NB, :])
                v.tensor_tensor(dst, src, h.bitcast(F32), ALU.subtract).then_inc(ev("unit_split"), 1)

            def low2(k, turn=None):
                if k >= U2:
                    return
                base = 0 if turn is None else turn * 16
                dve.wait_ge(ev("unit_high"), base + (U1 + k + 1))
                src, h = pack2(k, WH[:, k % NB, :])
                _, dst = pack2(k, WL[:, k % NB, :])
                v.tensor_tensor(dst, src, h.bitcast(F32), ALU.subtract).then_inc(ev("unit_split"), 1)

            def root(name, n):
                no = NORM_NO[name]
                dve.wait_ge(ev("std_ready"), no + 1)
                v.reciprocal(rstd[:, 0:n], std[:, 0:n]).then_inc(ev("rstd_ready"), 1)
                dve.wait_ge(ev("rstd_ready"), no + 1)

            def split(name, make, lows, n, highs_):
                k0 = SP_AT[name]

                def low(c):
                    k = k0 + c
                    dve.wait_ge(ev("split_high"), k + 1)
                    v.tensor_tensor(lows[c], XT[:, k % 2, 0:n], highs_[c].bitcast(F32), ALU.subtract)\
                        .then_inc(ev("split_low"), 1)

                for c in range(NSP[name]):
                    k = k0 + c
                    if c >= 2:
                        dve.wait_ge(ev("split_low"), k - 1)
                    make(c, XT[:, k % 2, 0:n]).then_inc(ev("split_value"), 1)
                    if c:
                        low(c - 1)
                low(NSP[name] - 1)

            def scaled(srcs, gains, n):
                return lambda c, dst: v.scalar_tensor_tensor(out=dst, in0=srcs[c], scalar=gains[c], in1=rstd[:, 0:n],
                                                             op0=ALU.mult, op1=ALU.mult)

            ch = lambda t, a=0, b=DC: [t[:, c, :] for c in range(a, b)]

            v.memset(KH[:, T:].bitcast(F32), 0.0).then_inc(ev("k_padded"), 1)
            v.memset(KL[:, T:].bitcast(F32), 0.0).then_inc(ev("k_padded"), 1)
            dve.wait_ge(ev("vrows_turned"), 2)
            v.tensor_copy(vec1[:], ps[:, 6, 0:NV1]).then_inc(ev("vecs_ready"), 1)
            v.tensor_copy(vec2[:], ps[:, 6, P:P + NV2]).then_inc(ev("vecs_ready"), 1)
            for c in range(1, DC, 2):
                dve.wait_ge(ev("x_turned"), c + 1)
                v.tensor_copy(hT[:, c, :], ps[:, c % 4, 0:T]).then_inc(ev("hT_by_vector"), 1)
            dve.wait_ge(ev("pos_loaded"), 16)
            v.tensor_scalar(pos_row[0:1, META:T], pos_int[0:1, :], float(META), None, ALU.add)\
                .then_inc(ev("pos_ready"), 1)
            dve.wait_ge(ev("vecs_ready"), 2)
            for k in range(NB - 1):
                low1(k)
            root("pre_mix", T)
            split("pre_mix", scaled(ch(hT), [g1("pre_mix_norm", c) for c in range(DC)], T), ch(xl1), T, ch(xh1))
            two_pi = 2 * math.pi
            p1 = 6.28125
            p2 = float(np.float32(np.round((two_pi - p1) * 2 ** 20) / 2 ** 20))
            p3 = two_pi - p1 - p2
            magic = 1.5 * 2 ** 23
            lim = 3.1415925
            dve.wait_ge(ev("angles"), 1)
            rows = slice(NOPE, QD)
            angp = ps[rows, 5, 0:T]
            for k, dst in enumerate((ang_k, ang)):
                turn = 0.25 * k
                tmp = rstd[rows, 0:T]
                chain(v.tensor_scalar(tmp, angp, 1 / two_pi, turn, ALU.mult, ALU.add))
                chain(v.tensor_scalar(tmp, tmp, magic, None, ALU.add))
                chain(v.tensor_scalar(tmp, tmp, -magic, None, ALU.add))
                chain(v.scalar_tensor_tensor(out=dst[rows, :], in0=tmp, scalar=-p1, in1=angp, op0=ALU.mult, op1=ALU.add))
                for part in (p2, p3):
                    chain(v.scalar_tensor_tensor(out=dst[rows, :], in0=tmp, scalar=-part, in1=dst[rows, :],
                                                 op0=ALU.mult, op1=ALU.add))
                chain(v.tensor_scalar(dst[rows, :], dst[rows, :], turn * two_pi, lim, ALU.add, ALU.min))
                v.tensor_scalar(dst[rows, :], dst[rows, :], -lim, None, ALU.max).then_inc(ev("angle_reduced"), 1)
            for k in range(4):
                low1(k + 3)
            for k in range(4):
                low1(k + 7)
            root("ckv", T)
            split("ckv", scaled([ckv], [g1("kv_norm")], T), [KL[:, 0:T]], T, [KH[:, 0:T]])
            root("cq", S)
            split("cq", scaled([cq[:, c, META:T] for c in range(2)], [g1("q_norm", c) for c in range(2)], S),
                  ch(HL, 0, 2), S, ch(HH, 0, 2))
            for k in range(8):
                low1(k + 11)
                un = FIRST1["xin0"] + k
                dve.wait_ge(ev("unit_used"), un + 1)
                if k < 4:
                    dve.wait_ge(ev("unit_taken_by_scalar"), taken1(FIRST1["gc0"] + k)[1])
                    v.tensor_tensor(u[:, k, :], ps[:, un % 4, 0:T], u[:, k, :], ALU.mult)\
                        .then_inc(ev("unit_taken_by_vector"), 1)
                    dve.wait_ge(ev("unit_taken_by_vector"), k + 1)
                    w = lambda tap: g1("conv_w", 4 * tap + k)
                    chain(v.tensor_scalar(yc[:, k, :], u[:, k, META:T], w(2), None, ALU.mult))
                    for back in (1, 2):
                        chain(v.scalar_tensor_tensor(out=yc[:, k, :], in0=u[:, k, META - back:T - back],
                                                     scalar=w(2 - back), in1=yc[:, k, :], op0=ALU.mult, op1=ALU.add))
                else:
                    v.tensor_tensor(yc[:, k - 4, :], ps[:, un % 4, META:T], yc[:, k - 4, :], ALU.mult)\
                        .then_inc(ev("unit_taken_by_vector"), 1)
            dve.wait_ge(ev("kpe_swapped"), 1)
            dve.wait_ge(ev("rope_table"), 2)
            chain(v.tensor_tensor(rope_a[rows, 0:T], ps[rows, 5, 0:T], sin_t[rows, :], ALU.mult))
            chain(v.tensor_tensor(kpe[rows, :], kpe[rows, :], cos_t[rows, :], ALU.mult))
            v.tensor_tensor(kcat[rows, :, :], kpe[rows, :].unsqueeze(1).to_broadcast([ROPE, HEADS, T]),
                            rope_a[rows, 0:T].unsqueeze(1).to_broadcast([ROPE, HEADS, T]), ALU.add)\
                .then_inc(ev("rope_keys"), 1)
            u0 = FIRST1["uq"]
            low1(u0 + 3)
            root("conv", S)
            split("conv", scaled(ch(yc, 0, 4), [g1("conv_out_norm", c) for c in range(4)], S), ch(xl2, 4, 8), S,
                  ch(xh2, 4, 8))
            for k in range(1, HEADS):
                low1(u0 + 3 + k)
            dve.wait_ge(ev("rope_keys"), 1)
            for j in range(HEADS // 2):
                if j:
                    dve.wait_ge(ev("q_roped"), j)
                dve.wait_ge(ev("q_swapped"), j + 1)
                qq = qcat[rows, 2 * j:2 * j + 2, :]
                both = lambda t: t[rows, META:T].unsqueeze(1).to_broadcast([ROPE, 2, S])
                tmp = rope_a[rows, :].rearrange("p (h t) -> p h t", h=2)
                sw = ps[rows, 4 + j % 2, :].rearrange("p (h t) -> p h t", h=2)
                chain(v.tensor_tensor(tmp, sw, both(sin_t), ALU.mult))
                chain(v.tensor_tensor(qq, qq, both(cos_t), ALU.mult))
                v.tensor_tensor(qq, qq, tmp, ALU.add).then_inc(ev("q_roped"), 1)
            dve.wait_ge(ev("q_roped"), 4)
            for k in range(3):
                dve.wait_ge(*((ev("values"), k + 1) if k < 2 else (ev("unit_used"), FIRST1["ukv"] + 1)))
                v.tensor_copy(vtok[:, k, :], ps[:, 4 + k, :]).then_inc(ev("values_ready"), 1)
            low1(u0 + 8 + 3)
            for n in range(HEADS * TT):
                h, qt = divmod(n, TT)
                keys = META + (qt + 1) * P
                b = n % 2
                sc = ps[:, 4 + b, 0:keys]
                dia = ps[:, 4 + b, keys - P:keys]
                dve.wait_ge(ev("scores"), n + 1)
                if n == 0:
                    dve.wait_ge(ev("masks_ready"), 2)
                if n >= 2:
                    dve.wait_ge(ev("exp_done"), n - 1)
                chain(v.tensor_tensor(dia, dia, causal[:], ALU.add))
                chain(v.tensor_reduce(small[:, 4 + b:5 + b], sc, AX.X, ALU.max))
                v.tensor_scalar(small[:, 6 + b:7 + b], small[:, 4 + b:5 + b], -SCALE1, None, ALU.mult)\
                    .then_inc(ev("neg_max"), 1)
                dve.wait_ge(ev("exp_done"), n + 1)
                chain(v.reciprocal(small[:, 10 + b:11 + b], small[:, 8 + b:9 + b]))
                v.tensor_scalar(prob[:, b, 0:keys], prob[:, b, 0:keys], small[:, 10 + b:11 + b], None, ALU.mult)\
                    .then_inc(ev("prob_ready"), 1)
            root("attn", S)
            split("attn", scaled(ch(aT, 0, 4), [g1("attn_out_norm", c) for c in range(4)], S), ch(xl2, 0, 4), S,
                  ch(xh2, 0, 4))
            for k in range(8):
                low1(FIRST1["out0"] + k + 3)
            root("post_mix", S)
            for c in range(DC):
                chain(v.scalar_tensor_tensor(out=mixT[:, c, :], in0=mixT[:, c, :], scalar=g1("post_mix_norm", c),
                                             in1=rstd[:, 0:S], op0=ALU.mult, op1=ALU.mult))
                v.tensor_tensor(hx[:, c, :], hx[:, c, :], mixT[:, c, :], ALU.add).then_inc(ev("h_mixed"), 1)
            root("pre_ffn", S)
            k0 = SP_AT["ffn"]

            def make_t(c, dst):
                chain(v.scalar_tensor_tensor(out=tT[:, c, :], in0=hx[:, c, :], scalar=g1("pre_ffn_norm", c),
                                             in1=rstd[:, 0:S], op0=ALU.mult, op1=ALU.mult))
                return v.tensor_copy(dst, tT[:, c, :])

            split("ffn", make_t, ch(xl2), S, ch(xh2))
            u0 = FIRST1["shg"]
            low1(u0 + 3)

            def make_hidden(c, dst):
                dve.wait_ge(*taken1(u0 + c))
                dve.wait_ge(ev("unit_used"), u0 + 2 + c + 1)
                return v.tensor_tensor(dst, ps[:, (u0 + 2 + c) % 4, 0:S], sact[:, c, :], ALU.mult)

            dve.wait_ge(ev("logits"), 1)
            dve.wait_ge(ev("routing_consts"), 4)
            chain(v.tensor_copy(logit, ps[:, 6, 0:2 * 36].rearrange("p (t n) -> p t n", t=TT)))
            bc = lambda x, n: x.unsqueeze(2).to_broadcast([P, TT, n])
            io = lambda n: iota_e[:, 0:n].unsqueeze(1).to_broadcast([P, TT, n])

            def first_max(x, n, m, key, onehot, lowest):
                chain(v.tensor_reduce(m, x, AX.X, ALU.max))
                chain(v.tensor_tensor(key, x, bc(m, n), ALU.is_equal))
                chain(v.scalar_tensor_tensor(out=key, in0=key, scalar=-1000.0, in1=io(n), op0=ALU.mult, op1=ALU.add))
                chain(v.tensor_reduce(lowest, key, AX.X, ALU.min))
                chain(v.tensor_tensor(onehot, key, bc(lowest, n), ALU.is_equal))

            first_max(glog, GROUPS, r_s(0), r_g4k, r_ohg, r_s(1))
            v.tensor_tensor(r_g4, glog, bc(r_s(0), GROUPS), ALU.subtract).then_inc(ev("group_centred"), 1)
            by_group = lambda x: x.rearrange("p t (g e) -> p t g e", g=GROUPS)
            gb = lambda x: x.unsqueeze(3).to_broadcast([P, TT, GROUPS, EPG])
            for t in range(TT):
                chain(v.tensor_tensor(by_group(r_em)[:, t], by_group(elog)[:, t], gb(r_ohg)[:, t], ALU.mult))
            chain(v.tensor_scalar(r_g4k, r_ohg, 1e30, -1e30, ALU.mult, ALU.add))
            for t in range(TT):
                chain(v.tensor_tensor(by_group(r_em)[:, t], by_group(r_em)[:, t], gb(r_g4k)[:, t], ALU.add))
            first_max(r_em, EXPERTS, r_s(2), r_key, r_oh1, r_s(1))
            chain(v.scalar_tensor_tensor(out=r_em, in0=r_oh1, scalar=-3e30, in1=r_em, op0=ALU.mult, op1=ALU.add))
            first_max(r_em, EXPERTS, r_s(3), r_key, r_oh2, r_s(1))
            v.tensor_tensor(r_s(4), r_s(3), r_s(2), ALU.subtract).then_inc(ev("pair_diff"), 1)
            v.tensor_tensor(r_m, r_oh1, r_oh2, ALU.add).then_inc(ev("chosen_ready"), 1)
            low1(u0 + 4)
            low1(u0 + 5)
            split("shared", make_hidden, ch(HL, 0, 2), S, ch(HH, 0, 2))
            dve.wait_ge(ev("group_exp"), 1)
            chain(v.tensor_reduce(r_s(6), r_ge, AX.X, ALU.add))
            dve.wait_ge(ev("pair_exp"), 1)
            chain(v.scalar_tensor_tensor(out=r_s(6), in0=r_s(5), scalar=1.0, in1=r_s(6), op0=ALU.add, op1=ALU.mult))
            chain(v.reciprocal(w_k(0), r_s(6)))
            chain(v.tensor_tensor(w_k(1), w_k(0), r_s(5), ALU.mult))
            dve.wait_ge(ev("ranks"), 1)
            rk = ps[:, 6, P:P + 2 * EXPERTS].rearrange("p (t n) -> p t n", t=TT)
            chain(v.scalar_tensor_tensor(out=rank_or[:, :, 0:EXPERTS], in0=rk, scalar=1.0, in1=r_m,
                                         op0=ALU.add, op1=ALU.mult))
            chain(v.tensor_scalar(rank_or[:, :, 0:EXPERTS], rank_or[:, :, 0:EXPERTS], -1.0, None, ALU.add))

            def select(b, first, width, done):
                for t in range(TT):
                    r = rank_or[:, t, bass.ds(first, width)].unsqueeze(2).to_broadcast([P, width, CAP])
                    i_ = iota_slot[:].unsqueeze(1).to_broadcast([P, width, CAP])
                    ins = v.tensor_tensor(sel[:, b, t, 0:width * CAP].rearrange("p (e s) -> p e s", e=width),
                                          r, i_, ALU.is_equal)
                ins.then_inc(done, 1)

            select(0, 0, 2, ev("sel_ready"))
            for k in range(TT):
                dve.wait_ge(ev("th_ready"), k + 1)
                v.tensor_tensor(tl[:, k, :].rearrange("p (b n) -> p b n", b=2), ps[:, 4:6, :],
                                th[:, k, :].rearrange("p (b n) -> p b n", b=2).bitcast(F32), ALU.subtract)\
                    .then_inc(ev("t_ready"), 1)
            for k, oh in enumerate((r_oh1, r_oh2)):
                chain(v.tensor_tensor(r_key, oh, rk, ALU.mult))
                chain(v.tensor_reduce(r_s(6), r_key, AX.X, ALU.add))
                chain(v.tensor_tensor(r_key, oh, io(EXPERTS), ALU.mult))
                chain(v.tensor_reduce(r_s(7), r_key, AX.X, ALU.add))
                chain(v.tensor_scalar(behind(k), r_s(6), CAP - 0.5, None, ALU.is_gt))
                chain(v.tensor_scalar(before_cap(k), behind(k), -1.0, 1.0, ALU.mult, ALU.add))
                chain(v.tensor_scalar(r_s(8), r_s(6), CAP - 1.0, None, ALU.min))
                chain(v.scalar_tensor_tensor(out=r_s(8), in0=r_s(7), scalar=float(CAP), in1=r_s(8),
                                             op0=ALU.mult, op1=ALU.add))
                chain(v.tensor_copy(slot_i[:, 2 * k:2 * k + 2], r_s(8)))
                chain(v.tensor_scalar(r_s(8), r_s(6), -float(CAP), 0.0, ALU.add, ALU.max))
                chain(v.scalar_tensor_tensor(out=r_s(8), in0=r_s(7), scalar=float(RANKS - CAP), in1=r_s(8),
                                             op0=ALU.mult, op1=ALU.add))
                chain(v.tensor_copy(slot_i[:, 2 * TT + 2 * k:2 * TT + 2 * k + 2], r_s(8)))
            chain(v.tensor_reduce(r_s(8)[0:1, 0:1], ps[0:1, 6, P + 2 * EXPERTS:P + 3 * EXPERTS], AX.X, ALU.max))
            chain(v.tensor_scalar(r_s(8)[0:1, 0:1], r_s(8)[0:1, 0:1], CAP + 0.5, None, ALU.is_gt))
            v.tensor_copy(overflow[:], r_s(8)[0:1, 0:1]).then_inc(ev("overflow_known"), 1)

            def gathered(b, done):
                v.tensor_copy(xg[:, b, 4:8, :], ps[:, 1, :].rearrange("p (c s) -> p c s", c=4)).then_inc(done, 1)

            dve.wait_ge(ev("second_half_gathered"), 1)
            gathered(0, ev("xg_by_vector"))
            with dve.Fori(0, TURNS) as i:
                for h in range(2):
                    select((h + 1) % 2, i * GROUP + 2 * (h + 1), 2, ev("sel_ready"))
                    dve.wait_ge(ev("expert_slab_used"), i * RING + (6 * h + 4))
                    dve.wait_ge(ev("silu_done"), i * 2 + (h + 1))
                    v.tensor_tensor(hid, gact, ps[:, 3, 0:FF], ALU.mult).then_inc(ev("hidden_ready"), 1)
                    dve.wait_ge(ev("hidden_turned"), i * 2 + (h + 1))
                    v.tensor_copy(hidT, ps[:, 2, FF:2 * FF].rearrange("p (f s) -> p f s", f=2))\
                        .then_inc(ev("hidT_ready"), 1)
                    dve.wait_ge(ev("second_half_gathered"), i * 2 + (h + 2))
                    gathered((h + 1) % 2, ev("xg_by_vector"))
                    dve.wait_ge(ev("expert_slab_used"), i * RING + (6 * h + 6))
                    dve.wait_ge(ev("row_buffer_free"), i * 2 + (h + 1))
                    v.tensor_copy(yrow[:, h, 512:D], ps[:, 5 + 2 * h, :]).then_inc(ev("rows_by_vector"), 1)

            dve.wait_ge(ev("overflow_known"), 1)
            more = dve.value_load(overflow[0:1, 0:1], min_val=0, max_val=1)
            with dve.If(more > 0):
                with dve.Fori(0, RANKS // CAP - 1) as r:
                    for t in range(TT):
                        v.tensor_scalar(rank_or[:, t, :], rank_or[:, t, :], -float(CAP), None, ALU.add)\
                            .then_inc(ev("o_ranks"), 1)
                    with dve.Fori(0, EXPERTS) as e:
                        b = r * EXPERTS + e
                        dve.wait_ge(ev("o_ranks"), r * TT + TT)
                        select(0, e, 1, ev("o_sel"))
                        dve.wait_ge(ev("o_gathered"), b + 1)
                        v.tensor_copy(xg[:, 0, :, 0:CAP], ps[:, 0, :].rearrange("p (c s) -> p c s", c=DC))\
                            .then_inc(ev("o_xg"), 1)
                        dve.wait_ge(ev("o_silu"), b + 1)
                        v.tensor_tensor(hid[0:CAP, :], gact[0:CAP, :], ps[0:CAP, 3, 0:FF], ALU.mult)\
                            .then_inc(ev("o_hidden"), 1)
                        dve.wait_ge(ev("o_turned"), b + 1)
                        v.tensor_copy(hidT, ps[:, 2, FF:2 * FF].rearrange("p (f s) -> p f s", f=2))\
                            .then_inc(ev("o_hidT"), 1)
                        dve.wait_ge(ev("o_down"), b + 1)
                        v.tensor_copy(yrow[0:CAP, 0, 512:D], ps[0:CAP, 5, :]).then_inc(ev("o_rows"), 1)

            for k in range(NB - 1):
                low2(k)
            lam = vec2[:, V2["lru_lambda_2"]:V2["lru_lambda_2"] + DC]
            sc = lambda k: small_lru[:, k * DC:(k + 1) * DC]
            chain(v.tensor_scalar(sc(0), lam, -1.0, None, ALU.mult))
            v.tensor_tensor(sc(1), lam, sc(0), ALU.min).then_inc(ev("lambda_abs"), 1)
            dve.wait_ge(ev("lambda_exp"), 1)
            chain(v.tensor_scalar(sc(3), sc(2), 2.0, None, ALU.add))
            chain(v.reciprocal(sc(3), sc(3)))
            chain(v.tensor_tensor(sc(2), sc(2), sc(3), ALU.mult))
            chain(v.tensor_tensor(sc(3), sc(2), sc(2), ALU.mult))
            terms = 9
            chain(v.tensor_scalar(sc(4), sc(3), 0.0, 1.0 / (2 * terms + 1), ALU.mult, ALU.add))
            for k in range(terms - 1, -1, -1):
                chain(v.tensor_tensor(sc(4), sc(4), sc(3), ALU.mult))
                chain(v.tensor_scalar(sc(4), sc(4), 1.0 / (2 * k + 1), None, ALU.add))
            chain(v.scalar_tensor_tensor(out=sc(4), in0=sc(4), scalar=2.0, in1=sc(2), op0=ALU.mult, op1=ALU.mult))
            chain(v.scalar_tensor_tensor(out=sc(4), in0=sc(0), scalar=0.0, in1=sc(4), op0=ALU.max, op1=ALU.add))
            chain(v.tensor_scalar(sc(4), sc(4), -LRU_C, None, ALU.mult))
            dve.wait_ge(ev("rows_gathered"), 16 * 2 * TT)
            with dve.If(more > 0):
                dve.wait_ge(ev("o_rows_gathered"), 16 * 2 * TT)
                for k in range(2 * TT):
                    v.tensor_scalar(gath[:, k, :], gath[:, k, :], small[:, 8 + k:9 + k], None, ALU.mult)\
                        .then_inc(ev("o_masked"), 1)
                    dve.wait_ge(ev("o_masked"), k + 1)
                    v.scalar_tensor_tensor(out=gath[:, k, :], in0=gath_more[:, k, :], scalar=small[:, 4 + k:5 + k],
                                           in1=gath[:, k, :], op0=ALU.mult, op1=ALU.add).then_inc(ev("o_replaced"), 1)
                dve.wait_ge(ev("o_replaced"), 2 * TT)
            for t in range(TT):
                chain(v.tensor_scalar(gath[:, t, :], gath[:, t, :], small[:, t:t + 1], None, ALU.mult))
                v.scalar_tensor_tensor(out=gath[:, t, :], in0=gath[:, TT + t, :], scalar=small[:, 2 + t:3 + t],
                                       in1=gath[:, t, :], op0=ALU.mult, op1=ALU.add).then_inc(ev("routed_ready"), 1)
            dve.wait_ge(ev("shT_ready"), 2)
            for c in range(DC):
                dve.wait_ge(ev("routed_turned"), c + 1)
                v.tensor_tensor(shT[:, c, :], shT[:, c, :], ps[:, 4 + c % 2, 0:S], ALU.add)\
                    .then_inc(ev("ffn_ready"), 1)
            root("post_ffn", S)
            for c in range(DC):
                chain(v.scalar_tensor_tensor(out=shT[:, c, :], in0=shT[:, c, :], scalar=g1("post_ffn_norm", c),
                                             in1=rstd[:, 0:S], op0=ALU.mult, op1=ALU.mult))
                v.tensor_tensor(hx[:, c, :], hx[:, c, :], shT[:, c, :], ALU.add).then_inc(ev("h_ffn"), 1)
            dve.wait_ge(ev("h_ffn"), DC)
            root("mix2", S)
            split("mix2", scaled(ch(hx), [g2("norm_mix_g_2", c) for c in range(DC)], S), ch(xl2), S, ch(xh2))
            two = lambda t, q: t[:, 2 * q:2 * q + 2, :]

            def gated_output(q):
                dve.wait_ge(ev("scanned"), 2 * q + 2)
                dve.wait_ge(ev("gelu_done"), 1 + q // 2)
                v.tensor_tensor(two(zg, q), two(zg, q), two(zc, q), ALU.mult).then_inc(ev("lru_done"), 1)

            for k in range(48):
                low2(k + 3)
                if 8 <= k < 16:
                    c = k - 8
                    dve.wait_ge(ev("unit_taken_by_scalar"), TAKEN_S1 + c + 1)
                    w = lambda tap: g2("conv_w_2", 8 * tap + c)
                    chain(v.tensor_scalar(zc[:, c, :], zx[:, c, :], w(3), g2("conv_b_2", c), ALU.mult, ALU.add))
                    for back in (1, 2, 3):
                        ins = v.scalar_tensor_tensor(out=zc[:, c, back:], in0=zx[:, c, 0:S - back],
                                                     scalar=w(3 - back), in1=zc[:, c, back:], op0=ALU.mult,
                                                     op1=ALU.add)
                        if back < 3:
                            chain(ins)
                    ins.then_inc(ev("conv_ready"), 1)
                if 22 <= k < 26:
                    q = k - 22
                    dve.wait_ge(ev("gate_act"), 2 * q + 2)
                    dve.wait_ge(ev("conv_ready"), DC)
                    v.tensor_tensor(two(zx, q), two(zx, q),
                                    sc(4)[:, 2 * q:2 * q + 2].unsqueeze(2).to_broadcast([P, 2, S]), ALU.mult)\
                        .then_inc(ev("log_a"), 1)
                    v.tensor_tensor(two(zi, q), two(zi, q), two(zc, q), ALU.mult).then_inc(ev("gated_input"), 1)
                if 29 <= k < 37:
                    c = k - 29
                    dve.wait_ge(ev("tanh_done"), 1 + c // 4)
                    th_, xt = zc[:, c, :], XT[:, 0, 0:S]
                    chain(v.tensor_scalar(xt, th_, -1.0, 1.0, ALU.mult, ALU.add))
                    chain(v.reciprocal(xt, xt))
                    v.scalar_tensor_tensor(out=th_, in0=th_, scalar=-2.0, in1=xt, op0=ALU.mult, op1=ALU.mult)\
                        .then_inc(ev("one_minus_a2"), 1)
                    dve.wait_ge(ev("one_minus_a2"), c + 1)
                if 40 <= k < 44:
                    q = k - 40
                    dve.wait_ge(ev("mult_ready"), 1 + q // 2)
                    dve.wait_ge(ev("gated_input"), 4)
                    v.tensor_tensor(two(zi, q), two(zi, q), two(zc, q), ALU.mult).then_inc(ev("lru_input"), 1)
                if 44 <= k < 48:
                    if k == 44:
                        dve.wait_ge(ev("lru_input"), 4)
                        dve.wait_ge(ev("a_ready"), 2)
                    for c in (2 * (k - 44), 2 * (k - 44) + 1):
                        v.tensor_tensor_scan(out=zc[:, c, :], data0=zx[:, c, :], data1=zi[:, c, :], initial=0.0,
                                             op0=ALU.mult, op1=ALU.add).then_inc(ev("scanned"), 1)
                    if k > 44:
                        gated_output(k - 45)
            gated_output(3)
            dve.wait_ge(ev("lru_done"), 4)
            dve.wait_ge(ev("v_ready"), TT)
            for b in range(2):
                chain(v.memset(cum(b)[:, :, S:S + 1], 1.0))
            for n in range(HEADS2):
                j, qt = divmod(n, TT)
                keys = (qt + 1) * P
                b = n % 2
                dve.wait_ge(ev("z_scores"), n + 1)
                zd = ps[:, 2 * b:2 * b + 2, keys - P:keys]
                v.tensor_tensor(zd, zd, strict[:].unsqueeze(1).to_broadcast([P, 2, P]), ALU.add)\
                    .then_inc(ev("z_masked"), 1)
                beta = att_buf(b).rearrange("p (h k) -> p h k", h=2)[:, :, 0:keys]
                omb = att_buf(2 + b).rearrange("p (h k) -> p h k", h=2)[:, :, 0:keys]
                dve.wait_ge(ev("sigm_done"), 2 * n + 1)
                for h in range(2):
                    ins = v.tensor_tensor_scan(out=cum(b)[:, h, S - keys:S][:, ::-1], data0=omb[:, h, ::-1],
                                               data1=ones[:, 0:1].to_broadcast([P, keys]), initial=1.0,
                                               op0=ALU.mult, op1=ALU.mult)
                    chain(ins)
                dve.wait_ge(ev("sigm_done"), 2 * n + 2)
                if n >= 2:
                    dve.wait_ge(ev("att_turned"), n - 1)
                v.tensor_tensor(att(b)[:, :, 0:keys], beta, cum(b)[:, :, S - keys + 1:S + 1], ALU.mult)\
                    .then_inc(ev("att_ready"), 1)
                if qt == TT - 1 and j:
                    dve.wait_ge(ev("y_att"), 2 * j)
                    v.tensor_copy(zk[:, j - 1, :], ps[:, 5 + (j - 1) % 2, 0:S]).then_inc(ev("y_att_taken"), 1)
            dve.wait_ge(ev("y_att"), HEADS2)
            v.tensor_copy(zk[:, DC - 1, :], ps[:, 5 + (DC - 1) % 2, 0:S]).then_inc(ev("y_att_taken"), 1)
            dve.wait_ge(ev("y_att_taken"), DC)
            for k in range(8):
                low2(U_GATT + 3 + k)
            split("y_lru", lambda c, dst: v.tensor_copy(dst, zg[:, c, :]), ch(xl2), S, ch(xh2))
            dve.wait_ge(ev("g_lru_ready"), 1)
            for k in range(8):
                low2(U_BRL + 3 + k)
                dve.wait_ge(ev("unit_used"), U1 + U_BRL + k + 1)
                v.tensor_tensor(zl[:, k, :], ps[:, (U_BRL + k) % 4, 0:S], zl[:, k, :], ALU.mult)\
                    .then_inc(ev("unit_taken_by_vector"), 1)
            split("y_att", lambda c, dst: v.tensor_copy(dst, zk[:, c, :]), ch(xl2), S, ch(xh2))
            dve.wait_ge(ev("unit_taken_by_scalar"), TAKEN_S1 + 56)
            for k in range(8):
                low2(U_BRA + 3 + k)
                dve.wait_ge(ev("unit_used"), U1 + U_BRA + k + 1)
                v.tensor_tensor(zq[:, k, :], ps[:, (U_BRA + k) % 4, 0:S], zq[:, k, :], ALU.mult)\
                    .then_inc(ev("unit_taken_by_vector"), 1)
            dve.wait_ge(ev("unit_taken_by_vector"), TAKEN_V1 + 16)
            split("merged2", lambda c, dst: v.tensor_tensor(dst, zl[:, c, :], zq[:, c, :], ALU.add), ch(xl2), S,
                  ch(xh2))
            for k in range(8):
                low2(U_OUT + 3 + k)
                dve.wait_ge(ev("unit_used"), U1 + U_OUT + k + 1)
                v.tensor_tensor(hx[:, k, :], hx[:, k, :], ps[:, (U_OUT + k) % 4, 0:S], ALU.add)\
                    .then_inc(ev("h_mixed2"), 1)
            dve.wait_ge(ev("h_mixed2"), DC)
            root("mlp2", S)
            split("mlp2", scaled(ch(hx), [g2("norm_mlp_g_2", c) for c in range(DC)], S), ch(xl2), S, ch(xh2))
            with dve.Fori(0, 4) as i:
                for k in range(16):
                    low2(U_MLP + k + 3, i)
                    if k % 4 < 2:
                        f = (k // 4) * 2 + k % 4
                        dve.wait_ge(ev("unit_used"), i * 16 + (U1 + U_MLP + k + 1))
                        x_ = ps[:, k % 4, 0:S]
                        v.tensor_scalar(zx[:, 2 + f % 2, :], x_, 0.0, None, ALU.max).then_inc(ev("relu"), 1)
                        dve.wait_ge(ev("relu"), i * 8 + (f + 1))
                        v.tensor_tensor(zx[:, f % 2, :], zx[:, 2 + f % 2, :], zx[:, 2 + f % 2, :], ALU.mult)\
                            .then_inc(ev("relu_done"), 1)
                        dve.wait_ge(ev("relu_high"), i * 8 + (f + 1))
                        v.tensor_tensor(HL[:, f % 2, :], zx[:, f % 2, :], HH[:, f % 2, :].bitcast(F32), ALU.subtract)\
                            .then_inc(ev("relu_low"), 1)
            dve.wait_ge(ev("p_turned"), 2)
            split("p2", lambda c, dst: v.tensor_copy(dst, ps[:, 2 + c, 0:S]), ch(HL, 0, 2), S, ch(HH, 0, 2))
            dve.wait_ge(ev("unit_used"), U1 + U_PLE)
            acc = ps[:, 4:8, :].rearrange("p b (c t) -> p (b c) t", c=2)
            for c in range(DC):
                v.tensor_tensor(hx[:, c, :], hx[:, c, :], acc[:, c, :], ALU.add).then_inc(ev("h_mlp"), 1)
            dve.wait_ge(ev("h_mlp"), DC)
            root("ple2", S)
            split("ple2", scaled(ch(hx), [g2("norm_ple_g_2", c) for c in range(DC)], S), ch(xl2), S, ch(xh2))
            for k in range(10):
                low2(U_PLE + 3 + k)
            for k in range(DC):
                dve.wait_ge(ev("unit_taken_by_scalar"), TAKEN_S1 + 57 + k)
                if k == 0:
                    dve.wait_ge(ev("unit_used"), U1 + U_PLE + 4)
                chain(v.tensor_tensor(zq[:, k, :], zq[:, k, :], acc[:, k, :], ALU.mult))
                v.tensor_tensor(hx[:, k, :], hx[:, k, :], zq[:, k, :], ALU.add).then_inc(ev("h_ple"), 1)
            dve.wait_ge(ev("h_ple"), DC)
            root("final2", S)
            for c in range(DC):
                v.scalar_tensor_tensor(out=zg[:, c, :], in0=hx[:, c, :], scalar=g2("norm_final_g_2", c),
                                       in1=rstd[:, 0:S], op0=ALU.mult, op1=ALU.mult).then_inc(ev("result"), 1)
            for k in range(TT):
                dve.wait_ge(ev("result_turned"), k + 1)
                v.tensor_copy(out_tok(k)[:, 512:D], ps[:, 4 * k + 1, :]).then_inc(ev("out_tokens_by_vector"), 1)

        @block.tensor
        def _(pe):
            mm = nc.tensor.matmul

            def triple(o, h, l, rh, rl, first, last, skip=False):
                mm(o, h, rh, start=first, stop=False, skip_group_check=skip)
                mm(o, h, rl, start=False, stop=False, skip_group_check=skip)
                return mm(o, l, rh, start=False, stop=last, skip_group_check=skip)

            def columns(b, bank, hi, lo, n, step=P, chunks=DC, arrived=None):
                for c in range(chunks):
                    if arrived is not None:
                        pe.wait_ge(ev("split_low"), arrived + c + 1)
                    w = slice(c * step, c * step + P)
                    last = triple(ps[:, bank, 0:n], WH[:, b, w], WL[:, b, w], hi[:, c, :], lo[:, c, :], c == 0,
                                  c == chunks - 1)
                return last

            def rows(b, banks, hi, lo, first):
                for n in range(DC):
                    w = slice(n * P, (n + 1) * P)
                    o = ps[:, banks + n // 2, (n % 2) * S:(n % 2 + 1) * S]
                    last = triple(o, WH[:, b, w], WL[:, b, w], hi, lo, first and n % 2 == 0, False, skip=True)
                return last

            def unit1(u_no, hi, lo, n, arrived=None, **k):
                pe.wait_ge(ev("unit_split"), u_no + 1)
                if u_no >= 4 and UNITS1[u_no - 4][1] not in UNCOUNTED:
                    pe.wait_ge(*taken1(u_no - 4))
                columns(u_no % NB, u_no % 4, hi, lo, n, arrived=arrived, **k).then_inc(ev("unit_used"), 1)

            def norm(name, n):
                k0, no = SQ_AT[name], NORM_NO[name]
                if no:
                    pe.wait_ge(ev("std_ready"), no)
                for c in range(NCH[name]):
                    pe.wait_ge(ev("square_ready"), k0 + c + 1)
                    mm(ps[:, 7, 0:n], ones[:], XT[:, (k0 + c) % 2, 0:n], start=c == 0, stop=c == NCH[name] - 1)\
                        .then_inc(ev("squares_summed"), 1)

            tr = nc.tensor.transpose
            pe.wait_ge(ev("ident_ready"), 1)
            pe.wait_ge(ev("vec1_loaded"), 16 * len(VEC1))
            tr(ps[:, 6, 0:NV1], vrow1[0:NV1, :], ident[0:NV1, 0:NV1]).then_inc(ev("vrows_turned"), 1)
            pe.wait_ge(ev("vec2_loaded"), 16 * len(VEC2))
            tr(ps[:, 6, P:P + NV2], vrow2[0:NV2, :], ident[0:NV2, 0:NV2]).then_inc(ev("vrows_turned"), 1)
            pe.wait_ge(ev("x_loaded"), 48)
            for c in range(DC):
                if c >= 4:
                    pe.wait_ge(ev("hT_by_vector" if c % 2 else "hT_by_scalar"), (c - 4) // 2 + 1)
                tr(ps[:, c % 4, 0:META], x_tok[0:META, 2, c * P:(c + 1) * P], ident[0:META, 0:META])
                for k in range(TT):
                    last = tr(ps[:, c % 4, META + k * P:META + (k + 1) * P], x_tok[:, k, c * P:(c + 1) * P], ident[:])
                last.then_inc(ev("x_turned"), 1)
            pe.wait_ge(ev("inv_ready"), ROPE // 2)
            pe.wait_ge(ev("meta_pos"), 1)
            pe.wait_ge(ev("pos_ready"), 1)
            mm(ps[0:QD, 5, 0:T], inv_row[0:1, 0:QD], pos_row[0:1, :], start=True, stop=True).then_inc(ev("angles"), 1)
            pe.wait_ge(ev("ones_ready"), 1)
            norm("pre_mix", T)
            for c in (DC - 2, DC - 1):
                pe.wait_ge(ev("hT_by_vector" if c % 2 else "hT_by_scalar"), c // 2 + 1)
            for k in range(4):
                unit1(k, xh1, xl1, T, arrived=0)
            norm("ckv", T)
            for k in range(4, 8):
                unit1(k, xh1, xl1, T)
                if k == 7:
                    norm("cq", S)
            for k in range(8, 16):
                unit1(k, xh1, xl1, T)
            pe.wait_ge(ev("swap_ready"), 2)
            pe.wait_ge(ev("unit_taken_by_scalar"), 4)
            pe.wait_ge(ev("angle_reduced"), 2)
            mm(ps[0:QD, 5, 0:T], swap[:], kpe[0:QD, :], start=True, stop=True).then_inc(ev("kpe_swapped"), 1)
            norm("conv", S)
            u0 = FIRST1["uq"]
            for k in range(HEADS):
                unit1(u0 + k, HH, HL, S, arrived=SP_AT["cq"] if k == 0 else None, chunks=2, step=QD)
            for j in range(HEADS // 2):
                pe.wait_ge(*taken1(u0 + 2 * j + 1))
                if j == 0:
                    pe.wait_ge(ev("rope_keys"), 1)
                if j >= 2:
                    pe.wait_ge(ev("q_roped"), j - 1)
                mm(ps[0:QD, 4 + j % 2, :], swap[:], qcat[0:QD, 2 * j:2 * j + 2, :].rearrange("p h t -> p (h t)"),
                   start=True, stop=True).then_inc(ev("q_swapped"), 1)
            uk = FIRST1["ukv"]
            pe.wait_ge(ev("unit_split"), uk + 1)
            pe.wait_ge(ev("split_low"), SP_AT["ckv"] + 1)
            pe.wait_ge(ev("k_padded"), 2)
            b = uk % NB
            for h in range(HEADS):
                if h >= 4:
                    pe.wait_ge(ev("nope_keys_taken"), h - 3)
                w = slice(h * NOPE, h * NOPE + P)
                triple(ps[:, h % 4, 0:T], WH[:, b, w], WL[:, b, w], KH[:, 0:T], KL[:, 0:T], True, True)\
                    .then_inc(ev("nope_keys"), 1)
            pe.wait_ge(ev("q_roped"), 4)
            for k in range(3):
                w = slice(HEADS * NOPE, UNIT)
                tk = slice(k * P, (k + 1) * P)
                mm(ps[:, 4 + k, :], KH[:, tk], WH[:, b, w], start=True, stop=False)
                mm(ps[:, 4 + k, :], KH[:, tk], WL[:, b, w], start=False, stop=False)
                mm(ps[:, 4 + k, :], KL[:, tk], WH[:, b, w], start=False, stop=True)\
                    .then_inc(ev("values" if k < 2 else "unit_used"), 1)
            pe.wait_ge(ev("values_ready"), 3)
            pe.wait_ge(ev("nope_keys_taken"), HEADS)

            def scores(n):
                h, qt = divmod(n, TT)
                keys = META + (qt + 1) * P
                if n >= 2:
                    pe.wait_ge(ev("exp_done"), n - 1)
                mm(ps[:, 4 + n % 2, 0:keys], qcat[0:QD, h, qt * P:(qt + 1) * P], kcat[0:QD, h, 0:keys],
                   start=True, stop=True).then_inc(ev("scores"), 1)

            scores(0)
            for n in range(HEADS * TT):
                h, qt = divmod(n, TT)
                if n + 1 < HEADS * TT:
                    scores(n + 1)
                pe.wait_ge(ev("prob_ready"), n + 1)
                if n:
                    pe.wait_ge(ev("probT_ready"), n)
                for k in range(qt + 1):
                    tr(ps[:, 6, k * P:(k + 1) * P], prob[:, n % 2, k * P:(k + 1) * P], ident[:])
                tr(ps[0:META, 6, 3 * P:4 * P], prob[:, n % 2, (qt + 1) * P:(qt + 1) * P + META], ident[:])\
                    .then_inc(ev("prob_turned"), 1)
                pe.wait_ge(ev("probT_ready"), n + 1)
                o = ps[(h % 2) * VD:(h % 2 + 1) * VD, h // 2, qt * P:(qt + 1) * P]
                vs = slice(h * VD, (h + 1) * VD)
                for k in range(qt + 1):
                    mm(o, vtok[:, k, vs], probT[:, k, :], start=k == 0, stop=False, skip_group_check=True)
                mm(o, vtok[0:META, qt + 1, vs], probT[0:META, 2, :], start=False, stop=True, skip_group_check=True)\
                    .then_inc(ev("att_out"), 1)
            norm("attn", S)
            pe.wait_ge(ev("aT_ready"), 4)
            pe.wait_ge(ev("split_low"), SP_AT["attn"] + 4)
            for k in range(8):
                unit1(FIRST1["out0"] + k, xh2, xl2, S)
            norm("post_mix", S)
            norm("pre_ffn", S)
            pe.wait_ge(ev("router_loaded"), 64)
            pe.wait_ge(ev("split_low"), SP_AT["ffn"] + DC)
            for t in range(TT):
                o = ps[:, 6, 36 * t:36 * (t + 1)]
                mm(o, ones[0:1, :], b_router[:], start=True, stop=False)
                for c in range(DC):
                    last = mm(o, tT[:, c, t * P:(t + 1) * P], w_router[:, c, :], start=False, stop=c == DC - 1)
            last.then_inc(ev("logits"), 1)
            u0 = FIRST1["shg"]
            for k in range(4):
                unit1(u0 + k, xh2, xl2, S)
            for k in range(TT):
                if k:
                    pe.wait_ge(ev("t_ready"), k)
                for c in range(DC):
                    last = tr(ps[:, 4 + c // 4, (c % 4) * P:(c % 4 + 1) * P], tT[:, c, k * P:(k + 1) * P], ident[:])
                last.then_inc(ev("t_turned"), 1)
                if k == 0:
                    pe.wait_ge(ev("chosen_ready"), 1)
                    o = lambda j: ps[:, 6, P + j * EXPERTS:P + (j + 1) * EXPERTS]
                    mm(o(0), before[:], r_m[:, 0, :], start=True, stop=True)
                    mm(o(1), ones[:], r_m[:, 0, :], start=True, stop=False)
                    mm(o(1), before[:], r_m[:, 1, :], start=False, stop=True)
                    mm(o(2), ones[:], r_m[:, 0, :], start=True, stop=False)
                    mm(o(2), ones[:], r_m[:, 1, :], start=False, stop=True).then_inc(ev("ranks"), 1)
            for k in range(2):
                un = u0 + 4 + k
                pe.wait_ge(ev("unit_split"), un + 1)
                pe.wait_ge(ev("split_low"), SP_AT["shared"] + 2)
                rows(un % NB, 0, HH[:, k, :], HL[:, k, :], k == 0).then_inc(ev("unit_used"), 1)

            def gather(b, pack, width, chunks, done):
                for c in chunks:
                    o = ps[:, c // pack, (c % pack) * width:(c % pack + 1) * width]
                    for t in range(TT):
                        for part, x in enumerate((th, tl)):
                            last = mm(o, x[:, t, c:D:DC], sel[:, b, t, 0:width], start=t == 0 and part == 0,
                                      stop=t == TT - 1 and part == 1)
                last.then_inc(done, 1)

            def half_experts(s, h, up, n):
                for c in range(DC):
                    for q in range(n):
                        last = mm(ps[q * CAP:(q + 1) * CAP, 2 + up, 0:FF],
                                  xg[:, h, c, q * CAP:(q + 1) * CAP], slot(s + q)[:, c * FF:(c + 1) * FF],
                                  start=c == 0, stop=c == DC - 1, skip_group_check=True)
                return last

            def turn_hidden():
                for f in range(2):
                    last = tr(ps[:, 2, FF + f * P:FF + (f + 1) * P], hid[:, f * P:(f + 1) * P], ident[:])
                return last

            def down(s, bank, experts):
                for n in range(2):
                    for f in range(2):
                        for q in range(experts):
                            last = mm(ps[q * CAP:(q + 1) * CAP, bank + n, :], hidT[:, f, q * CAP:(q + 1) * CAP],
                                      slot(s + q)[:, f * D + n * 512:f * D + (n + 1) * 512],
                                      start=f == 0, stop=f == 1, skip_group_check=True)
                return last

            pe.wait_ge(ev("t_ready"), TT)
            pe.wait_ge(ev("sel_ready"), 1)
            pe.wait_ge(ev("shT_ready"), 2)
            gather(0, 4, 2 * CAP, range(4), ev("first_half_gathered"))
            gather(0, 4, 2 * CAP, range(4, DC), ev("second_half_gathered"))
            pe.wait_ge(ev("overflow_known"), 1)
            for k in range(2):
                pe.sem_inc(ev("rows_by_scalar"), 1)
                pe.sem_inc(ev("rows_by_vector"), 1)
            with pe.Fori(0, TURNS) as i:
                for h in range(2):
                    pe.wait_ge(ev("xg_by_scalar"), i * 2 + (h + 1))
                    pe.wait_ge(ev("xg_by_vector"), i * 2 + (h + 1))
                    for up in range(2):
                        sl = 6 * h + 2 * up
                        for q in range(2):
                            pe.wait_ge(*slab_e(i, sl + q))
                        half_experts(sl, h, up, 2).then_inc(ev("expert_slab_used"), 2)
                    pe.wait_ge(ev("sel_ready"), i * 2 + (h + 2))
                    gather((h + 1) % 2, 4, 2 * CAP, range(4), ev("first_half_gathered"))
                    pe.wait_ge(ev("hidden_ready"), i * 2 + (h + 1))
                    turn_hidden().then_inc(ev("hidden_turned"), 1)
                    gather((h + 1) % 2, 4, 2 * CAP, range(4, DC), ev("second_half_gathered"))
                    pe.wait_ge(ev("hidT_ready"), i * 2 + (h + 1))
                    pe.wait_ge(ev("rows_by_scalar"), i * 2 + (h + 1))
                    pe.wait_ge(ev("rows_by_vector"), i * 2 + (h + 1))
                    sl = 6 * h + 4
                    for q in range(2):
                        pe.wait_ge(*slab_e(i, sl + q))
                    down(sl, 4 + 2 * h, 2).then_inc(ev("expert_slab_used"), 2)
            pe.wait_ge(ev("rows_by_scalar"), EXPERTS // 2 + 2)
            pe.wait_ge(ev("rows_by_vector"), EXPERTS // 2 + 2)
            pe.wait_ge(ev("xg_by_scalar"), 2 * TURNS + 1)
            pe.wait_ge(ev("xg_by_vector"), 2 * TURNS + 1)
            more = pe.value_load(overflow[0:1, 0:1], min_val=0, max_val=1)
            with pe.If(more > 0):
                with pe.Fori(0, RANKS // CAP - 1) as r:
                    with pe.Fori(0, EXPERTS) as e:
                        b = r * EXPERTS + e
                        pe.wait_ge(ev("o_sel"), b + 1)
                        gather(0, 8, CAP, range(DC), ev("o_gathered"))
                        pe.wait_ge(ev("o_xg"), b + 1)
                        pe.wait_ge(ev("o_loaded"), b * 48 + 48)
                        half_experts(RING2, 0, 0, 1)
                        half_experts(RING2 + 1, 0, 1, 1).then_inc(ev("o_gate_up"), 1)
                        pe.wait_ge(ev("o_hidden"), b + 1)
                        turn_hidden().then_inc(ev("o_turned"), 1)
                        pe.wait_ge(ev("o_hidT"), b + 1)
                        down(RING2 + 2, 4, 1).then_inc(ev("o_down"), 1)
                        pe.wait_ge(ev("o_rows"), b * 2 + 2)

            pe.wait_ge(ev("routed_ready"), TT)
            for c in range(DC):
                if c >= 2:
                    pe.wait_ge(ev("ffn_ready"), c - 1)
                for t in range(TT):
                    last = tr(ps[:, 4 + c % 2, t * P:(t + 1) * P], gath[:, t, c * P:(c + 1) * P], ident[:])
                last.then_inc(ev("routed_turned"), 1)
            norm("post_ffn", S)
            norm("mix2", S)
            pe.wait_ge(ev("split_low"), SP_AT["mix2"] + DC)
            gw = slot(SLAB_LRU % RING2)[:, 0:2 * 512].rearrange("p (k c n) -> p k c n", k=2, c=DC)

            def gates(c):
                pe.wait_ge(ev("conv_ready"), c + 1)
                if c >= 4:
                    pe.wait_ge(ev("gate_act"), c - 3)
                for k in range(2):
                    for half in range(2):
                        r_ = slice(64 * half, 64 * half + 64)
                        last = mm(ps[r_, 4 + c % 4, k * S:(k + 1) * S], gw[r_, k, c, :], zc[r_, c, :],
                                  start=True, stop=True, skip_group_check=True)
                last.then_inc(ev("gates_done"), 1)

            def in_units(first, i=0):
                for k in range(first, first + 8):
                    pe.wait_ge(ev("unit_split"), i * 8 + (U1 + k + 1))
                    pe.wait_ge(ev("unit_taken_by_scalar"), i * 8 + (TAKEN_S1 + k - 3))
                    columns(k % NB, k % 4, xh2, xl2, S).then_inc(ev("unit_used"), 1)

            with pe.Fori(0, 2) as i:
                in_units(0, i)
            pe.wait_ge(ev("rgate_loaded"), 16)
            pe.wait_ge(*slab2(SLAB_LRU))
            for c in range(4):
                gates(c)
            for k in range(16, 20):
                pe.wait_ge(ev("unit_split"), U1 + k + 1)
                pe.wait_ge(ev("unit_taken_by_scalar"), TAKEN_S1 + k - 3)
                columns(k % NB, k % 4, xh2, xl2, S).then_inc(ev("unit_used"), 1)
            for c in range(4, DC):
                gates(c)
            with pe.Fori(0, 3) as i:
                in_units(20, i)
            for k in range(44, 48):
                pe.wait_ge(ev("unit_split"), U1 + k + 1)
                pe.wait_ge(ev("unit_taken_by_scalar"), TAKEN_S1 + k - 3)
                columns(k % NB, k % 4, xh2, xl2, S).then_inc(ev("unit_used"), 1)
            pe.wait_ge(ev("gate_act"), DC)
            for k in range(TT):
                if k:
                    pe.wait_ge(ev("v_ready"), k)
                for c in range(DC):
                    last = tr(ps[:, 4 + c // 4, (c % 4) * P:(c % 4 + 1) * P], zv[:, c, k * P:(k + 1) * P], ident[:])
                last.then_inc(ev("v_turned"), 1)
            pe.wait_ge(ev("unit_taken_by_scalar"), TAKEN_S1 + 48)

            def z_scores(n):
                j, qt = divmod(n, TT)
                keys = (qt + 1) * P
                b = n % 2
                if n >= 2:
                    pe.wait_ge(ev("sigm_done"), 2 * (n - 1))
                for h in range(2):
                    r_ = slice(64 * h, 64 * h + 64)
                    last = mm(ps[:, 2 * b + h, 0:keys], zq[r_, j, qt * P:(qt + 1) * P], zk[r_, j, 0:keys],
                              start=True, stop=True)
                last.then_inc(ev("z_scores"), 1)

            pe.wait_ge(ev("v_ready"), TT)
            z_scores(0)
            for n in range(HEADS2):
                j, qt = divmod(n, TT)
                nk = qt + 1
                if n + 1 < HEADS2:
                    z_scores(n + 1)
                pe.wait_ge(ev("att_ready"), n + 1)
                if n:
                    pe.wait_ge(ev("attT_ready"), n)
                for h in range(2):
                    for k in range(nk):
                        last = tr(ps[:, 4, (h * nk + k) * P:(h * nk + k + 1) * P],
                                  att(n % 2)[:, h, k * P:(k + 1) * P], ident[:])
                last.then_inc(ev("att_turned"), 1)
                pe.wait_ge(ev("attT_ready"), n + 1)
                if qt == 0 and j >= 2:
                    pe.wait_ge(ev("y_att_taken"), j - 1)
                for h in range(2):
                    o = ps[64 * h:64 * h + 64, 5 + j % 2, qt * P:(qt + 1) * P]
                    for k in range(nk):
                        a = (h * nk + k) * P
                        last = mm(o, vtok2[:, k, (2 * j + h) * DH2:(2 * j + h + 1) * DH2], att_buf(8)[:, a:a + P],
                                  start=k == 0, stop=k == nk - 1, skip_group_check=True)
                last.then_inc(ev("y_att"), 1)

            def unit2(v_no, hi, lo, free=None, arrived=None):
                pe.wait_ge(ev("unit_split"), U1 + v_no + 1)
                if free:
                    pe.wait_ge(*free)
                columns(v_no % NB, v_no % 4, hi, lo, S, arrived=arrived).then_inc(ev("unit_used"), 1)

            by_s = lambda n: (ev("unit_taken_by_scalar"), TAKEN_S1 + n)
            by_v = lambda n: (ev("unit_taken_by_vector"), TAKEN_V1 + n)
            for k in range(8):
                unit2(U_GATT + k, xh2, xl2, by_s(48 + k - 3))
            for k in range(8):
                unit2(U_BRL + k, xh2, xl2, by_s(56 + k - 3) if k < 4 else by_v(k - 3),
                      arrived=None if k else SP_AT["y_lru"])
            for k in range(8):
                unit2(U_BRA + k, xh2, xl2, by_v(8 + k - 3), arrived=None if k else SP_AT["y_att"])
            for k in range(8):
                unit2(U_OUT + k, xh2, xl2, by_v(16 + k - 3) if k < 4 else (ev("h_mixed2"), k - 3),
                      arrived=None if k else SP_AT["merged2"])
            norm("mlp2", S)
            pe.wait_ge(ev("zeros_ready"), 2)
            pe.wait_ge(ev("std_ready"), NORM_NO["mlp2"] + 1)
            for b in range(4):
                mm(ps[:, 4 + b, :], zero_w, zero_x, start=True, stop=True)
            pe.wait_ge(ev("split_low"), SP_AT["mlp2"] + DC)
            with pe.Fori(0, 4) as i:
                for k in range(16):
                    pe.wait_ge(ev("unit_split"), i * 16 + (U1 + U_MLP + k + 1))
                    if k % 4 < 2:
                        columns(k % NB, k % 4, xh2, xl2, S).then_inc(ev("unit_used"), 1)
                    else:
                        f = (k // 4) * 2 + k % 2
                        pe.wait_ge(ev("relu_low"), i * 8 + (f + 1))
                        rows(k % NB, 4, HH[:, f % 2, :], HL[:, f % 2, :], False).then_inc(ev("unit_used"), 1)
            pe.wait_ge(ev("p_loaded"), 16 * TT)
            for c in range(2):
                for t in range(TT):
                    last = tr(ps[:, 2 + c, t * P:(t + 1) * P], p_tok(t)[:, c * P:(c + 1) * P], ident[:])
                last.then_inc(ev("p_turned"), 1)
            pe.wait_ge(ev("h_mlp"), DC)
            norm("ple2", S)
            pe.wait_ge(ev("std_ready"), NORM_NO["ple2"] + 1)
            gate_units = [k for k in range(10) if SLABS2[UNITS2[U_PLE + k][0]][0] == "col"]
            for k in range(10):
                if k in gate_units:
                    former = by_s(56 + gate_units.index(k - 4) + 1) if k - 4 in gate_units else None
                    unit2(U_PLE + k, xh2, xl2, former, arrived=None if k else SP_AT["ple2"])
                else:
                    pe.wait_ge(ev("unit_split"), U1 + U_PLE + k + 1)
                    pe.wait_ge(ev("split_low"), SP_AT["p2"] + 2)
                    rows(k % NB, 4, HH[:, k - 2, :], HL[:, k - 2, :], k == 2).then_inc(ev("unit_used"), 1)
            pe.wait_ge(ev("h_ple"), DC)
            norm("final2", S)
            pe.wait_ge(ev("result"), DC)
            for k in range(TT):
                for c in range(DC):
                    last = tr(ps[:, 4 * k + c // 4, (c % 4) * P:(c % 4 + 1) * P], zg[:, c, k * P:(k + 1) * P], ident[:])
                last.then_inc(ev("result_turned"), 1)


def kernel(**inputs):
    import concourse.bacc as bacc
    from concourse.bass_utils import run_bass_kernel_spmd

    nc = bacc.Bacc("TRN2", target_bir_lowering=False, num_devices=1)
    arrays, aps = {}, {}
    for name, a in inputs.items():
        a = np.ascontiguousarray(a)
        arrays[f"in_{name}"] = a
        aps[name] = nc.dram_tensor(f"in_{name}", a.shape, mybir.dt.from_np(a.dtype), kind="ExternalInput").ap()
    out = nc.dram_tensor("out_tokens_by_features", (1, S, D), F32, kind="ExternalOutput").ap()
    build(nc, aps, out)
    r = run_bass_kernel_spmd(nc, [arrays], core_ids=[0])
    return r.results[0]["out_tokens_by_features"]
```

```python
import math
from contextlib import ExitStack

import numpy as np
import concourse.bass as bass
from concourse import mybir

F32 = mybir.dt.float32
F32R = mybir.dt.float32r
BF16 = mybir.dt.bfloat16
I32 = mybir.dt.int32
ALU = mybir.AluOpType
ACT = mybir.ActivationFunctionType
AX = mybir.AxisListType

P = 128
D = 1024
DC = D // P
S = 256
META = 16
T = S + META
TT = S // P
EPS = 1e-6
HEADS, NOPE, ROPE, VD = 8, 64, 32, 64
QD = NOPE + ROPE
Q_LORA, KV_LORA, CONV = 256, 128, 512
ATTN = HEADS * VD
SCALE1 = QD ** -0.5
GROUPS, EPG, EXPERTS, FF = 4, 8, 32, 256
CAP = 64
RANKS = S
HEADS2, DH2 = 16, 64
SCALE2 = DH2 ** -0.5
FF2 = 4 * D
LRU_C = 8.0
MASKED = -(2.0 ** 100)

SLAB = 2048
RING = 12
RING2 = 8
NB = 4
UNIT = 1024

SLABS1 = [("cq", 2), ("kv", 2), ("gc0", 2), ("gc1", 2), ("xin0", 2), ("xin1", 2), ("gb0", 2), ("gb1", 2),
          ("uq", 8), ("ukv", 1), ("out0", 2), ("out1", 2), ("out2", 2), ("out3", 2),
          ("shg", 2), ("shu", 2), ("shd", 2)]
N1 = len(SLABS1)
SHIFT1 = (-N1) % RING
U1 = sum(n for _, n in SLABS1)
UNITS1 = [(i, name, j) for i, (name, n) in enumerate(SLABS1) for j in range(n)]
LAST1 = [max(u for u, (i, _, _) in enumerate(UNITS1) if i == s) for s in range(N1)]
FIRST1 = {name: min(u for u, (i, _, _) in enumerate(UNITS1) if i == s) for s, (name, _) in enumerate(SLABS1)}
BY_VECTOR = ("xin0", "xin1", "gb0", "gb1")
UNCOUNTED = ("ukv", "shu", "shd")

SLABS2 = ([("col", "w_in_2", s) for s in range(8)] + [("lru", "", 0)] + [("col", "w_in_2", s) for s in range(8, 28)]
          + [("col", "w_br_lru_2", s) for s in range(4)] + [("col", "w_br_att_2", s) for s in range(4)]
          + [("col", "w_out_2", s) for s in range(4)]
          + [(("col", "w_mlp_up_2", s), ("row", "w_mlp_down_2", s))[k] for s in range(FF2 // 256) for k in range(2)]
          + [("col", "w_ple_gate_2", 0), ("row", "w_ple_2", 0)] + [("col", "w_ple_gate_2", s) for s in (1, 2, 3)])
N2 = len(SLABS2)
UNITS2 = [(m, j) for m, (kind, _, _) in enumerate(SLABS2) if kind != "lru" for j in range(2)]
U2 = len(UNITS2)
SLAB_LRU = 8
SLAB_MLP = 28 + 3 * 4 + 1
U_IN, U_GATT, U_BRL, U_BRA, U_OUT, U_MLP, U_PLE = 0, 48, 56, 64, 72, 80, 144

VEC1 = [("pre_mix_norm", 8), ("post_mix_norm", 8), ("pre_ffn_norm", 8), ("post_ffn_norm", 8), ("q_norm", 2),
        ("kv_norm", 1), ("attn_out_norm", 4), ("conv_out_norm", 4), ("conv_w", 12)]
VEC2 = [("norm_mix_g_2", 8), ("conv_w_2", 32), ("conv_b_2", 8), ("b_rgate_2", 8), ("b_igate_2", 8),
        ("lru_lambda_2", 8), ("norm_mlp_g_2", 8), ("norm_ple_g_2", 8), ("norm_final_g_2", 8)]


def offsets(table):
    at, out = 0, {}
    for name, n in table:
        out[name] = at
        at += n
    return out, at


V1, NV1 = offsets(VEC1)
V2, NV2 = offsets(VEC2)
NORMS = [("pre_mix", 8), ("ckv", 1), ("cq", 2), ("conv", 4), ("attn", 4), ("post_mix", 8), ("pre_ffn", 8),
         ("post_ffn", 8), ("mix2", 8), ("mlp2", 8), ("ple2", 8), ("final2", 8)]
SQ_AT, _ = offsets(NORMS)
NORM_NO = {name: i for i, (name, _) in enumerate(NORMS)}
NCH = dict(NORMS)
SPLITS = [("pre_mix", 8), ("ckv", 1), ("cq", 2), ("conv", 4), ("attn", 4), ("ffn", 8), ("shared", 2),
          ("mix2", 8), ("y_lru", 8), ("y_att", 8), ("merged2", 8), ("mlp2", 8), ("p2", 2), ("ple2", 8)]
SP_AT, _ = offsets(SPLITS)
NSP = dict(SPLITS)
IN_PLACE = ("y_lru", "y_att", "merged2")
VALUE_AT, _ = offsets([(name, 0 if name in IN_PLACE else n) for name, n in SPLITS])


def build(nc, A, out):
    ctx = ExitStack()
    with ctx:
        def sb(name, shape, dt=F32):
            return ctx.enter_context(nc.sbuf_tensor(name, shape, dt))

        made = {}

        def ev(name):
            if name not in made:
                made[name] = ctx.enter_context(nc.semaphore(name))
            return made[name]

        y_rows = nc.dram_tensor("expert_rows", [EXPERTS * CAP, D], F32, kind="Internal").ap()
        y_more = nc.dram_tensor("expert_rows_behind", [EXPERTS * (RANKS - CAP), D], F32, kind="Internal").ap()

        ARENA = RING * SLAB
        big = sb("big", [P, ARENA + 8448])
        WH = sb("WH", [P, NB, UNIT], F32R)
        WL = sb("WL", [P, NB, UNIT], F32R)
        XH = sb("XH", [P, DC * T], F32R)
        XL = sb("XL", [P, DC * T], F32R)
        HH = sb("HH", [P, 2, S], F32R)
        HL = sb("HL", [P, 2, S], F32R)
        KH = sb("KH", [P, 3 * P], F32R)
        KL = sb("KL", [P, 3 * P], F32R)
        hT = sb("hT", [P, DC, T])
        XT = sb("XT", [P, 2, T])
        std = sb("std", [P, T])
        rstd = sb("rstd", [P, T])
        cos_t = sb("cos_t", [P, T])
        sin_t = sb("sin_t", [P, T])
        ident = sb("ident", [P, P])
        ones = sb("ones", [P, P])
        before = sb("before", [P, P])
        swap = sb("swap", [QD, QD])
        causal = sb("causal", [P, P])
        strict = sb("strict", [P, P])
        sel = sb("sel", [P, 2, TT, 2 * CAP], F32R)
        w_router = sb("w_router", [P, DC, GROUPS + EXPERTS])
        b_router = sb("b_router", [1, GROUPS + EXPERTS])
        vec1 = sb("vec1", [P, NV1])
        vec2 = sb("vec2", [P, NV2])
        rank_or = sb("rank_or", [P, TT, EXPERTS + 2])
        iota_slot = sb("iota_slot", [P, CAP])
        iota_e = sb("iota_e", [P, EXPERTS])
        small = sb("small", [P, 12])
        warm = sb("warm", [1, 5])
        small_lru = sb("small_lru", [P, 5 * DC])
        overflow = sb("overflow", [1, 1], I32)
        slot_i = sb("slot_i", [P, 4 * TT], I32)
        ps = ctx.enter_context(nc.psum_tensor("ps", [P, 8, 512], F32))

        def ar(a, n, **k):
            return big[:, ARENA + a:ARENA + a + n]

        def slot(s):
            return big[:, s * SLAB:(s + 1) * SLAB]

        x_tok = ar(0, 3 * D).rearrange("p (t d) -> p t d", t=3)
        vrow1, vrow2 = ar(3072, P), ar(3200, P)
        inv_row, pos_row = ar(3328, P), ar(3456, T)
        pos_int = ar(3728, S).bitcast(I32)
        kpe = ar(0, T)
        cq = ar(272, 2 * T).rearrange("p (c t) -> p c t", c=2)
        ckv = ar(816, T)
        u = ar(1088, 4 * T).rearrange("p (c t) -> p c t", c=4)
        yc = ar(2176, 4 * S).rearrange("p (c t) -> p c t", c=4)
        vtok = ar(640, 3 * ATTN).rearrange("p (k n) -> p k n", k=3)
        qcat = ar(3200, HEADS * S).rearrange("p (h t) -> p h t", h=HEADS)
        kcat = ar(5248, HEADS * T).rearrange("p (h t) -> p h t", h=HEADS)
        prob = ar(7424, 2 * T).rearrange("p (b t) -> p b t", b=2)

        def probT(b):
            t = (ar(7968, 3 * P), XT[:].rearrange("p b t -> p (b t)")[:, 0:3 * P])[b]
            return t.rearrange("p (k t) -> p k t", k=3)

        rope_a = ar(7424, 2 * S)
        ang = ar(5248, T)
        ang_k = ar(5520, T)
        aT = ar(2176, 4 * S).rearrange("p (c t) -> p c t", c=4)
        mixT = ar(3200, DC * S).rearrange("p (c t) -> p c t", c=DC)
        tT = ar(5248, DC * S).rearrange("p (c t) -> p c t", c=DC)
        xg = ar(0, 2 * DC * 2 * CAP).rearrange("p (b c s) -> p b c s", b=2, c=DC)
        yrow = ar(2048, 2 * D).rearrange("p (b d) -> p b d", b=2)
        gact = ar(4096, FF)
        hid = ar(4352, FF)
        hidT = ar(4608, FF).rearrange("p (f s) -> p f s", f=2)
        sact = ar(4608, 2 * S).rearrange("p (f t) -> p f t", f=2)
        rt = ar(7296, 1152)
        shT = ar(5248, DC * S).rearrange("p (c t) -> p c t", c=DC)
        gath = ar(0, 4 * D).rearrange("p (k d) -> p k d", k=4)
        gath_more = big[:, RING2 * SLAB:RING2 * SLAB + 4 * D].rearrange("p (k d) -> p k d", k=4)
        Z0 = RING2 * SLAB

        def z(g):
            return big[:, Z0 + g * SLAB:Z0 + (g + 1) * SLAB].rearrange("p (c t) -> p c t", c=DC)

        zx, zg, zq, zk, zv, zl, zc, zi = (z(g) for g in range(8))
        vtok2 = big[:, Z0 + 6 * SLAB:Z0 + 7 * SLAB].rearrange("p (k n) -> p k n", k=TT)

        def att_buf(i):
            g = (0, 4, 7)[i // 4]
            at = Z0 + g * SLAB + (i % 4) * 512
            return big[:, at:at + 512]

        def attT(b):
            return att_buf(8 + 2 * b)

        def cum(b):
            at = Z0 + 4 * SLAB + b * 2 * (S + 1)
            return big[:, at:at + 2 * (S + 1)].rearrange("p (h k) -> p h k", h=2)

        def att(b):
            at = (Z0 + 4 * SLAB + 4 * (S + 1), Z0 + 7 * SLAB + 512)[b]
            return big[:, at:at + 2 * S].rearrange("p (h k) -> p h k", h=2)

        def p_tok(t):
            return big[:, Z0 + 6 * SLAB + t * 256:Z0 + 6 * SLAB + (t + 1) * 256]

        def out_tok(k):
            return big[:, Z0 + (2 + k) * SLAB:Z0 + (2 + k) * SLAB + D]

        zero_w = cos_t[0:1, 0:P // 2].bitcast(BF16)
        zero_x = sin_t[0:1, 0:256].bitcast(BF16)

        X8 = lambda t, n: t[:, 0:DC * n].rearrange("p (c t) -> p c t", c=DC)
        xh1, xl1 = X8(XH, T), X8(XL, T)
        xh2, xl2 = X8(XH, S), X8(XL, S)
        th = XH[:, 0:TT * D].rearrange("p (k d) -> p k d", k=TT)
        tl = XL[:, 0:TT * D].rearrange("p (k d) -> p k d", k=TT)
        hx = hT[:, :, META:T]

        def pcn(ap, c=DC):
            return ap.rearrange("(c p) n -> p c n", p=P)

        w_in, w_uq, w_ukv, w_out = A["w_in"][0], A["w_uq"][0], A["w_ukv"][0], A["w_out"][0]

        def pack1(u_no, buf):
            i, name, j = UNITS1[u_no]
            s = slot((i + SHIFT1) % RING)
            if name == "kv":
                v = s[:, 0:8 * 160].rearrange("p (c n) -> p c n", c=DC)
                o = buf.rearrange("p (c n) -> p c n", c=DC)
                if j == 0:
                    return v[:, :, 0:P], o
                rep = v[:, :, P:P + ROPE].unsqueeze(2).to_broadcast([P, DC, 4, ROPE])
                return rep, buf.rearrange("p (c r n) -> p c r n", c=DC, r=4)
            if name == "uq":
                v = s[:, 0:2 * 768].rearrange("p (c n) -> p c n", c=2)
                return v[:, :, j * QD:(j + 1) * QD], buf[:, 0:2 * QD].rearrange("p (c n) -> p c n", c=2)
            if name == "ukv":
                v = s[:, 0:D].rearrange("p (h two n) -> p two h n", h=HEADS, two=2)
                return v, buf.rearrange("p (two h n) -> p two h n", h=HEADS, two=2)
            if name == "shd":
                return s[:, j * D:(j + 1) * D], buf
            return col_half(s, j), buf.rearrange("p (c n) -> p c n", c=DC)

        def col_half(s, j):
            return s.rearrange("p (c n) -> p c n", c=DC)[:, :, j * P:(j + 1) * P]

        def pack2(u_no, buf):
            m, j = UNITS2[u_no]
            s = slot(m % RING2)
            if SLABS2[m][0] == "row":
                return s[:, j * D:(j + 1) * D], buf
            return col_half(s, j), buf.rearrange("p (c n) -> p c n", c=DC)

        def slab1(i):
            s = (i + SHIFT1) % RING
            return ev(f"slab_in_slot_{s}"), 16 * (1 + sum((k + SHIFT1) % RING == s for k in range(i)))

        uses1 = [sum((k + SHIFT1) % RING == s for k in range(N1)) for s in range(RING)]
        GROUP = 4
        TURNS = EXPERTS // GROUP

        def slab_e(i, s):
            return ev(f"slab_in_slot_{s}"), 16 * (uses1[s] + 1) + i * 16

        def slab2(m, turn=None, per=0):
            s = m % RING2
            v = 16 * (uses1[s] + TURNS + m // RING2 + 1)
            return ev(f"slab_in_slot_{s}"), v if turn is None else turn * (16 * per // RING2) + v

        def taken1(u_no):
            names = [UNITS1[k][1] for k in range(u_no + 1) if UNITS1[k][1] not in UNCOUNTED]
            mine = names[-1] in BY_VECTOR
            n = sum((x in BY_VECTOR) == mine for x in names)
            return ev("unit_taken_by_vector" if mine else "unit_taken_by_scalar"), n

        TAKEN_S1 = sum(n for x, n in SLABS1 if x not in BY_VECTOR + UNCOUNTED)
        TAKEN_V1 = sum(n for x, n in SLABS1 if x in BY_VECTOR)

        g1 = lambda name, c=0: vec1[:, V1[name] + c:V1[name] + c + 1]
        g2 = lambda name, c=0: vec2[:, V2[name] + c:V2[name] + c + 1]

        def rts(a, n, k=None):
            v = rt[:, a:a + TT * n]
            return v.rearrange("p (t n) -> p t n", t=TT)

        logit = rts(0, 36)
        glog, elog = logit[:, :, 0:GROUPS], logit[:, :, GROUPS:]
        r_oh1, r_oh2 = rts(72, 32), rts(136, 32)
        r_em, r_key = rts(200, 32), rts(264, 32)
        r_m = rts(392, 32)
        r_g4, r_g4k, r_ohg = rts(456, 4), rts(464, 4), rts(472, 4)
        r_ge = rts(480, 4)
        r_s = lambda i: rt[:, 488 + 2 * i:490 + 2 * i]
        w_k = lambda k: small[:, 2 * k:2 * k + 2]
        diag = lambda k: rt[:, k * P:(k + 1) * P]
        behind = lambda k: small[:, 4 + 2 * k:6 + 2 * k]
        before_cap = lambda k: small[:, 8 + 2 * k:10 + 2 * k]

        block = ctx.enter_context(nc.Block())

        @block.sync
        def _(sp):
            for k in range(TT):
                sp.dma_start(x_tok[:, k, :], A["x"][0, k * P:(k + 1) * P, :]).then_inc(ev("x_loaded"), 16)
            sp.dma_start(x_tok[0:META, 2, :], A["meta_tokens"]).then_inc(ev("x_loaded"), 16)
            cols = {"cq": (0, 256), "kv": (256, 416), "gb0": (416, 672), "gb1": (672, 928), "gc0": (928, 1184),
                    "gc1": (1184, 1440), "xin0": (1440, 1696), "xin1": (1696, 1952)}
            sp.wait_ge(ev("vec1_loaded"), 16 * len(VEC1))
            for i, (name, _) in enumerate(SLABS1):
                if i >= RING:
                    sp.wait_ge(ev("unit_split"), LAST1[i - RING] + 1)
                s = slot((i + SHIFT1) % RING)
                if name in cols:
                    a, b = cols[name]
                    dst, src = s[:, 0:DC * (b - a)].rearrange("p (c n) -> p c n", c=DC), pcn(w_in)[:, :, a:b]
                elif name == "uq":
                    dst, src = s[:, 0:2 * 768].rearrange("p (c n) -> p c n", c=2), pcn(w_uq)
                elif name == "ukv":
                    dst, src = s[:, 0:D], w_ukv
                elif name.startswith("out"):
                    a = 256 * int(name[3:])
                    dst, src = s.rearrange("p (c n) -> p c n", c=DC), pcn(w_out)[:, :, a:a + 256]
                elif name in ("shg", "shu"):
                    w = A["w_sh_gate" if name == "shg" else "w_sh_up"][0]
                    dst, src = s.rearrange("p (c n) -> p c n", c=DC), pcn(w)
                else:
                    dst, src = s.rearrange("p (c n) -> p c n", c=2), pcn(A["w_sh_down"][0])
                sp.dma_start(dst, src).then_inc(slab1(i)[0], 16)

            def expert_slab(e, s, kind):
                if kind < 2:
                    w = A["w_gate" if kind == 0 else "w_up"][0]
                    src = w[bass.ds(e, 1)].rearrange("e (p c) n -> p (e c) n", p=P)
                    dst = slot(s).rearrange("p (c n) -> p c n", c=DC)
                else:
                    src = A["w_down"][0][bass.ds(e, 1)].rearrange("e (c p) n -> p (e c) n", p=P)
                    dst = slot(s).rearrange("p (c n) -> p c n", c=2)
                sp.dma_start(dst, src).then_inc(ev(f"slab_in_slot_{s}"), 16)

            KINDS = [(0, 0), (1, 0), (0, 1), (1, 1), (0, 2), (1, 2)]

            for s in range(RING):
                last = max(i for i in range(N1) if (i + SHIFT1) % RING == s)
                sp.wait_ge(ev("unit_split"), LAST1[last] + 1)
                e, kind = KINDS[s % 6]
                expert_slab(2 * (s // 6) + e, s, kind)
            with sp.Fori(0, TURNS - 1) as i:
                for s in range(RING):
                    sp.wait_ge(ev("expert_slab_used"), i * RING + (s + 1))
                    e, kind = KINDS[s % 6]
                    expert_slab(i * GROUP + (GROUP + 2 * (s // 6) + e), s, kind)

            def second_slab(m, ds=0):
                kind, name, j = SLABS2[m]
                s = slot(m % RING2)
                if kind == "lru":
                    for k, (w, done) in enumerate(((A["w_rgate_2"], ev("rgate_loaded")), (A["w_igate_2"], slab2(m)[0]))):
                        sp.dma_start(s[:, k * 512:(k + 1) * 512].rearrange("p (c n) -> p c n", c=DC),
                                     w[0].rearrange("(c b) r n -> (b r) c n", b=2)).then_inc(done, 16)
                    return
                w = A[name][0]
                if kind == "col":
                    sp.dma_start(s.rearrange("p (c n) -> p c n", c=DC),
                                 pcn(w)[:, :, bass.ds(j * 256 + ds, 256)]).then_inc(slab2(m)[0], 16)
                else:
                    sp.dma_start(s.rearrange("p (c n) -> p c n", c=2),
                                 w[bass.ds(j * 256 + ds, 256), :].rearrange("(c p) n -> p c n", p=P))\
                        .then_inc(slab2(m)[0], 16)

            for m in range(RING2):
                sp.wait_ge(ev("expert_slab_used"), RING * (TURNS - 1) + m + 1)
                if m == 2:
                    for k in range(2 * TT):
                        sp.wait_ge(ev(f"rows_gathered_{k}"), 16)
                second_slab(m)

            def slot_empty(m):
                before_m = m - RING2
                if before_m == SLAB_LRU:
                    sp.wait_ge(ev("gates_done"), DC)
                else:
                    done = max(k for k, (mm, _) in enumerate(UNITS2) if mm == before_m) + 1
                    sp.wait_ge(ev("unit_split"), U1 + done)

            for m in range(RING2, SLAB_MLP + RING2):
                slot_empty(m)
                second_slab(m)
            with sp.Fori(0, 3) as i:
                for m in range(SLAB_MLP + RING2, SLAB_MLP + 2 * RING2):
                    sp.wait_ge(ev("unit_split"), i * (2 * RING2) + (U1 + U_MLP + 2 * (m - RING2 - SLAB_MLP + 1)))
                    second_slab(m, i * (RING2 // 2 * 256))
            for m in range(SLAB_MLP + 4 * RING2, N2):
                slot_empty(m)
                second_slab(m)

            for k in range(TT):
                sp.wait_ge(ev("out_tokens_by_scalar"), k + 1)
                sp.wait_ge(ev("out_tokens_by_vector"), k + 1)
                sp.dma_start(out[0, k * P:(k + 1) * P, :], out_tok(k))\
                    .then_inc(ev("out_stored"), 16)
            sp.wait_ge(ev("out_stored"), 16 * TT)

        @block.gpsimd
        def _(pool):
            g = nc.gpsimd
            g.memset(ident[:], 0.0).then_inc(ev("pool_zeroed"), 1)
            g.memset(before[:], 0.0).then_inc(ev("pool_zeroed"), 1)
            g.memset(swap[:], 0.0).then_inc(ev("pool_zeroed"), 1)
            g.memset(causal[:], 0.0).then_inc(ev("pool_zeroed"), 1)
            g.memset(strict[:], 0.0).then_inc(ev("pool_zeroed"), 1)
            g.memset(inv_row[0:1, :], 0.0).then_inc(ev("pool_zeroed"), 1)
            pool.wait_ge(ev("pool_zeroed"), 6)
            g.affine_select(out=ident[:], in_=ident[:], compare_op=ALU.not_equal, fill=1.0, base=0,
                            pattern=[[-1, P]], channel_multiplier=1).then_inc(ev("ident_ready"), 1)
            g.memset(zero_w, 0.0).then_inc(ev("zeros_ready"), 1)
            g.memset(zero_x, 0.0).then_inc(ev("zeros_ready"), 1)
            g.memset(ones[:], 1.0).then_inc(ev("ones_ready"), 1)
            for f in range(ROPE // 2):
                inv = float(np.float32(1.0) / np.float32(np.float32(10000.0) ** np.float32(2 * f / ROPE)))
                g.memset(inv_row[0:1, NOPE + f:QD:ROPE // 2], inv).then_inc(ev("inv_ready"), 1)
            g.affine_select(out=before[:], in_=before[:], compare_op=ALU.is_ge, fill=1.0, base=0,
                            pattern=[[-1, P]], channel_multiplier=1).then_inc(ev("routing_consts"), 1)
            g.affine_select(out=causal[:], in_=causal[:], compare_op=ALU.is_ge, fill=MASKED, base=0,
                            pattern=[[-1, P]], channel_multiplier=1).then_inc(ev("masks_ready"), 1)
            g.affine_select(out=strict[:], in_=strict[:], compare_op=ALU.is_gt, fill=MASKED, base=0,
                            pattern=[[-1, P]], channel_multiplier=1).then_inc(ev("masks_ready"), 1)
            half = ROPE // 2
            a = swap[:, NOPE:NOPE + half]
            g.affine_select(out=a, in_=a, compare_op=ALU.not_equal, fill=-1.0, base=-(NOPE + half),
                            pattern=[[-1, half]], channel_multiplier=1).then_inc(ev("swap_ready"), 1)
            a = swap[:, NOPE + half:QD]
            g.affine_select(out=a, in_=a, compare_op=ALU.not_equal, fill=1.0, base=-NOPE,
                            pattern=[[-1, half]], channel_multiplier=1).then_inc(ev("swap_ready"), 1)
            g.iota(iota_slot[:], [[1, CAP]], base=0, channel_multiplier=0,
                   allow_small_or_imprecise_dtypes=True).then_inc(ev("routing_consts"), 1)
            g.iota(iota_e[:], [[1, EXPERTS]], base=0, channel_multiplier=0,
                   allow_small_or_imprecise_dtypes=True).then_inc(ev("routing_consts"), 1)
            g.iota(pos_row[0:1, 0:META], [[1, META]], base=0, channel_multiplier=0,
                   allow_small_or_imprecise_dtypes=True).then_inc(ev("meta_pos"), 1)
            g.memset(rank_or[:], -1.0).then_inc(ev("routing_consts"), 1)
            row = 0
            for name, n in VEC2:
                v = A[name] if name == "norm_final_g_2" else A[name][0]
                if len(v.shape) == 2:
                    v = v.rearrange("k n -> (k n)")
                pool.dma_start(vrow2[row:row + n, :], v.rearrange("(c p) -> c p", p=P)).then_inc(ev("vec2_loaded"), 16)
                row += n

            pool.sem_inc(ev("row_buffer_free"), 2)
            with pool.Fori(0, TURNS) as i:
                for h in range(2):
                    pool.wait_ge(ev("rows_by_scalar"), i * 2 + (h + 1 + 2))
                    pool.wait_ge(ev("rows_by_vector"), i * 2 + (h + 1 + 2))
                    pool.dma_start(y_rows[bass.ds((i * 2 + h) * (2 * CAP), 2 * CAP), :], yrow[:, h, :])\
                        .then_inc(ev("rows_stored"), 16)
                    pool.wait_ge(ev("rows_stored"), i * 32 + 16 * (h + 1))
                    pool.sem_inc(ev("row_buffer_free"), 1)
            pool.wait_ge(ev("overflow_known"), 1)
            more = pool.value_load(overflow[0:1, 0:1], min_val=0, max_val=1)
            with pool.If(more > 0):
                with pool.Fori(0, RANKS // CAP - 1) as r:
                    with pool.Fori(0, EXPERTS) as e:
                        b = r * EXPERTS + e
                        for kind, w in enumerate((A["w_gate"], A["w_up"], A["w_down"])):
                            lay = "e (p c) n -> p (e c) n" if kind < 2 else "e (c p) n -> p (e c) n"
                            pool.dma_start(slot(RING2 + kind).rearrange("p (c n) -> p c n", c=DC if kind < 2 else 2),
                                           w[0][bass.ds(e, 1)].rearrange(lay, p=P)).then_inc(ev("o_loaded"), 16)
                        pool.wait_ge(ev("o_rows"), 2 * b + 2)
                        pool.dma_start(y_more[bass.ds(e * (RANKS - CAP) + r * CAP, CAP), :], yrow[0:CAP, 0, :])\
                            .then_inc(ev("o_stored"), 16)
                        pool.wait_ge(ev("o_stored"), b * 16 + 16)
                for k in range(2 * TT):
                    g.indirect_dma_start(gath_more[:, k, :], None, y_more[:, :],
                                         bass.IndirectOffsetOnAxis(ap=slot_i[:, 2 * TT + k:2 * TT + k + 1], axis=0))\
                        .then_inc(ev("o_rows_gathered"), 16)
            for t in range(TT):
                for k in range(2):
                    g.indirect_dma_start(gath[:, 2 * k + t, :], None, y_rows[:, :],
                                         bass.IndirectOffsetOnAxis(ap=slot_i[:, 2 * k + t:2 * k + t + 1], axis=0))\
                        .then_inc(ev(f"rows_gathered_{TT * k + t}"), 16)
            pool.wait_ge(ev("y_att"), HEADS2)
            for t in range(TT):
                pool.dma_start(p_tok(t), A["p_2"][0, 0, t * P:(t + 1) * P, :]).then_inc(ev("p_loaded"), 16)

        @block.scalar
        def _(act):
            s = nc.scalar
            row = 0
            act.dma_start(pos_int[0:1, :], A["positions"]).then_inc(ev("pos_loaded"), 16)
            for name, n in VEC1:
                v = A[name][0]
                if len(v.shape) == 2:
                    v = v.rearrange("k n -> (k n)")
                act.dma_start(vrow1[row:row + n, :], v.rearrange("(c p) -> c p", p=P)).then_inc(ev("vec1_loaded"), 16)
                row += n
            act.dma_start(w_router[:, :, 0:GROUPS], pcn(A["w_group_router"][0])).then_inc(ev("router_loaded"), 16)
            act.dma_start(w_router[:, :, GROUPS:], pcn(A["w_expert_router"][0])).then_inc(ev("router_loaded"), 16)
            act.dma_start(b_router[:, 0:GROUPS], A["b_group_router"]).then_inc(ev("router_loaded"), 16)
            act.dma_start(b_router[:, GROUPS:], A["b_expert_router"]).then_inc(ev("router_loaded"), 16)

            def high1(u_no):
                if u_no >= U1:
                    return
                if u_no >= NB:
                    act.wait_ge(ev("unit_used"), u_no - NB + 1)
                act.wait_ge(*slab1(UNITS1[u_no][0]))
                src, dst = pack1(u_no, WH[:, u_no % NB, :])
                s.activation(dst, src, ACT.Copy).then_inc(ev("unit_high"), 1)

            def high2(v, turn=None):
                if v >= U2:
                    return
                n = U1 + v
                m = UNITS2[v][0]
                base = 0 if turn is None else turn * 16
                act.wait_ge(ev("unit_used"), base + (n - NB + 1))
                act.wait_ge(*slab2(m, turn, RING2))
                src, dst = pack2(v, WH[:, v % NB, :])
                s.activation(dst, src, ACT.Copy).then_inc(ev("unit_high"), 1)

            def take1(u_no, dst, func=ACT.Copy, rows=P, n=T):
                act.wait_ge(ev("unit_used"), u_no + 1)
                s.activation(dst, ps[0:rows, u_no % 4, 0:n], func).then_inc(ev("unit_taken_by_scalar"), 1)

            def square_root_ahead(k):
                s.activation(warm[0:1, k:k + 1], ones[0:1, 0:1], ACT.Sqrt)

            def squares(name, srcs, n, each=None):
                for c, src in enumerate(srcs):
                    if each:
                        act.wait_ge(ev(each), c + 1)
                    square(name, c, src, n)
                root_of_mean(name, n)

            def square(name, c, src, n):
                splits_before = {"pre_mix": 0, "ckv": 8, "cq": 9, "conv": 11, "attn": 15, "post_mix": 19,
                                 "pre_ffn": 19, "post_ffn": 29, "mix2": 29, "mlp2": 61, "ple2": 71, "final2": 79}
                if c == 0 and splits_before[name]:
                    act.wait_ge(ev("split_low"), splits_before[name])
                k = SQ_AT[name] + c
                if k >= 2:
                    act.wait_ge(ev("squares_summed"), k - 1)
                s.activation(XT[:, k % 2, 0:n], src, ACT.Square).then_inc(ev("square_ready"), 1)

            def root_of_mean(name, n):
                act.wait_ge(ev("squares_summed"), SQ_AT[name] + NCH[name])
                if NORM_NO[name]:
                    act.wait_ge(ev("rstd_ready"), NORM_NO[name])
                s.activation(std[:, 0:n], ps[:, 7, 0:n], ACT.Sqrt, scale=1.0 / (NCH[name] * P), bias=EPS)\
                    .then_inc(ev("std_ready"), 1)

            def highs_in_place(name, srcs, dsts, wait):
                act.wait_ge(*wait)
                for src, dst in zip(srcs, dsts):
                    s.activation(dst, src, ACT.Copy).then_inc(ev("split_high"), 1)

            def highs(name, dsts, n, wait=None):
                if wait:
                    act.wait_ge(*wait)
                for c, dst in enumerate(dsts):
                    k = SP_AT[name] + c
                    act.wait_ge(ev("split_value"), VALUE_AT[name] + c + 1)
                    s.activation(dst, XT[:, k % 2, 0:n], ACT.Copy).then_inc(ev("split_high"), 1)

            for c in range(0, DC, 2):
                act.wait_ge(ev("x_turned"), c + 1)
                s.activation(hT[:, c, :], ps[:, c % 4, 0:T], ACT.Copy).then_inc(ev("hT_by_scalar"), 1)
            act.wait_ge(ev("hT_by_scalar"), 4)
            act.wait_ge(ev("hT_by_vector"), 4)
            act.wait_ge(ev("ones_ready"), 1)
            square_root_ahead(0)
            squares("pre_mix", [hT[:, c, :] for c in range(DC)], T)
            for k in range(NB - 1):
                high1(k)
            highs("pre_mix", [xh1[:, c, :] for c in range(DC)], T)
            for k, dst in enumerate((cq[:, 0, :], cq[:, 1, :], ckv, kpe)):
                high1(k + 3)
                take1(k, dst)
            act.wait_ge(ev("unit_taken_by_scalar"), 3)
            squares("ckv", [ckv], T)
            for k in range(4):
                high1(k + 7)
                take1(FIRST1["gc0"] + k, u[:, k, :])
            highs("ckv", [KH[:, 0:T]], T, (ev("k_padded"), 2))
            squares("cq", [cq[:, c, META:T] for c in range(2)], S)
            highs("cq", [HH[:, c, :] for c in range(2)], S)
            for k in range(8):
                high1(k + 11)
                if k in (3, 6):
                    j = k // 6
                    act.wait_ge(ev("angle_reduced"), j + 1)
                    s.activation((sin_t, cos_t)[j][NOPE:QD, :], (ang_k, ang)[j][NOPE:QD, :], ACT.Sin)\
                        .then_inc(ev("rope_table"), 1)
            u0 = FIRST1["uq"]
            for k in range(HEADS):
                high1(u0 + 3 + k)
                if k == 0:
                    act.wait_ge(ev("unit_taken_by_vector"), 8)
                    squares("conv", [yc[:, c, :] for c in range(4)], S)
                    highs("conv", [xh2[:, 4 + c, :] for c in range(4)], S, (ev("unit_used"), FIRST1["gb0"] + 4))
                take1(u0 + k, qcat[0:QD, k, :], rows=QD, n=S)
            for h in range(HEADS):
                act.wait_ge(ev("nope_keys"), h + 1)
                if h == 0:
                    act.wait_ge(ev("rope_table"), 2)
                s.activation(kcat[0:NOPE, h, :], ps[0:NOPE, h % 4, 0:T], ACT.Copy)\
                    .then_inc(ev("nope_keys_taken"), 1)
            high1(u0 + 8 + 3)
            def exps(n):
                keys = META + (n % TT + 1) * P
                b = n % 2
                act.wait_ge(ev("neg_max"), n + 1)
                if n >= 2:
                    act.wait_ge(ev("prob_turned"), n - 1)
                s.activation(prob[:, b, 0:keys], ps[:, 4 + b, 0:keys], ACT.Exp, scale=SCALE1,
                             bias=small[:, 6 + b:7 + b], accum_out=small[:, 8 + b:9 + b]).then_inc(ev("exp_done"), 1)

            exps(0)
            for n in range(HEADS * TT):
                if n + 1 < HEADS * TT:
                    exps(n + 1)
                act.wait_ge(ev("prob_turned"), n + 1)
                if n >= 2:
                    act.wait_ge(ev("att_out"), n - 1)
                full = n % TT + 1
                b = n % 2
                s.activation(probT(b)[:, 0:full, :], ps[:, 6 + b, 0:full * P].rearrange("p (k t) -> p k t", k=full),
                             ACT.Copy)
                s.activation(probT(b)[0:META, 2, :], ps[0:META, 6 + b, 3 * P:4 * P], ACT.Copy)\
                    .then_inc(ev("probT_ready"), 1)
            act.wait_ge(ev("att_out"), HEADS * TT)
            act.wait_ge(ev("unit_taken_by_vector"), 8)
            act.wait_ge(ev("split_low"), SP_AT["attn"])
            square_root_ahead(3)
            for c in range(4):
                s.activation(aT[:, c, :], ps[:, c, 0:S], ACT.Copy).then_inc(ev("aT_ready"), 1)
            act.wait_ge(ev("aT_ready"), 4)
            squares("attn", [aT[:, c, :] for c in range(4)], S)
            highs("attn", [xh2[:, c, :] for c in range(4)], S)
            for k in range(8):
                uu = FIRST1["out0"] + k
                high1(uu + 3)
                take1(uu, mixT[:, k, :], n=S)
                act.wait_ge(ev("unit_taken_by_scalar"), taken1(uu)[1])
                square("post_mix", k, mixT[:, k, :], S)
            root_of_mean("post_mix", S)
            squares("pre_ffn", [hx[:, c, :] for c in range(DC)], S, "h_mixed")
            highs("ffn", [xh2[:, c, :] for c in range(DC)], S)
            u0 = FIRST1["shg"]
            for k in range(2):
                high1(u0 + 3 + k)
                take1(u0 + k, sact[:, k, :], func=ACT.Silu, n=S)
            high1(u0 + 5)
            act.wait_ge(ev("group_centred"), 1)
            s.activation(r_ge, r_g4, ACT.Exp).then_inc(ev("group_exp"), 1)
            act.wait_ge(ev("pair_diff"), 1)
            s.activation(r_s(5), r_s(4), ACT.Exp).then_inc(ev("pair_exp"), 1)
            highs("shared", [HH[:, c, :] for c in range(2)], S)
            for k in range(TT):
                act.wait_ge(ev("t_turned"), k + 1)
                s.activation(th[:, k, :].rearrange("p (b n) -> p b n", b=2), ps[:, 4:6, :], ACT.Copy)\
                    .then_inc(ev("th_ready"), 1)
            act.wait_ge(ev("unit_used"), U1)
            for k in range(2):
                s.activation(shT[:, 4 * k:4 * k + 4, :], ps[:, 2 * k:2 * k + 2, :].rearrange("p b (c t) -> p (b c) t", c=2),
                             ACT.Copy).then_inc(ev("shT_ready"), 1)

            def gathered(b, done):
                s.activation(xg[:, b, 0:4, :], ps[:, 0, :].rearrange("p (c s) -> p c s", c=4), ACT.Copy)\
                    .then_inc(done, 1)

            act.wait_ge(ev("first_half_gathered"), 1)
            gathered(0, ev("xg_by_scalar"))
            with act.Fori(0, TURNS) as i:
                for h in range(2):
                    act.wait_ge(ev("expert_slab_used"), i * RING + (6 * h + 2))
                    s.activation(gact, ps[:, 2, 0:FF], ACT.Silu).then_inc(ev("silu_done"), 1)
                    act.wait_ge(ev("first_half_gathered"), i * 2 + (h + 2))
                    gathered((h + 1) % 2, ev("xg_by_scalar"))
                    act.wait_ge(ev("expert_slab_used"), i * RING + (6 * h + 6))
                    act.wait_ge(ev("row_buffer_free"), i * 2 + (h + 1))
                    s.activation(yrow[:, h, 0:512], ps[:, 4 + 2 * h, :], ACT.Copy)\
                        .then_inc(ev("rows_by_scalar"), 1)
            act.wait_ge(ev("overflow_known"), 1)
            more = act.value_load(overflow[0:1, 0:1], min_val=0, max_val=1)
            with act.If(more > 0):
                with act.Fori(0, RANKS // CAP - 1) as r:
                    with act.Fori(0, EXPERTS) as e:
                        b = r * EXPERTS + e
                        act.wait_ge(ev("o_gate_up"), b + 1)
                        s.activation(gact[0:CAP, :], ps[0:CAP, 2, 0:FF], ACT.Silu).then_inc(ev("o_silu"), 1)
                        act.wait_ge(ev("o_down"), b + 1)
                        s.activation(yrow[0:CAP, 0, 0:512], ps[0:CAP, 4, :], ACT.Copy).then_inc(ev("o_rows"), 1)

            for v in range(NB - 1):
                high2(v)
            act.wait_ge(ev("lambda_abs"), 1)
            s.activation(small_lru[:, 2 * DC:3 * DC], small_lru[:, DC:2 * DC], ACT.Exp).then_inc(ev("lambda_exp"), 1)
            square_root_ahead(1)
            squares("post_ffn", [shT[:, c, :] for c in range(DC)], S, "ffn_ready")
            squares("mix2", [hx[:, c, :] for c in range(DC)], S, "h_ffn")
            highs("mix2", [xh2[:, c, :] for c in range(DC)], S)
            half_of = lambda t, b: t[:, 4 * b:4 * b + 4, :]
            for k in range(48):
                high2(k + 3)
                act.wait_ge(ev("unit_used"), U1 + k + 1)
                s.activation(z(k // DC)[:, k % DC, :], ps[:, k % 4, 0:S], ACT.Copy)\
                    .then_inc(ev("unit_taken_by_scalar"), 1)
                if k in (16, 17, 20, 21):
                    for c in range(*{16: (0, 2), 17: (2, 4), 20: (4, 6), 21: (6, 8)}[k]):
                        act.wait_ge(ev("gates_done"), c + 1)
                        s.activation(zx[:, c, :], ps[:, 4 + c % 4, 0:S], ACT.Sigmoid, bias=g2("b_rgate_2", c))
                        s.activation(zi[:, c, :], ps[:, 4 + c % 4, 256:512], ACT.Sigmoid, bias=g2("b_igate_2", c))\
                            .then_inc(ev("gate_act"), 1)
                if k in (27, 28):
                    if k == 27:
                        act.wait_ge(ev("gated_input"), 4)
                    s.activation(half_of(zc, k - 27), half_of(zx, k - 27), ACT.Tanh).then_inc(ev("tanh_done"), 1)
                if k in (29, 30):
                    act.wait_ge(ev("tanh_done"), k - 28)
                    s.activation(half_of(zx, k - 29), half_of(zx, k - 29), ACT.Exp).then_inc(ev("a_ready"), 1)
                if k in (31, 32):
                    if k == 31:
                        act.wait_ge(ev("unit_taken_by_scalar"), TAKEN_S1 + 16)
                    s.activation(half_of(zg, k - 31), half_of(zg, k - 31), ACT.Gelu_apprx_tanh)\
                        .then_inc(ev("gelu_done"), 1)
                if k in (38, 39):
                    act.wait_ge(ev("one_minus_a2"), 4 * (k - 37))
                    s.activation(half_of(zc, k - 38), half_of(zc, k - 38), ACT.Sqrt).then_inc(ev("mult_ready"), 1)
            act.wait_ge(ev("unit_taken_by_scalar"), TAKEN_S1 + 48)
            act.wait_ge(ev("v_turned"), 1)
            act.wait_ge(ev("lru_done"), 4)
            s.activation(vtok2[:, 0, :].rearrange("p (b n) -> p b n", b=2), ps[:, 4:6, :], ACT.Copy)\
                .then_inc(ev("v_ready"), 1)
            def sigmoids(n):
                keys = (n % TT + 1) * P
                b = n % 2
                if n >= 2:
                    act.wait_ge(ev("att_ready"), n - 1)
                act.wait_ge(ev("z_masked"), n + 1)
                zz = ps[:, 2 * b:2 * b + 2, 0:keys]
                beta = att_buf(b).rearrange("p (h k) -> p h k", h=2)[:, :, 0:keys]
                omb = att_buf(2 + b).rearrange("p (h k) -> p h k", h=2)[:, :, 0:keys]
                s.activation(omb, zz, ACT.Sigmoid, scale=-SCALE2).then_inc(ev("sigm_done"), 1)
                s.activation(beta, zz, ACT.Sigmoid, scale=SCALE2).then_inc(ev("sigm_done"), 1)

            sigmoids(0)
            for n in range(HEADS2):
                if n + 1 < HEADS2:
                    sigmoids(n + 1)
                keys = (n % TT + 1) * P
                act.wait_ge(ev("att_turned"), n + 1)
                if n >= 2:
                    act.wait_ge(ev("y_att"), n - 1)
                s.activation(attT(n % 2)[:, 0:2 * keys], ps[:, (4, 7)[n % 2], 0:2 * keys], ACT.Copy)\
                    .then_inc(ev("attT_ready"), 1)

            s.activation(zl, zl, ACT.Sigmoid).then_inc(ev("g_lru_ready"), 1)

            def take2(v, dst, func=ACT.Copy):
                act.wait_ge(ev("unit_used"), U1 + v + 1)
                s.activation(dst, ps[:, v % 4, 0:S], func).then_inc(ev("unit_taken_by_scalar"), 1)

            for k in range(8):
                high2(U_GATT + 3 + k)
                take2(U_GATT + k, zq[:, k, :], ACT.Sigmoid)
            highs_in_place("y_lru", [zg[:, c, :] for c in range(DC)], [xh2[:, c, :] for c in range(DC)],
                           (ev("unit_used"), U1 + U_BRL))
            for k in range(8):
                high2(U_BRL + 3 + k)
            act.wait_ge(ev("y_att_taken"), DC)
            highs_in_place("y_att", [zk[:, c, :] for c in range(DC)], [xh2[:, c, :] for c in range(DC)],
                           (ev("unit_used"), U1 + U_BRA))
            for k in range(8):
                high2(U_BRA + 3 + k)
            act.wait_ge(ev("merged"), DC)
            highs_in_place("merged2", [zl[:, c, :] for c in range(DC)], [xh2[:, c, :] for c in range(DC)],
                           (ev("unit_used"), U1 + U_OUT))
            square_root_ahead(2)
            for k in range(8):
                high2(U_OUT + 3 + k)
                if k:
                    act.wait_ge(ev("h_mixed2"), k)
                    square("mlp2", k - 1, hx[:, k - 1, :], S)
            act.wait_ge(ev("h_mixed2"), DC)
            square("mlp2", DC - 1, hx[:, DC - 1, :], S)
            root_of_mean("mlp2", S)
            highs("mlp2", [xh2[:, c, :] for c in range(DC)], S)
            with act.Fori(0, 4) as i:
                for v in range(16):
                    high2(U_MLP + v + 3, i)
                    if v % 4 < 2:
                        f = (v // 4) * 2 + v % 4
                        act.wait_ge(ev("relu_done"), i * 8 + (f + 1))
                        act.wait_ge(ev("unit_used"), i * 16 + (U1 + U_MLP + v - 1))
                        s.activation(HH[:, f % 2, :], zx[:, f % 2, :], ACT.Copy).then_inc(ev("relu_high"), 1)
            highs("p2", [HH[:, c, :] for c in range(2)], S, (ev("unit_used"), U1 + U_PLE))
            squares("ple2", [hx[:, c, :] for c in range(DC)], S, "h_mlp")
            highs("ple2", [xh2[:, c, :] for c in range(DC)], S)

            def result_chunk(c):
                act.wait_ge(ev("h_ple"), c + 1)
                s.activation(zg[:, c, :], hx[:, c, :], ACT.Copy, scale=g2("norm_final_g_2", c))\
                    .then_inc(ev("result"), 1)
                square("final2", c, hx[:, c, :], S)

            for k in range(10):
                v = U_PLE + k
                high2(v + 3)
                if k >= 8:
                    result_chunk(k - 8)
                if SLABS2[UNITS2[v][0]][0] == "col":
                    g = k if k < 2 else k - 2
                    take2(v, zq[:, g, :], ACT.Sigmoid)
            square_root_ahead(4)
            for c in range(2, DC):
                result_chunk(c)
            act.wait_ge(ev("squares_summed"), SQ_AT["final2"] + DC)
            s.activation(small[:, 0:TT], ps[:, 4, 0:TT], ACT.Sqrt, scale=1.0 / D, bias=EPS)\
                .then_inc(ev("std_ready"), 1)
            act.wait_ge(ev("rstd_ready"), NORM_NO["final2"] + 1)
            act.wait_ge(ev("result_turned"), DC)
            for k in range(TT):
                s.activation(out_tok(k)[:, 0:512], ps[:, 2 * k, :], ACT.Copy, scale=small[:, TT + k:TT + k + 1])\
                    .then_inc(ev("out_tokens_by_scalar"), 1)

        @block.vector
        def _(dve):
            v = nc.vector
            steps = [0]

            def chain(ins):
                steps[0] += 1
                ins.then_inc(ev("vector_step"), 1)
                dve.wait_ge(ev("vector_step"), steps[0])

            def low1(u_no):
                if u_no >= U1:
                    return
                dve.wait_ge(ev("unit_high"), u_no + 1)
                src, h = pack1(u_no, WH[:, u_no % NB, :])
                _, dst = pack1(u_no, WL[:, u_no % NB, :])
                v.tensor_tensor(dst, src, h.bitcast(F32), ALU.subtract).then_inc(ev("unit_split"), 1)

            def low2(k, turn=None):
                if k >= U2:
                    return
                base = 0 if turn is None else turn * 16
                dve.wait_ge(ev("unit_high"), base + (U1 + k + 1))
                src, h = pack2(k, WH[:, k % NB, :])
                _, dst = pack2(k, WL[:, k % NB, :])
                v.tensor_tensor(dst, src, h.bitcast(F32), ALU.subtract).then_inc(ev("unit_split"), 1)

            def root(name, n):
                no = NORM_NO[name]
                dve.wait_ge(ev("std_ready"), no + 1)
                v.reciprocal(rstd[:, 0:n], std[:, 0:n]).then_inc(ev("rstd_ready"), 1)
                dve.wait_ge(ev("rstd_ready"), no + 1)

            def split(name, make, lows, n, highs_):
                k0 = SP_AT[name]

                def low(c):
                    k = k0 + c
                    dve.wait_ge(ev("split_high"), k + 1)
                    v.tensor_tensor(lows[c], XT[:, k % 2, 0:n], highs_[c].bitcast(F32), ALU.subtract)\
                        .then_inc(ev("split_low"), 1)

                for c in range(NSP[name]):
                    k = k0 + c
                    if c >= 2:
                        dve.wait_ge(ev("split_low"), k - 1)
                    make(c, XT[:, k % 2, 0:n]).then_inc(ev("split_value"), 1)
                    if c:
                        low(c - 1)
                low(NSP[name] - 1)

            def lows_in_place(name, src):
                for c in range(DC):
                    dve.wait_ge(ev("split_high"), SP_AT[name] + c + 1)
                    v.tensor_tensor(xl2[:, c, :], src[:, c, :], xh2[:, c, :].bitcast(F32), ALU.subtract)\
                        .then_inc(ev("split_low"), 1)

            def scaled(srcs, gains, n):
                return lambda c, dst: v.scalar_tensor_tensor(out=dst, in0=srcs[c], scalar=gains[c], in1=rstd[:, 0:n],
                                                             op0=ALU.mult, op1=ALU.mult)

            ch = lambda t, a=0, b=DC: [t[:, c, :] for c in range(a, b)]

            v.memset(KH[:, T:].bitcast(F32), 0.0).then_inc(ev("k_padded"), 1)
            v.memset(KL[:, T:].bitcast(F32), 0.0).then_inc(ev("k_padded"), 1)
            for c in range(1, DC, 2):
                dve.wait_ge(ev("x_turned"), c + 1)
                v.tensor_copy(hT[:, c, :], ps[:, c % 4, 0:T]).then_inc(ev("hT_by_vector"), 1)
            dve.wait_ge(ev("pos_loaded"), 16)
            v.tensor_scalar(pos_row[0:1, META:T], pos_int[0:1, :], float(META), None, ALU.add)\
                .then_inc(ev("pos_ready"), 1)
            dve.wait_ge(ev("vrows_turned"), 1)
            v.tensor_copy(vec1[:], ps[:, 6, 0:NV1]).then_inc(ev("vecs_ready"), 1)
            dve.wait_ge(ev("vecs_ready"), 1)
            root("pre_mix", T)
            low1(0)
            split("pre_mix", scaled(ch(hT), [g1("pre_mix_norm", c) for c in range(DC)], T), ch(xl1), T, ch(xh1))
            low1(1)
            low1(2)
            for k in range(4):
                low1(k + 3)
            for k in range(4):
                low1(k + 7)
            dve.wait_ge(ev("vrows_turned"), 2)
            v.tensor_copy(vec2[:], ps[:, 6, 0:NV2]).then_inc(ev("vecs_ready"), 1)
            dve.wait_ge(ev("vecs_ready"), 2)
            root("ckv", T)
            split("ckv", scaled([ckv], [g1("kv_norm")], T), [KL[:, 0:T]], T, [KH[:, 0:T]])
            root("cq", S)
            split("cq", scaled([cq[:, c, META:T] for c in range(2)], [g1("q_norm", c) for c in range(2)], S),
                  ch(HL, 0, 2), S, ch(HH, 0, 2))
            two_pi = 2 * math.pi
            p1 = 6.28125
            p2 = float(np.float32(np.round((two_pi - p1) * 2 ** 20) / 2 ** 20))
            p3 = two_pi - p1 - p2
            magic = 1.5 * 2 ** 23
            lim = 3.1415925
            rows = slice(NOPE, QD)
            angp = ps[rows, 5, 0:T]

            def reduce_angle(k):
                dst = (ang_k, ang)[k]
                turn = 0.25 * k
                tmp = rstd[rows, 0:T]
                chain(v.tensor_scalar(tmp, angp, 1 / two_pi, turn, ALU.mult, ALU.add))
                chain(v.tensor_scalar(tmp, tmp, magic, None, ALU.add))
                chain(v.tensor_scalar(tmp, tmp, -magic, None, ALU.add))
                chain(v.scalar_tensor_tensor(out=dst[rows, :], in0=tmp, scalar=-p1, in1=angp, op0=ALU.mult, op1=ALU.add))
                for part in (p2, p3):
                    chain(v.scalar_tensor_tensor(out=dst[rows, :], in0=tmp, scalar=-part, in1=dst[rows, :],
                                                 op0=ALU.mult, op1=ALU.add))
                chain(v.tensor_scalar(dst[rows, :], dst[rows, :], turn * two_pi, lim, ALU.add, ALU.min))
                v.tensor_scalar(dst[rows, :], dst[rows, :], -lim, None, ALU.max).then_inc(ev("angle_reduced"), 1)
            for k in range(8):
                low1(k + 11)
                if k in (1, 4):
                    dve.wait_ge(ev("angles"), 1)
                    reduce_angle(k // 4)
                un = FIRST1["xin0"] + k
                dve.wait_ge(ev("unit_used"), un + 1)
                if k < 4:
                    dve.wait_ge(ev("unit_taken_by_scalar"), taken1(FIRST1["gc0"] + k)[1])
                    v.tensor_tensor(u[:, k, :], ps[:, un % 4, 0:T], u[:, k, :], ALU.mult)\
                        .then_inc(ev("unit_taken_by_vector"), 1)
                    dve.wait_ge(ev("unit_taken_by_vector"), k + 1)
                    w = lambda tap: g1("conv_w", 4 * tap + k)
                    chain(v.tensor_scalar(yc[:, k, :], u[:, k, META:T], w(2), None, ALU.mult))
                    for back in (1, 2):
                        chain(v.scalar_tensor_tensor(out=yc[:, k, :], in0=u[:, k, META - back:T - back],
                                                     scalar=w(2 - back), in1=yc[:, k, :], op0=ALU.mult, op1=ALU.add))
                else:
                    v.tensor_tensor(yc[:, k - 4, :], ps[:, un % 4, META:T], yc[:, k - 4, :], ALU.mult)\
                        .then_inc(ev("unit_taken_by_vector"), 1)
            dve.wait_ge(ev("kpe_swapped"), 1)
            dve.wait_ge(ev("rope_table"), 2)
            chain(v.tensor_tensor(rope_a[rows, 0:T], ps[rows, 5, 0:T], sin_t[rows, :], ALU.mult))
            chain(v.tensor_tensor(kpe[rows, :], kpe[rows, :], cos_t[rows, :], ALU.mult))
            v.tensor_tensor(kcat[rows, :, :], kpe[rows, :].unsqueeze(1).to_broadcast([ROPE, HEADS, T]),
                            rope_a[rows, 0:T].unsqueeze(1).to_broadcast([ROPE, HEADS, T]), ALU.add)\
                .then_inc(ev("rope_keys"), 1)
            u0 = FIRST1["uq"]
            low1(u0 + 3)
            root("conv", S)
            split("conv", scaled(ch(yc, 0, 4), [g1("conv_out_norm", c) for c in range(4)], S), ch(xl2, 4, 8), S,
                  ch(xh2, 4, 8))
            for k in range(1, HEADS):
                low1(u0 + 3 + k)
            dve.wait_ge(ev("rope_keys"), 1)
            for j in range(HEADS // 2):
                if j:
                    dve.wait_ge(ev("q_roped"), j)
                dve.wait_ge(ev("q_swapped"), j + 1)
                qq = qcat[rows, 2 * j:2 * j + 2, :]
                both = lambda t: t[rows, META:T].unsqueeze(1).to_broadcast([ROPE, 2, S])
                tmp = rope_a[rows, :].rearrange("p (h t) -> p h t", h=2)
                sw = ps[rows, 4 + j % 2, :].rearrange("p (h t) -> p h t", h=2)
                chain(v.tensor_tensor(tmp, sw, both(sin_t), ALU.mult))
                chain(v.tensor_tensor(qq, qq, both(cos_t), ALU.mult))
                v.tensor_tensor(qq, qq, tmp, ALU.add).then_inc(ev("q_roped"), 1)
            dve.wait_ge(ev("q_roped"), 4)
            for k in range(3):
                dve.wait_ge(*((ev("values"), k + 1) if k < 2 else (ev("unit_used"), FIRST1["ukv"] + 1)))
                v.tensor_copy(vtok[:, k, :], ps[:, 4 + k, :]).then_inc(ev("values_ready"), 1)
            low1(u0 + 8 + 3)
            def negative_max(n):
                keys = META + (n % TT + 1) * P
                b = n % 2
                sc = ps[:, 4 + b, 0:keys]
                dia = ps[:, 4 + b, keys - P:keys]
                dve.wait_ge(ev("scores"), n + 1)
                if n == 0:
                    dve.wait_ge(ev("masks_ready"), 2)
                if n >= 2:
                    dve.wait_ge(ev("exp_done"), n - 1)
                chain(v.tensor_tensor(dia, dia, causal[:], ALU.add))
                chain(v.tensor_reduce(small[:, 4 + b:5 + b], sc, AX.X, ALU.max))
                v.tensor_scalar(small[:, 6 + b:7 + b], small[:, 4 + b:5 + b], -SCALE1, None, ALU.mult)\
                    .then_inc(ev("neg_max"), 1)

            negative_max(0)
            for n in range(HEADS * TT):
                keys = META + (n % TT + 1) * P
                b = n % 2
                if n + 1 < HEADS * TT:
                    negative_max(n + 1)
                dve.wait_ge(ev("exp_done"), n + 1)
                chain(v.reciprocal(small[:, 10 + b:11 + b], small[:, 8 + b:9 + b]))
                v.tensor_scalar(prob[:, b, 0:keys], prob[:, b, 0:keys], small[:, 10 + b:11 + b], None, ALU.mult)\
                    .then_inc(ev("prob_ready"), 1)
            root("attn", S)
            split("attn", scaled(ch(aT, 0, 4), [g1("attn_out_norm", c) for c in range(4)], S), ch(xl2, 0, 4), S,
                  ch(xh2, 0, 4))
            for k in range(8):
                low1(FIRST1["out0"] + k + 3)
            root("post_mix", S)
            for c in range(DC):
                chain(v.scalar_tensor_tensor(out=mixT[:, c, :], in0=mixT[:, c, :], scalar=g1("post_mix_norm", c),
                                             in1=rstd[:, 0:S], op0=ALU.mult, op1=ALU.mult))
                v.tensor_tensor(hx[:, c, :], hx[:, c, :], mixT[:, c, :], ALU.add).then_inc(ev("h_mixed"), 1)
            root("pre_ffn", S)
            k0 = SP_AT["ffn"]

            def make_t(c, dst):
                chain(v.scalar_tensor_tensor(out=tT[:, c, :], in0=hx[:, c, :], scalar=g1("pre_ffn_norm", c),
                                             in1=rstd[:, 0:S], op0=ALU.mult, op1=ALU.mult))
                return v.tensor_copy(dst, tT[:, c, :])

            split("ffn", make_t, ch(xl2), S, ch(xh2))
            u0 = FIRST1["shg"]
            low1(u0 + 3)

            def make_hidden(c, dst):
                dve.wait_ge(*taken1(u0 + c))
                dve.wait_ge(ev("unit_used"), u0 + 2 + c + 1)
                return v.tensor_tensor(dst, ps[:, (u0 + 2 + c) % 4, 0:S], sact[:, c, :], ALU.mult)

            dve.wait_ge(ev("logits"), 1)
            dve.wait_ge(ev("routing_consts"), 4)
            chain(v.tensor_copy(logit, ps[:, 6, 0:2 * 36].rearrange("p (t n) -> p t n", t=TT)))
            bc = lambda x, n: x.unsqueeze(2).to_broadcast([P, TT, n])
            io = lambda n: iota_e[:, 0:n].unsqueeze(1).to_broadcast([P, TT, n])

            def first_max(x, n, m, key, onehot, lowest):
                chain(v.tensor_reduce(m, x, AX.X, ALU.max))
                chain(v.tensor_tensor(key, x, bc(m, n), ALU.is_equal))
                chain(v.scalar_tensor_tensor(out=key, in0=key, scalar=-1000.0, in1=io(n), op0=ALU.mult, op1=ALU.add))
                chain(v.tensor_reduce(lowest, key, AX.X, ALU.min))
                chain(v.tensor_tensor(onehot, key, bc(lowest, n), ALU.is_equal))

            first_max(glog, GROUPS, r_s(0), r_g4k, r_ohg, r_s(1))
            v.tensor_tensor(r_g4, glog, bc(r_s(0), GROUPS), ALU.subtract).then_inc(ev("group_centred"), 1)
            by_group = lambda x: x.rearrange("p t (g e) -> p t g e", g=GROUPS)
            gb = lambda x: x.unsqueeze(3).to_broadcast([P, TT, GROUPS, EPG])
            for t in range(TT):
                chain(v.tensor_tensor(by_group(r_em)[:, t], by_group(elog)[:, t], gb(r_ohg)[:, t], ALU.mult))
            chain(v.tensor_scalar(r_g4k, r_ohg, 1e30, -1e30, ALU.mult, ALU.add))
            for t in range(TT):
                chain(v.tensor_tensor(by_group(r_em)[:, t], by_group(r_em)[:, t], gb(r_g4k)[:, t], ALU.add))
            first_max(r_em, EXPERTS, r_s(2), r_key, r_oh1, r_s(1))
            chain(v.scalar_tensor_tensor(out=r_em, in0=r_oh1, scalar=-3e30, in1=r_em, op0=ALU.mult, op1=ALU.add))
            first_max(r_em, EXPERTS, r_s(3), r_key, r_oh2, r_s(1))
            v.tensor_tensor(r_s(4), r_s(3), r_s(2), ALU.subtract).then_inc(ev("pair_diff"), 1)
            v.tensor_tensor(r_m, r_oh1, r_oh2, ALU.add).then_inc(ev("chosen_ready"), 1)
            low1(u0 + 4)
            low1(u0 + 5)
            split("shared", make_hidden, ch(HL, 0, 2), S, ch(HH, 0, 2))
            dve.wait_ge(ev("group_exp"), 1)
            chain(v.tensor_reduce(r_s(6), r_ge, AX.X, ALU.add))
            dve.wait_ge(ev("pair_exp"), 1)
            chain(v.scalar_tensor_tensor(out=r_s(6), in0=r_s(5), scalar=1.0, in1=r_s(6), op0=ALU.add, op1=ALU.mult))
            chain(v.reciprocal(w_k(0), r_s(6)))
            chain(v.tensor_tensor(w_k(1), w_k(0), r_s(5), ALU.mult))
            dve.wait_ge(ev("ranks"), 1)
            rk = ps[:, 6, P:P + 2 * EXPERTS].rearrange("p (t n) -> p t n", t=TT)
            chain(v.scalar_tensor_tensor(out=rank_or[:, :, 0:EXPERTS], in0=rk, scalar=1.0, in1=r_m,
                                         op0=ALU.add, op1=ALU.mult))
            chain(v.tensor_scalar(rank_or[:, :, 0:EXPERTS], rank_or[:, :, 0:EXPERTS], -1.0, None, ALU.add))

            def select(b, first, width, done):
                for t in range(TT):
                    r = rank_or[:, t, bass.ds(first, width)].unsqueeze(2).to_broadcast([P, width, CAP])
                    i_ = iota_slot[:].unsqueeze(1).to_broadcast([P, width, CAP])
                    ins = v.tensor_tensor(sel[:, b, t, 0:width * CAP].rearrange("p (e s) -> p e s", e=width),
                                          r, i_, ALU.is_equal)
                ins.then_inc(done, 1)

            select(0, 0, 2, ev("sel_ready"))
            for k in range(TT):
                dve.wait_ge(ev("th_ready"), k + 1)
                v.tensor_tensor(tl[:, k, :].rearrange("p (b n) -> p b n", b=2), ps[:, 4:6, :],
                                th[:, k, :].rearrange("p (b n) -> p b n", b=2).bitcast(F32), ALU.subtract)\
                    .then_inc(ev("t_ready"), 1)
            for k, oh in enumerate((r_oh1, r_oh2)):
                chain(v.tensor_tensor(r_key, oh, rk, ALU.mult))
                chain(v.tensor_reduce(r_s(6), r_key, AX.X, ALU.add))
                chain(v.tensor_tensor(r_key, oh, io(EXPERTS), ALU.mult))
                chain(v.tensor_reduce(r_s(7), r_key, AX.X, ALU.add))
                chain(v.tensor_scalar(behind(k), r_s(6), CAP - 0.5, None, ALU.is_gt))
                chain(v.tensor_scalar(before_cap(k), behind(k), -1.0, 1.0, ALU.mult, ALU.add))
                chain(v.tensor_scalar(r_s(8), r_s(6), CAP - 1.0, None, ALU.min))
                chain(v.scalar_tensor_tensor(out=r_s(8), in0=r_s(7), scalar=float(CAP), in1=r_s(8),
                                             op0=ALU.mult, op1=ALU.add))
                chain(v.tensor_copy(slot_i[:, 2 * k:2 * k + 2], r_s(8)))
                chain(v.tensor_scalar(r_s(8), r_s(6), -float(CAP), 0.0, ALU.add, ALU.max))
                chain(v.scalar_tensor_tensor(out=r_s(8), in0=r_s(7), scalar=float(RANKS - CAP), in1=r_s(8),
                                             op0=ALU.mult, op1=ALU.add))
                chain(v.tensor_copy(slot_i[:, 2 * TT + 2 * k:2 * TT + 2 * k + 2], r_s(8)))
            chain(v.tensor_reduce(r_s(8)[0:1, 0:1], ps[0:1, 6, P + 2 * EXPERTS:P + 3 * EXPERTS], AX.X, ALU.max))
            chain(v.tensor_scalar(r_s(8)[0:1, 0:1], r_s(8)[0:1, 0:1], CAP + 0.5, None, ALU.is_gt))
            v.tensor_copy(overflow[:], r_s(8)[0:1, 0:1]).then_inc(ev("overflow_known"), 1)

            def gathered(b, done):
                v.tensor_copy(xg[:, b, 4:8, :], ps[:, 1, :].rearrange("p (c s) -> p c s", c=4)).then_inc(done, 1)

            dve.wait_ge(ev("second_half_gathered"), 1)
            gathered(0, ev("xg_by_vector"))
            with dve.Fori(0, TURNS) as i:
                for h in range(2):
                    select((h + 1) % 2, i * GROUP + 2 * (h + 1), 2, ev("sel_ready"))
                    dve.wait_ge(ev("expert_slab_used"), i * RING + (6 * h + 4))
                    dve.wait_ge(ev("silu_done"), i * 2 + (h + 1))
                    v.tensor_tensor(hid, gact, ps[:, 3, 0:FF], ALU.mult).then_inc(ev("hidden_ready"), 1)
                    dve.wait_ge(ev("hidden_turned"), i * 2 + (h + 1))
                    v.tensor_copy(hidT, ps[:, 2, FF:2 * FF].rearrange("p (f s) -> p f s", f=2))\
                        .then_inc(ev("hidT_ready"), 1)
                    dve.wait_ge(ev("second_half_gathered"), i * 2 + (h + 2))
                    gathered((h + 1) % 2, ev("xg_by_vector"))
                    dve.wait_ge(ev("expert_slab_used"), i * RING + (6 * h + 6))
                    dve.wait_ge(ev("row_buffer_free"), i * 2 + (h + 1))
                    v.tensor_copy(yrow[:, h, 512:D], ps[:, 5 + 2 * h, :]).then_inc(ev("rows_by_vector"), 1)

            dve.wait_ge(ev("overflow_known"), 1)
            more = dve.value_load(overflow[0:1, 0:1], min_val=0, max_val=1)
            with dve.If(more > 0):
                with dve.Fori(0, RANKS // CAP - 1) as r:
                    for t in range(TT):
                        v.tensor_scalar(rank_or[:, t, :], rank_or[:, t, :], -float(CAP), None, ALU.add)\
                            .then_inc(ev("o_ranks"), 1)
                    with dve.Fori(0, EXPERTS) as e:
                        b = r * EXPERTS + e
                        dve.wait_ge(ev("o_ranks"), r * TT + TT)
                        select(0, e, 1, ev("o_sel"))
                        dve.wait_ge(ev("o_gathered"), b + 1)
                        v.tensor_copy(xg[:, 0, :, 0:CAP], ps[:, 0, :].rearrange("p (c s) -> p c s", c=DC))\
                            .then_inc(ev("o_xg"), 1)
                        dve.wait_ge(ev("o_silu"), b + 1)
                        v.tensor_tensor(hid[0:CAP, :], gact[0:CAP, :], ps[0:CAP, 3, 0:FF], ALU.mult)\
                            .then_inc(ev("o_hidden"), 1)
                        dve.wait_ge(ev("o_turned"), b + 1)
                        v.tensor_copy(hidT, ps[:, 2, FF:2 * FF].rearrange("p (f s) -> p f s", f=2))\
                            .then_inc(ev("o_hidT"), 1)
                        dve.wait_ge(ev("o_down"), b + 1)
                        v.tensor_copy(yrow[0:CAP, 0, 512:D], ps[0:CAP, 5, :]).then_inc(ev("o_rows"), 1)

            for w_no in range(2 * TT):
                v.tensor_scalar(diag(w_no), ident[:], small[:, w_no:w_no + 1], None, ALU.mult)\
                    .then_inc(ev("weights_ready"), 1)
            for k in range(NB - 1):
                low2(k)
            lam = vec2[:, V2["lru_lambda_2"]:V2["lru_lambda_2"] + DC]
            sc = lambda k: small_lru[:, k * DC:(k + 1) * DC]
            chain(v.tensor_scalar(sc(0), lam, -1.0, None, ALU.mult))
            v.tensor_tensor(sc(1), lam, sc(0), ALU.min).then_inc(ev("lambda_abs"), 1)
            dve.wait_ge(ev("lambda_exp"), 1)
            chain(v.tensor_scalar(sc(3), sc(2), 2.0, None, ALU.add))
            chain(v.reciprocal(sc(3), sc(3)))
            chain(v.tensor_tensor(sc(2), sc(2), sc(3), ALU.mult))
            chain(v.tensor_tensor(sc(3), sc(2), sc(2), ALU.mult))
            terms = 9
            chain(v.tensor_scalar(sc(4), sc(3), 0.0, 1.0 / (2 * terms + 1), ALU.mult, ALU.add))
            for k in range(terms - 1, -1, -1):
                chain(v.tensor_tensor(sc(4), sc(4), sc(3), ALU.mult))
                chain(v.tensor_scalar(sc(4), sc(4), 1.0 / (2 * k + 1), None, ALU.add))
            chain(v.scalar_tensor_tensor(out=sc(4), in0=sc(4), scalar=2.0, in1=sc(2), op0=ALU.mult, op1=ALU.mult))
            chain(v.scalar_tensor_tensor(out=sc(4), in0=sc(0), scalar=0.0, in1=sc(4), op0=ALU.max, op1=ALU.add))
            chain(v.tensor_scalar(sc(4), sc(4), -LRU_C, None, ALU.mult))
            with dve.If(more > 0):
                for k in range(2 * TT):
                    dve.wait_ge(ev(f"rows_gathered_{k}"), 16)
                dve.wait_ge(ev("o_rows_gathered"), 16 * 2 * TT)
                for k in range(2 * TT):
                    v.tensor_scalar(gath[:, k, :], gath[:, k, :], small[:, 8 + k:9 + k], None, ALU.mult)\
                        .then_inc(ev("o_masked"), 1)
                    dve.wait_ge(ev("o_masked"), k + 1)
                    v.scalar_tensor_tensor(out=gath[:, k, :], in0=gath_more[:, k, :], scalar=small[:, 4 + k:5 + k],
                                           in1=gath[:, k, :], op0=ALU.mult, op1=ALU.add).then_inc(ev("o_replaced"), 1)
                dve.wait_ge(ev("o_replaced"), 2 * TT)
            dve.wait_ge(ev("shT_ready"), 2)
            for c in range(DC):
                dve.wait_ge(ev("routed_turned"), c + 1)
                v.tensor_tensor(shT[:, c, :], shT[:, c, :], ps[:, c // 2, (c % 2) * S:(c % 2 + 1) * S], ALU.add)\
                    .then_inc(ev("ffn_ready"), 1)
            root("post_ffn", S)
            for c in range(DC):
                chain(v.scalar_tensor_tensor(out=shT[:, c, :], in0=shT[:, c, :], scalar=g1("post_ffn_norm", c),
                                             in1=rstd[:, 0:S], op0=ALU.mult, op1=ALU.mult))
                v.tensor_tensor(hx[:, c, :], hx[:, c, :], shT[:, c, :], ALU.add).then_inc(ev("h_ffn"), 1)
            dve.wait_ge(ev("h_ffn"), DC)
            root("mix2", S)
            split("mix2", scaled(ch(hx), [g2("norm_mix_g_2", c) for c in range(DC)], S), ch(xl2), S, ch(xh2))
            two = lambda t, q: t[:, 2 * q:2 * q + 2, :]

            def gated_output(q):
                dve.wait_ge(ev("scanned"), 2 * q + 2)
                dve.wait_ge(ev("gelu_done"), 1 + q // 2)
                v.tensor_tensor(two(zg, q), two(zg, q), two(zc, q), ALU.mult).then_inc(ev("lru_done"), 1)

            for k in range(48):
                low2(k + 3)
                if 8 <= k < 16:
                    c = k - 8
                    dve.wait_ge(ev("unit_taken_by_scalar"), TAKEN_S1 + c + 1)
                    w = lambda tap: g2("conv_w_2", 8 * tap + c)
                    chain(v.tensor_scalar(zc[:, c, :], zx[:, c, :], w(3), g2("conv_b_2", c), ALU.mult, ALU.add))
                    for back in (1, 2, 3):
                        ins = v.scalar_tensor_tensor(out=zc[:, c, back:], in0=zx[:, c, 0:S - back],
                                                     scalar=w(3 - back), in1=zc[:, c, back:], op0=ALU.mult,
                                                     op1=ALU.add)
                        if back < 3:
                            chain(ins)
                    ins.then_inc(ev("conv_ready"), 1)
                if 22 <= k < 26:
                    q = k - 22
                    dve.wait_ge(ev("gate_act"), 2 * q + 2)
                    dve.wait_ge(ev("conv_ready"), DC)
                    v.tensor_tensor(two(zx, q), two(zx, q),
                                    sc(4)[:, 2 * q:2 * q + 2].unsqueeze(2).to_broadcast([P, 2, S]), ALU.mult)
                    v.tensor_tensor(two(zi, q), two(zi, q), two(zc, q), ALU.mult).then_inc(ev("gated_input"), 1)
                if 29 <= k < 37:
                    c = k - 29
                    dve.wait_ge(ev("tanh_done"), 1 + c // 4)
                    th_, xt = zc[:, c, :], XT[:, 0, 0:S]
                    chain(v.tensor_scalar(xt, th_, -1.0, 1.0, ALU.mult, ALU.add))
                    chain(v.reciprocal(xt, xt))
                    v.scalar_tensor_tensor(out=th_, in0=th_, scalar=-2.0, in1=xt, op0=ALU.mult, op1=ALU.mult)\
                        .then_inc(ev("one_minus_a2"), 1)
                    dve.wait_ge(ev("one_minus_a2"), c + 1)
                if 40 <= k < 44:
                    q = k - 40
                    dve.wait_ge(ev("mult_ready"), 1 + q // 2)
                    dve.wait_ge(ev("gated_input"), 4)
                    v.tensor_tensor(two(zi, q), two(zi, q), two(zc, q), ALU.mult).then_inc(ev("lru_input"), 1)
                if 44 <= k < 48:
                    if k == 44:
                        dve.wait_ge(ev("lru_input"), 4)
                        dve.wait_ge(ev("a_ready"), 2)
                    for c in (2 * (k - 44), 2 * (k - 44) + 1):
                        v.tensor_tensor_scan(out=zc[:, c, :], data0=zx[:, c, :], data1=zi[:, c, :], initial=0.0,
                                             op0=ALU.mult, op1=ALU.add).then_inc(ev("scanned"), 1)
                    if k > 44:
                        gated_output(k - 45)
            gated_output(3)
            dve.wait_ge(ev("lru_done"), 4)
            dve.wait_ge(ev("v_turned"), 2)
            v.tensor_copy(vtok2[:, 1, :].rearrange("p (b n) -> p b n", b=2), ps[:, 6:8, :]).then_inc(ev("v_ready"), 1)
            dve.wait_ge(ev("v_ready"), TT)
            for b in range(2):
                chain(v.memset(cum(b)[:, :, S:S + 1], 1.0))
            def mask(n):
                keys = (n % TT + 1) * P
                dve.wait_ge(ev("z_scores"), n + 1)
                zd = ps[:, 2 * (n % 2):2 * (n % 2) + 2, keys - P:keys]
                v.tensor_tensor(zd, zd, strict[:].unsqueeze(1).to_broadcast([P, 2, P]), ALU.add)\
                    .then_inc(ev("z_masked"), 1)

            mask(0)
            for n in range(HEADS2):
                j, qt = divmod(n, TT)
                keys = (qt + 1) * P
                b = n % 2
                if n + 1 < HEADS2:
                    mask(n + 1)
                beta = att_buf(b).rearrange("p (h k) -> p h k", h=2)[:, :, 0:keys]
                omb = att_buf(2 + b).rearrange("p (h k) -> p h k", h=2)[:, :, 0:keys]
                dve.wait_ge(ev("sigm_done"), 2 * n + 1)
                for h in range(2):
                    ins = v.tensor_tensor_scan(out=cum(b)[:, h, S - keys:S][:, ::-1], data0=omb[:, h, ::-1],
                                               data1=ones[:, 0:1].to_broadcast([P, keys]), initial=1.0,
                                               op0=ALU.mult, op1=ALU.mult)
                    chain(ins)
                dve.wait_ge(ev("sigm_done"), 2 * n + 2)
                if n >= 2:
                    dve.wait_ge(ev("att_turned"), n - 1)
                v.tensor_tensor(att(b)[:, :, 0:keys], beta, cum(b)[:, :, S - keys + 1:S + 1], ALU.mult)\
                    .then_inc(ev("att_ready"), 1)
                if qt == TT - 1 and j:
                    dve.wait_ge(ev("y_att"), 2 * j)
                    v.tensor_copy(zk[:, j - 1, :], ps[:, 5 + (j - 1) % 2, 0:S]).then_inc(ev("y_att_taken"), 1)
            dve.wait_ge(ev("y_att"), HEADS2)
            v.tensor_copy(zk[:, DC - 1, :], ps[:, 5 + (DC - 1) % 2, 0:S]).then_inc(ev("y_att_taken"), 1)
            dve.wait_ge(ev("y_att_taken"), DC)
            for k in range(8):
                low2(U_GATT + 3 + k)
            lows_in_place("y_lru", zg)
            dve.wait_ge(ev("g_lru_ready"), 1)
            for k in range(8):
                low2(U_BRL + 3 + k)
                dve.wait_ge(ev("unit_used"), U1 + U_BRL + k + 1)
                v.tensor_tensor(zl[:, k, :], ps[:, (U_BRL + k) % 4, 0:S], zl[:, k, :], ALU.mult)\
                    .then_inc(ev("unit_taken_by_vector"), 1)
            lows_in_place("y_att", zk)
            dve.wait_ge(ev("unit_taken_by_scalar"), TAKEN_S1 + 56)
            for k in range(8):
                low2(U_BRA + 3 + k)
                dve.wait_ge(ev("unit_used"), U1 + U_BRA + k + 1)
                v.tensor_tensor(zq[:, k, :], ps[:, (U_BRA + k) % 4, 0:S], zq[:, k, :], ALU.mult)\
                    .then_inc(ev("unit_taken_by_vector"), 1)
                dve.wait_ge(ev("unit_taken_by_vector"), TAKEN_V1 + 8 + k + 1)
                v.tensor_tensor(zl[:, k, :], zl[:, k, :], zq[:, k, :], ALU.add).then_inc(ev("merged"), 1)
            lows_in_place("merged2", zl)
            for k in range(8):
                low2(U_OUT + 3 + k)
                dve.wait_ge(ev("unit_used"), U1 + U_OUT + k + 1)
                v.tensor_tensor(hx[:, k, :], hx[:, k, :], ps[:, (U_OUT + k) % 4, 0:S], ALU.add)\
                    .then_inc(ev("h_mixed2"), 1)
            dve.wait_ge(ev("h_mixed2"), DC)
            root("mlp2", S)
            split("mlp2", scaled(ch(hx), [g2("norm_mlp_g_2", c) for c in range(DC)], S), ch(xl2), S, ch(xh2))
            with dve.Fori(0, 4) as i:
                for k in range(16):
                    low2(U_MLP + k + 3, i)
                    if k % 4 < 2:
                        f = (k // 4) * 2 + k % 4
                        dve.wait_ge(ev("unit_used"), i * 16 + (U1 + U_MLP + k + 1))
                        x_ = ps[:, k % 4, 0:S]
                        v.tensor_scalar(zx[:, 2 + f % 2, :], x_, 0.0, None, ALU.max).then_inc(ev("relu"), 1)
                        dve.wait_ge(ev("relu"), i * 8 + (f + 1))
                        v.tensor_tensor(zx[:, f % 2, :], zx[:, 2 + f % 2, :], zx[:, 2 + f % 2, :], ALU.mult)\
                            .then_inc(ev("relu_done"), 1)
                        dve.wait_ge(ev("relu_high"), i * 8 + (f + 1))
                        v.tensor_tensor(HL[:, f % 2, :], zx[:, f % 2, :], HH[:, f % 2, :].bitcast(F32), ALU.subtract)\
                            .then_inc(ev("relu_low"), 1)
            dve.wait_ge(ev("p_turned"), 2)
            split("p2", lambda c, dst: v.tensor_copy(dst, ps[:, 2 + c, 0:S]), ch(HL, 0, 2), S, ch(HH, 0, 2))
            dve.wait_ge(ev("unit_used"), U1 + U_PLE)
            acc = ps[:, 4:8, :].rearrange("p b (c t) -> p (b c) t", c=2)
            for c in range(DC):
                v.tensor_tensor(hx[:, c, :], hx[:, c, :], acc[:, c, :], ALU.add).then_inc(ev("h_mlp"), 1)
            dve.wait_ge(ev("h_mlp"), DC)
            root("ple2", S)
            split("ple2", scaled(ch(hx), [g2("norm_ple_g_2", c) for c in range(DC)], S), ch(xl2), S, ch(xh2))
            for k in range(10):
                low2(U_PLE + 3 + k)
            for k in range(DC):
                dve.wait_ge(ev("unit_taken_by_scalar"), TAKEN_S1 + 57 + k)
                if k == 0:
                    dve.wait_ge(ev("unit_used"), U1 + U_PLE + 4)
                chain(v.tensor_tensor(zq[:, k, :], zq[:, k, :], acc[:, k, :], ALU.mult))
                v.tensor_tensor(hx[:, k, :], hx[:, k, :], zq[:, k, :], ALU.add).then_inc(ev("h_ple"), 1)
            dve.wait_ge(ev("std_ready"), NORM_NO["final2"] + 1)
            v.reciprocal(small[:, TT:2 * TT], small[:, 0:TT]).then_inc(ev("rstd_ready"), 1)
            dve.wait_ge(ev("rstd_ready"), NORM_NO["final2"] + 1)
            dve.wait_ge(ev("result_turned"), DC)
            for k in range(TT):
                v.tensor_scalar(out_tok(k)[:, 512:D], ps[:, 2 * k + 1, :], small[:, TT + k:TT + k + 1], None, ALU.mult)\
                    .then_inc(ev("out_tokens_by_vector"), 1)

        @block.tensor
        def _(pe):
            mm = nc.tensor.matmul

            def triple(o, h, l, rh, rl, first, last, skip=False):
                mm(o, h, rh, start=first, stop=False, skip_group_check=skip)
                mm(o, h, rl, start=False, stop=False, skip_group_check=skip)
                return mm(o, l, rh, start=False, stop=last, skip_group_check=skip)

            def columns(b, bank, hi, lo, n, step=P, chunks=DC, arrived=None, arriving=DC):
                for c in range(chunks):
                    if arrived is not None and c < arriving:
                        pe.wait_ge(ev("split_low"), arrived + c + 1)
                    w = slice(c * step, c * step + P)
                    last = triple(ps[:, bank, 0:n], WH[:, b, w], WL[:, b, w], hi[:, c, :], lo[:, c, :], c == 0,
                                  c == chunks - 1)
                return last

            def rows(b, banks, hi, lo, first):
                for n in range(DC):
                    w = slice(n * P, (n + 1) * P)
                    o = ps[:, banks + n // 2, (n % 2) * S:(n % 2 + 1) * S]
                    last = triple(o, WH[:, b, w], WL[:, b, w], hi, lo, first and n % 2 == 0, False, skip=True)
                return last

            def unit1(u_no, hi, lo, n, arrived=None, **k):
                pe.wait_ge(ev("unit_split"), u_no + 1)
                if u_no >= 4 and UNITS1[u_no - 4][1] not in UNCOUNTED:
                    pe.wait_ge(*taken1(u_no - 4))
                columns(u_no % NB, u_no % 4, hi, lo, n, arrived=arrived, **k).then_inc(ev("unit_used"), 1)

            def sum_square(name, c, n):
                if c == 0 and NORM_NO[name]:
                    pe.wait_ge(ev("std_ready"), NORM_NO[name])
                k = SQ_AT[name] + c
                pe.wait_ge(ev("square_ready"), k + 1)
                mm(ps[:, 7, 0:n], ones[:], XT[:, k % 2, 0:n], start=c == 0, stop=c == NCH[name] - 1)\
                    .then_inc(ev("squares_summed"), 1)

            def norm(name, n):
                for c in range(NCH[name]):
                    sum_square(name, c, n)

            tr = nc.tensor.transpose
            pe.wait_ge(ev("ident_ready"), 1)
            pe.wait_ge(ev("x_loaded"), 48)
            for c in range(DC):
                if c >= 4:
                    pe.wait_ge(ev("hT_by_vector" if c % 2 else "hT_by_scalar"), (c - 4) // 2 + 1)
                tr(ps[:, c % 4, 0:META], x_tok[0:META, 2, c * P:(c + 1) * P], ident[0:META, 0:META])
                for k in range(TT):
                    last = tr(ps[:, c % 4, META + k * P:META + (k + 1) * P], x_tok[:, k, c * P:(c + 1) * P], ident[:])
                last.then_inc(ev("x_turned"), 1)
            pe.wait_ge(ev("inv_ready"), ROPE // 2)
            pe.wait_ge(ev("meta_pos"), 1)
            pe.wait_ge(ev("pos_ready"), 1)
            mm(ps[0:QD, 5, 0:T], inv_row[0:1, 0:QD], pos_row[0:1, :], start=True, stop=True).then_inc(ev("angles"), 1)
            pe.wait_ge(ev("ones_ready"), 1)
            norm("pre_mix", T)
            pe.wait_ge(ev("vec1_loaded"), 16 * len(VEC1))
            tr(ps[:, 6, 0:NV1], vrow1[0:NV1, :], ident[0:NV1, 0:NV1]).then_inc(ev("vrows_turned"), 1)
            for c in (DC - 2, DC - 1):
                pe.wait_ge(ev("hT_by_vector" if c % 2 else "hT_by_scalar"), c // 2 + 1)
            for k in range(4):
                unit1(k, xh1, xl1, T, arrived=0)
            pe.wait_ge(ev("vec2_loaded"), 16 * len(VEC2))
            pe.wait_ge(ev("vecs_ready"), 1)
            tr(ps[:, 6, 0:NV2], vrow2[0:NV2, :], ident[0:NV2, 0:NV2]).then_inc(ev("vrows_turned"), 1)
            norm("ckv", T)
            for k in range(4, 8):
                unit1(k, xh1, xl1, T)
                if k == 7:
                    norm("cq", S)
            for k in range(8, 16):
                unit1(k, xh1, xl1, T)
            pe.wait_ge(ev("swap_ready"), 2)
            pe.wait_ge(ev("unit_taken_by_scalar"), 4)
            pe.wait_ge(ev("angle_reduced"), 2)
            mm(ps[0:QD, 5, 0:T], swap[:], kpe[0:QD, :], start=True, stop=True).then_inc(ev("kpe_swapped"), 1)
            norm("conv", S)
            u0 = FIRST1["uq"]
            for k in range(HEADS):
                unit1(u0 + k, HH, HL, S, arrived=SP_AT["cq"] if k == 0 else None, chunks=2, step=QD)

            def swap_queries(j):
                pe.wait_ge(*taken1(u0 + 2 * j + 1))
                if j == 0:
                    pe.wait_ge(ev("rope_keys"), 1)
                if j >= 2:
                    pe.wait_ge(ev("q_roped"), j - 1)
                mm(ps[0:QD, 4 + j % 2, :], swap[:], qcat[0:QD, 2 * j:2 * j + 2, :].rearrange("p h t -> p (h t)"),
                   start=True, stop=True).then_inc(ev("q_swapped"), 1)

            swap_queries(0)
            swap_queries(1)
            uk = FIRST1["ukv"]
            pe.wait_ge(ev("unit_split"), uk + 1)
            pe.wait_ge(ev("split_low"), SP_AT["ckv"] + 1)
            pe.wait_ge(ev("k_padded"), 2)
            pe.wait_ge(*taken1(uk - 1))
            b = uk % NB
            for h in range(HEADS):
                if h >= 4:
                    pe.wait_ge(ev("nope_keys_taken"), h - 3)
                w = slice(h * NOPE, h * NOPE + P)
                triple(ps[:, h % 4, 0:T], WH[:, b, w], WL[:, b, w], KH[:, 0:T], KL[:, 0:T], True, True)\
                    .then_inc(ev("nope_keys"), 1)
                if h in (3, 6):
                    swap_queries(2 + h // 6)
            pe.wait_ge(ev("q_roped"), 4)
            for k in range(3):
                w = slice(HEADS * NOPE, UNIT)
                tk = slice(k * P, (k + 1) * P)
                mm(ps[:, 4 + k, :], KH[:, tk], WH[:, b, w], start=True, stop=False)
                mm(ps[:, 4 + k, :], KH[:, tk], WL[:, b, w], start=False, stop=False)
                mm(ps[:, 4 + k, :], KL[:, tk], WH[:, b, w], start=False, stop=True)\
                    .then_inc(ev("values" if k < 2 else "unit_used"), 1)
            pe.wait_ge(ev("values_ready"), 3)
            pe.wait_ge(ev("nope_keys_taken"), HEADS)

            def scores(n):
                h, qt = divmod(n, TT)
                keys = META + (qt + 1) * P
                if n >= 2:
                    pe.wait_ge(ev("exp_done"), n - 1)
                mm(ps[:, 4 + n % 2, 0:keys], qcat[0:QD, h, qt * P:(qt + 1) * P], kcat[0:QD, h, 0:keys],
                   start=True, stop=True).then_inc(ev("scores"), 1)

            scores(0)
            scores(1)
            def weigh_values(n):
                h, qt = divmod(n, TT)
                pe.wait_ge(ev("probT_ready"), n + 1)
                o = ps[(h % 2) * VD:(h % 2 + 1) * VD, h // 2, qt * P:(qt + 1) * P]
                vs = slice(h * VD, (h + 1) * VD)
                pT = probT(n % 2)
                for k in range(qt + 1):
                    mm(o, vtok[:, k, vs], pT[:, k, :], start=k == 0, stop=False, skip_group_check=True)
                mm(o, vtok[0:META, qt + 1, vs], pT[0:META, 2, :], start=False, stop=True, skip_group_check=True)\
                    .then_inc(ev("att_out"), 1)

            for n in range(HEADS * TT):
                qt = n % TT
                if n + 2 < HEADS * TT:
                    scores(n + 2)
                pe.wait_ge(ev("prob_ready"), n + 1)
                if n >= 2:
                    pe.wait_ge(ev("probT_ready"), n - 1)
                elif n == 1:
                    pe.wait_ge(ev("std_ready"), NORM_NO["conv"] + 1)
                b = n % 2
                for k in range(qt + 1):
                    tr(ps[:, 6 + b, k * P:(k + 1) * P], prob[:, b, k * P:(k + 1) * P], ident[:])
                tr(ps[0:META, 6 + b, 3 * P:4 * P], prob[:, b, (qt + 1) * P:(qt + 1) * P + META], ident[:])\
                    .then_inc(ev("prob_turned"), 1)
                if n:
                    weigh_values(n - 1)
            weigh_values(HEADS * TT - 1)
            pe.wait_ge(ev("probT_ready"), HEADS * TT)
            norm("attn", S)
            pe.wait_ge(ev("aT_ready"), 4)
            for k in range(8):
                unit1(FIRST1["out0"] + k, xh2, xl2, S, arrived=None if k else SP_AT["attn"], arriving=4)
                if k:
                    sum_square("post_mix", k - 1, S)
            sum_square("post_mix", DC - 1, S)
            norm("pre_ffn", S)
            pe.wait_ge(ev("router_loaded"), 64)
            for c in range(DC):
                pe.wait_ge(ev("split_value"), VALUE_AT["ffn"] + c + 1)
                for t in range(TT):
                    o = ps[:, 6, 36 * t:36 * (t + 1)]
                    if c == 0:
                        mm(o, ones[0:1, :], b_router[:], start=t == 0, stop=False, skip_group_check=True)
                    last = mm(o, tT[:, c, t * P:(t + 1) * P], w_router[:, c, :], start=False, stop=c == DC - 1,
                              skip_group_check=True)
            last.then_inc(ev("logits"), 1)
            u0 = FIRST1["shg"]
            for k in range(4):
                unit1(u0 + k, xh2, xl2, S, arrived=None if k else SP_AT["ffn"])
            for k in range(TT):
                if k:
                    pe.wait_ge(ev("t_ready"), k)
                for c in range(DC):
                    last = tr(ps[:, 4 + c // 4, (c % 4) * P:(c % 4 + 1) * P], tT[:, c, k * P:(k + 1) * P], ident[:])
                last.then_inc(ev("t_turned"), 1)
                if k == 0:
                    pe.wait_ge(ev("chosen_ready"), 1)
                    o = lambda j: ps[:, 6, P + j * EXPERTS:P + (j + 1) * EXPERTS]
                    mm(o(0), before[:], r_m[:, 0, :], start=True, stop=True)
                    mm(o(1), ones[:], r_m[:, 0, :], start=True, stop=False)
                    mm(o(1), before[:], r_m[:, 1, :], start=False, stop=True)
                    mm(o(2), ones[:], r_m[:, 0, :], start=True, stop=False)
                    mm(o(2), ones[:], r_m[:, 1, :], start=False, stop=True).then_inc(ev("ranks"), 1)
            for k in range(2):
                un = u0 + 4 + k
                pe.wait_ge(ev("unit_split"), un + 1)
                pe.wait_ge(ev("split_low"), SP_AT["shared"] + 2)
                rows(un % NB, 0, HH[:, k, :], HL[:, k, :], k == 0).then_inc(ev("unit_used"), 1)

            def gather(b, pack, width, chunks, done):
                for c in chunks:
                    o = ps[:, c // pack, (c % pack) * width:(c % pack + 1) * width]
                    for t in range(TT):
                        for part, x in enumerate((th, tl)):
                            last = mm(o, x[:, t, c:D:DC], sel[:, b, t, 0:width], start=t == 0 and part == 0,
                                      stop=t == TT - 1 and part == 1)
                last.then_inc(done, 1)

            def half_experts(s, h, up, n):
                for c in range(DC):
                    for q in range(n):
                        last = mm(ps[q * CAP:(q + 1) * CAP, 2 + up, 0:FF],
                                  xg[:, h, c, q * CAP:(q + 1) * CAP], slot(s + q)[:, c * FF:(c + 1) * FF],
                                  start=c == 0, stop=c == DC - 1, skip_group_check=True)
                return last

            def turn_hidden():
                for f in range(2):
                    last = tr(ps[:, 2, FF + f * P:FF + (f + 1) * P], hid[:, f * P:(f + 1) * P], ident[:])
                return last

            def down(s, bank, experts):
                for n in range(2):
                    for f in range(2):
                        for q in range(experts):
                            last = mm(ps[q * CAP:(q + 1) * CAP, bank + n, :], hidT[:, f, q * CAP:(q + 1) * CAP],
                                      slot(s + q)[:, f * D + n * 512:f * D + (n + 1) * 512],
                                      start=f == 0, stop=f == 1, skip_group_check=True)
                return last

            pe.wait_ge(ev("t_ready"), TT)
            pe.wait_ge(ev("sel_ready"), 1)
            pe.wait_ge(ev("shT_ready"), 2)
            gather(0, 4, 2 * CAP, range(4), ev("first_half_gathered"))
            gather(0, 4, 2 * CAP, range(4, DC), ev("second_half_gathered"))
            pe.wait_ge(ev("overflow_known"), 1)
            for k in range(2):
                pe.sem_inc(ev("rows_by_scalar"), 1)
                pe.sem_inc(ev("rows_by_vector"), 1)
            with pe.Fori(0, TURNS) as i:
                for h in range(2):
                    pe.wait_ge(ev("xg_by_scalar"), i * 2 + (h + 1))
                    pe.wait_ge(ev("xg_by_vector"), i * 2 + (h + 1))
                    for up in range(2):
                        sl = 6 * h + 2 * up
                        for q in range(2):
                            pe.wait_ge(*slab_e(i, sl + q))
                        half_experts(sl, h, up, 2).then_inc(ev("expert_slab_used"), 2)
                    pe.wait_ge(ev("sel_ready"), i * 2 + (h + 2))
                    gather((h + 1) % 2, 4, 2 * CAP, range(4), ev("first_half_gathered"))
                    pe.wait_ge(ev("hidden_ready"), i * 2 + (h + 1))
                    turn_hidden().then_inc(ev("hidden_turned"), 1)
                    gather((h + 1) % 2, 4, 2 * CAP, range(4, DC), ev("second_half_gathered"))
                    pe.wait_ge(ev("hidT_ready"), i * 2 + (h + 1))
                    pe.wait_ge(ev("rows_by_scalar"), i * 2 + (h + 1))
                    pe.wait_ge(ev("rows_by_vector"), i * 2 + (h + 1))
                    sl = 6 * h + 4
                    for q in range(2):
                        pe.wait_ge(*slab_e(i, sl + q))
                    down(sl, 4 + 2 * h, 2).then_inc(ev("expert_slab_used"), 2)
            pe.wait_ge(ev("rows_by_scalar"), EXPERTS // 2 + 2)
            pe.wait_ge(ev("rows_by_vector"), EXPERTS // 2 + 2)
            pe.wait_ge(ev("xg_by_scalar"), 2 * TURNS + 1)
            pe.wait_ge(ev("xg_by_vector"), 2 * TURNS + 1)
            more = pe.value_load(overflow[0:1, 0:1], min_val=0, max_val=1)
            with pe.If(more > 0):
                with pe.Fori(0, RANKS // CAP - 1) as r:
                    with pe.Fori(0, EXPERTS) as e:
                        b = r * EXPERTS + e
                        pe.wait_ge(ev("o_sel"), b + 1)
                        gather(0, 8, CAP, range(DC), ev("o_gathered"))
                        pe.wait_ge(ev("o_xg"), b + 1)
                        pe.wait_ge(ev("o_loaded"), b * 48 + 48)
                        half_experts(RING2, 0, 0, 1)
                        half_experts(RING2 + 1, 0, 1, 1).then_inc(ev("o_gate_up"), 1)
                        pe.wait_ge(ev("o_hidden"), b + 1)
                        turn_hidden().then_inc(ev("o_turned"), 1)
                        pe.wait_ge(ev("o_hidT"), b + 1)
                        down(RING2 + 2, 4, 1).then_inc(ev("o_down"), 1)
                        pe.wait_ge(ev("o_rows"), b * 2 + 2)

            with pe.If(more > 0):
                pe.wait_ge(ev("o_replaced"), 2 * TT)
            pe.wait_ge(ev("weights_ready"), 2 * TT)
            for t in range(TT):
                for k in range(2):
                    pe.wait_ge(ev(f"rows_gathered_{TT * k + t}"), 16)
                    for c in range(DC):
                        last = mm(ps[:, c // 2, (c % 2) * S + t * P:(c % 2) * S + (t + 1) * P],
                                  gath[:, TT * k + t, c * P:(c + 1) * P], diag(TT * k + t),
                                  start=t == 0 and k == 0 and c % 2 == 0, stop=t == TT - 1 and k == 1,
                                  skip_group_check=True)
                        if t == TT - 1 and k == 1 and c % 2:
                            last.then_inc(ev("routed_turned"), 2)
            norm("post_ffn", S)
            norm("mix2", S)
            gw = slot(SLAB_LRU % RING2)[:, 0:2 * 512].rearrange("p (k c n) -> p k c n", k=2, c=DC)

            def gates(c):
                pe.wait_ge(ev("conv_ready"), c + 1)
                if c >= 4:
                    pe.wait_ge(ev("gate_act"), c - 3)
                for k in range(2):
                    for half in range(2):
                        r_ = slice(64 * half, 64 * half + 64)
                        last = mm(ps[r_, 4 + c % 4, k * S:(k + 1) * S], gw[r_, k, c, :], zc[r_, c, :],
                                  start=True, stop=True, skip_group_check=True)
                last.then_inc(ev("gates_done"), 1)

            def in_units(first, i=0):
                for k in range(first, first + 8):
                    pe.wait_ge(ev("unit_split"), i * 8 + (U1 + k + 1))
                    pe.wait_ge(ev("unit_taken_by_scalar"), i * 8 + (TAKEN_S1 + k - 3))
                    columns(k % NB, k % 4, xh2, xl2, S).then_inc(ev("unit_used"), 1)

            for k in range(16):
                pe.wait_ge(ev("unit_split"), U1 + k + 1)
                if k >= 4:
                    pe.wait_ge(ev("unit_taken_by_scalar"), TAKEN_S1 + k - 3)
                columns(k % NB, k % 4, xh2, xl2, S, arrived=None if k else SP_AT["mix2"])\
                    .then_inc(ev("unit_used"), 1)
            pe.wait_ge(ev("rgate_loaded"), 16)
            pe.wait_ge(*slab2(SLAB_LRU))
            for c in range(4):
                gates(c)
            for k in range(16, 20):
                pe.wait_ge(ev("unit_split"), U1 + k + 1)
                pe.wait_ge(ev("unit_taken_by_scalar"), TAKEN_S1 + k - 3)
                columns(k % NB, k % 4, xh2, xl2, S).then_inc(ev("unit_used"), 1)
            for c in range(4, DC):
                gates(c)
            with pe.Fori(0, 3) as i:
                in_units(20, i)
            pe.wait_ge(ev("gate_act"), DC)
            for k in range(TT):
                for c in range(DC):
                    last = tr(ps[:, 4 + 2 * k + c // 4, (c % 4) * P:(c % 4 + 1) * P], zv[:, c, k * P:(k + 1) * P],
                              ident[:])
                last.then_inc(ev("v_turned"), 1)
            for k in range(44, 48):
                pe.wait_ge(ev("unit_split"), U1 + k + 1)
                pe.wait_ge(ev("unit_taken_by_scalar"), TAKEN_S1 + k - 3)
                columns(k % NB, k % 4, xh2, xl2, S).then_inc(ev("unit_used"), 1)
            pe.wait_ge(ev("unit_taken_by_scalar"), TAKEN_S1 + 48)

            def z_scores(n):
                j, qt = divmod(n, TT)
                keys = (qt + 1) * P
                b = n % 2
                if n >= 2:
                    pe.wait_ge(ev("sigm_done"), 2 * (n - 1))
                for h in range(2):
                    r_ = slice(64 * h, 64 * h + 64)
                    last = mm(ps[:, 2 * b + h, 0:keys], zq[r_, j, qt * P:(qt + 1) * P], zk[r_, j, 0:keys],
                              start=True, stop=True)
                last.then_inc(ev("z_scores"), 1)

            def weigh_values(n):
                j, qt = divmod(n, TT)
                nk = qt + 1
                pe.wait_ge(ev("attT_ready"), n + 1)
                if qt == 0 and j >= 2:
                    pe.wait_ge(ev("y_att_taken"), j - 1)
                for h in range(2):
                    o = ps[64 * h:64 * h + 64, 5 + j % 2, qt * P:(qt + 1) * P]
                    for k in range(nk):
                        a = (h * nk + k) * P
                        last = mm(o, vtok2[:, k, (2 * j + h) * DH2:(2 * j + h + 1) * DH2], attT(n % 2)[:, a:a + P],
                                  start=k == 0, stop=k == nk - 1, skip_group_check=True)
                last.then_inc(ev("y_att"), 1)

            z_scores(0)
            z_scores(1)
            pe.wait_ge(ev("v_ready"), TT)
            for n in range(HEADS2):
                j, qt = divmod(n, TT)
                nk = qt + 1
                if n + 2 < HEADS2:
                    z_scores(n + 2)
                pe.wait_ge(ev("att_ready"), n + 1)
                if n >= 2:
                    pe.wait_ge(ev("attT_ready"), n - 1)
                for h in range(2):
                    for k in range(nk):
                        last = tr(ps[:, (4, 7)[n % 2], (h * nk + k) * P:(h * nk + k + 1) * P],
                                  att(n % 2)[:, h, k * P:(k + 1) * P], ident[:])
                last.then_inc(ev("att_turned"), 1)
                if n:
                    weigh_values(n - 1)
            weigh_values(HEADS2 - 1)

            def unit2(v_no, hi, lo, free=None, arrived=None):
                pe.wait_ge(ev("unit_split"), U1 + v_no + 1)
                if free:
                    pe.wait_ge(*free)
                columns(v_no % NB, v_no % 4, hi, lo, S, arrived=arrived).then_inc(ev("unit_used"), 1)

            by_s = lambda n: (ev("unit_taken_by_scalar"), TAKEN_S1 + n)
            by_v = lambda n: (ev("unit_taken_by_vector"), TAKEN_V1 + n)
            for k in range(8):
                unit2(U_GATT + k, xh2, xl2, by_s(48 + k - 3))
            for k in range(8):
                unit2(U_BRL + k, xh2, xl2, by_s(56 + k - 3) if k < 4 else by_v(k - 3),
                      arrived=None if k else SP_AT["y_lru"])
            for k in range(8):
                unit2(U_BRA + k, xh2, xl2, by_v(8 + k - 3), arrived=None if k else SP_AT["y_att"])
            for k in range(8):
                unit2(U_OUT + k, xh2, xl2, by_v(16 + k - 3) if k < 4 else (ev("h_mixed2"), k - 3),
                      arrived=None if k else SP_AT["merged2"])
                if k >= 2:
                    sum_square("mlp2", k - 2, S)
            for c in (DC - 2, DC - 1):
                sum_square("mlp2", c, S)
            pe.wait_ge(ev("zeros_ready"), 2)
            pe.wait_ge(ev("std_ready"), NORM_NO["mlp2"] + 1)
            for b in range(4):
                mm(ps[:, 4 + b, :], zero_w, zero_x, start=True, stop=True)

            def mlp_turn(i, first):
                for k in range(16):
                    pe.wait_ge(ev("unit_split"), i * 16 + (U1 + U_MLP + k + 1))
                    if k % 4 < 2:
                        columns(k % NB, k % 4, xh2, xl2, S, arrived=SP_AT["mlp2"] if first and k == 0 else None)\
                            .then_inc(ev("unit_used"), 1)
                    else:
                        f = (k // 4) * 2 + k % 2
                        pe.wait_ge(ev("relu_low"), i * 8 + (f + 1))
                        rows(k % NB, 4, HH[:, f % 2, :], HL[:, f % 2, :], False).then_inc(ev("unit_used"), 1)

            mlp_turn(0, True)
            with pe.Fori(1, 4) as i:
                mlp_turn(i, False)
            pe.wait_ge(ev("p_loaded"), 16 * TT)
            for c in range(2):
                for t in range(TT):
                    last = tr(ps[:, 2 + c, t * P:(t + 1) * P], p_tok(t)[:, c * P:(c + 1) * P], ident[:])
                last.then_inc(ev("p_turned"), 1)
            pe.wait_ge(ev("h_mlp"), DC)
            norm("ple2", S)
            pe.wait_ge(ev("std_ready"), NORM_NO["ple2"] + 1)
            gate_units = [k for k in range(10) if SLABS2[UNITS2[U_PLE + k][0]][0] == "col"]
            for k in range(10):
                if k in gate_units:
                    former = by_s(56 + gate_units.index(k - 4) + 1) if k - 4 in gate_units else None
                    unit2(U_PLE + k, xh2, xl2, former, arrived=None if k else SP_AT["ple2"])
                else:
                    pe.wait_ge(ev("unit_split"), U1 + U_PLE + k + 1)
                    pe.wait_ge(ev("split_low"), SP_AT["p2"] + 2)
                    rows(k % NB, 4, HH[:, k - 2, :], HL[:, k - 2, :], k == 2).then_inc(ev("unit_used"), 1)
            pe.wait_ge(*by_s(56 + DC))
            pe.wait_ge(ev("h_ple"), 2)
            for c in range(DC):
                pe.wait_ge(ev("result"), c + 1)
                for k in range(TT):
                    last = tr(ps[:, 2 * k + c // 4, (c % 4) * P:(c % 4 + 1) * P], zg[:, c, k * P:(k + 1) * P], ident[:])
                last.then_inc(ev("result_turned"), 1)
                n = SQ_AT["final2"] + c
                pe.wait_ge(ev("square_ready"), n + 1)
                for k in range(TT):
                    last = mm(ps[:, 4, k:k + 1], XT[:, n % 2, k * P:(k + 1) * P], ones[:, 0:1],
                              start=c == 0 and k == 0, stop=c == DC - 1, skip_group_check=True)
                last.then_inc(ev("squares_summed"), 1)


def kernel(**inputs):
    import concourse.bacc as bacc
    from concourse.bass_utils import run_bass_kernel_spmd

    nc = bacc.Bacc("TRN2", target_bir_lowering=False, num_devices=1)
    arrays, aps = {}, {}
    for name, a in inputs.items():
        a = np.ascontiguousarray(a)
        arrays[f"in_{name}"] = a
        aps[name] = nc.dram_tensor(f"in_{name}", a.shape, mybir.dt.from_np(a.dtype), kind="ExternalInput").ap()
    out = nc.dram_tensor("out_tokens_by_features", (1, S, D), F32, kind="ExternalOutput").ap()
    build(nc, aps, out)
    r = run_bass_kernel_spmd(nc, [arrays], core_ids=[0])
    return r.results[0]["out_tokens_by_features"]
```
